# Optimizing a Trainium2 kernel written in Bass

```python
import jax, jax.numpy as jnp
from jax import lax
import numpy as np

D_MODEL = 1024
BATCH = 1
SEQ = 256
DEPTH = 2

D_FF = 2816
NORM_EPS = 1e-6
LRU_WIDTH = 512
LRU_HEADS = 8
LRU_HEAD_DIM = LRU_WIDTH // LRU_HEADS
LRU_CONV_WIDTH = 4
LRU_C = 8.0
MLA_HEADS = 8
QK_NOPE_DIM = 64
QK_ROPE_DIM = 32
V_HEAD_DIM = 64
Q_LORA_RANK = 384
KV_LORA_RANK = 256
ROPE_THETA = 10000.0
Q_BLOCK = 128
CONV_CH = 512
CONV_WIDTH = 31
N_BRANCH = 3
IN_A = 2 * LRU_WIDTH
IN_B = Q_LORA_RANK + KV_LORA_RANK + QK_ROPE_DIM
IN_C = 2 * CONV_CH
IN_G = N_BRANCH * D_MODEL
D_IN = IN_A + IN_B + IN_C + IN_G
MAX_POS_OFFSET = 4096


def rms_norm(x, g):
    xf = x.astype(jnp.float32)
    y = xf * lax.rsqrt(jnp.mean(xf * xf, axis=-1, keepdims=True) + NORM_EPS)
    return (y * g.astype(jnp.float32)).astype(x.dtype)

def layer_norm(x, g, b):
    xf = x.astype(jnp.float32)
    mu = jnp.mean(xf, axis=-1, keepdims=True)
    var = jnp.mean(jnp.square(xf - mu), axis=-1, keepdims=True)
    y = (xf - mu) * lax.rsqrt(var + NORM_EPS)
    return (y * g.astype(jnp.float32) + b.astype(jnp.float32)).astype(x.dtype)

def swiglu(x, w1, w2):
    gu = x @ w1
    g, u = gu[..., :D_FF], gu[..., D_FF:]
    return (jax.nn.silu(g) * u) @ w2

def causal_depthwise_conv(x, w, b):
    k = w.shape[0]
    y = lax.conv_general_dilated(
        x, w[:, None, :].astype(x.dtype), window_strides=(1,), padding=[(k - 1, 0)],
        dimension_numbers=('NWC', 'WIO', 'NWC'), feature_group_count=x.shape[-1])
    return y + b.astype(x.dtype)

def rg_lru(x, w_gate, b_gate, lam):
    b, s, w = x.shape
    xf = x.astype(jnp.float32)
    xh = xf.reshape(b, s, LRU_HEADS, LRU_HEAD_DIM)
    gates = jnp.einsum('bshd,hde->bshe', xh, w_gate.astype(jnp.float32)) + b_gate.astype(jnp.float32)
    r = jax.nn.sigmoid(gates[..., :LRU_HEAD_DIM]).reshape(b, s, w)
    i = jax.nn.sigmoid(gates[..., LRU_HEAD_DIM:]).reshape(b, s, w)
    log_a = -LRU_C * r * jax.nn.softplus(-lam.astype(jnp.float32))
    a = jnp.exp(log_a)
    u = jnp.sqrt(-jnp.expm1(2.0 * log_a)) * (i * xf)

    def combine(left, right):
        a_l, h_l = left
        a_r, h_r = right
        return a_l * a_r, a_r * h_l + h_r

    _, h = lax.associative_scan(combine, (a, u), axis=1)
    return h.astype(x.dtype)

def rope_tables(positions):
    inv_freq = ROPE_THETA ** (-jnp.arange(0, QK_ROPE_DIM, 2, dtype=jnp.float32) / QK_ROPE_DIM)
    ang = positions.astype(jnp.float32)[..., None] * inv_freq
    return jnp.cos(ang), jnp.sin(ang)

def apply_rope(x, cos, sin):
    half = x.shape[-1] // 2
    x1, x2 = x[..., :half], x[..., half:]
    cos = cos.astype(x.dtype)
    sin = sin.astype(x.dtype)
    return jnp.concatenate([x1 * cos - x2 * sin, x2 * cos + x1 * sin], axis=-1)

def mla_branch(cq, ckv, kpe, positions, q_norm, w_uq, kv_norm, w_ukv, w_o):
    b, s, _ = cq.shape
    q = (rms_norm(cq, q_norm) @ w_uq).reshape(b, s, MLA_HEADS, QK_NOPE_DIM + QK_ROPE_DIM)
    q_nope, q_pe = q[..., :QK_NOPE_DIM], q[..., QK_NOPE_DIM:]
    kv = (rms_norm(ckv, kv_norm) @ w_ukv).reshape(b, s, MLA_HEADS, QK_NOPE_DIM + V_HEAD_DIM)
    k_nope, v = kv[..., :QK_NOPE_DIM], kv[..., QK_NOPE_DIM:]
    cos, sin = rope_tables(positions)
    q_pe = apply_rope(q_pe, cos[:, :, None, :], sin[:, :, None, :])
    k_pe = apply_rope(kpe, cos, sin)
    n_blk = s // Q_BLOCK
    qn_blocks = q_nope.reshape(b, n_blk, Q_BLOCK, MLA_HEADS, QK_NOPE_DIM).swapaxes(0, 1)
    qp_blocks = q_pe.reshape(b, n_blk, Q_BLOCK, MLA_HEADS, QK_ROPE_DIM).swapaxes(0, 1)
    scale = (QK_NOPE_DIM + QK_ROPE_DIM) ** -0.5
    key_idx = jnp.arange(s)

    def attend(args):
        qn, qp, blk = args
        sc = (jnp.einsum('bqhd,bkhd->bhqk', qn, k_nope, preferred_element_type=jnp.float32)
              + jnp.einsum('bqhr,bkr->bhqk', qp, k_pe, preferred_element_type=jnp.float32)) * scale
        q_idx = blk * Q_BLOCK + jnp.arange(Q_BLOCK)
        mask = key_idx[None, :] <= q_idx[:, None]
        sc = jnp.where(mask, sc, jnp.finfo(jnp.float32).min)
        p = jax.nn.softmax(sc, axis=-1).astype(v.dtype)
        return jnp.einsum('bhqk,bkhd->bqhd', p, v)

    o = lax.map(attend, (qn_blocks, qp_blocks, jnp.arange(n_blk)))
    o = o.swapaxes(0, 1).reshape(b, s, MLA_HEADS * V_HEAD_DIM)
    return o @ w_o

def conformer_conv_branch(pc, dw_w, dw_b, ln_g, ln_b, w_pw, b_pw):
    c = pc[..., :CONV_CH] * jax.nn.sigmoid(pc[..., CONV_CH:])
    c = causal_depthwise_conv(c, dw_w, dw_b)
    c = jax.nn.silu(layer_norm(c, ln_g, ln_b))
    return c @ w_pw + b_pw

def hybrid_mixer(h, positions, w_in, b_in, lru_conv_w, lru_conv_b, lru_w_gate, lru_b_gate,
                 lru_lambda, lru_w_out, q_norm, w_uq, kv_norm, w_ukv, mla_w_o,
                 conv_dw_w, conv_dw_b, conv_ln_g, conv_ln_b, conv_w_out, conv_b_out, w_out):
    proj = h @ w_in + b_in
    o1, o2, o3 = IN_A, IN_A + IN_B, IN_A + IN_B + IN_C
    pa, pb, pc, pg = proj[..., :o1], proj[..., o1:o2], proj[..., o2:o3], proj[..., o3:]
    xa = causal_depthwise_conv(pa[..., :LRU_WIDTH], lru_conv_w, lru_conv_b)
    y_a = (rg_lru(xa, lru_w_gate, lru_b_gate, lru_lambda) * jax.nn.gelu(pa[..., LRU_WIDTH:])) @ lru_w_out
    cq = pb[..., :Q_LORA_RANK]
    ckv = pb[..., Q_LORA_RANK:Q_LORA_RANK + KV_LORA_RANK]
    kpe = pb[..., Q_LORA_RANK + KV_LORA_RANK:]
    y_b = mla_branch(cq, ckv, kpe, positions, q_norm, w_uq, kv_norm, w_ukv, mla_w_o)
    y_c = conformer_conv_branch(pc, conv_dw_w, conv_dw_b, conv_ln_g, conv_ln_b, conv_w_out, conv_b_out)
    gates = jax.nn.sigmoid(pg.astype(jnp.float32)).astype(h.dtype)
    gates = gates.reshape(*pg.shape[:-1], N_BRANCH, D_MODEL)
    merged = gates[..., 0, :] * y_a + gates[..., 1, :] * y_b + gates[..., 2, :] * y_c
    return merged @ w_out

def first_inputs(seed: int = 0) -> dict:
    key = jax.random.key(seed)
    ks = iter(jax.random.split(key, 48))
    L = DEPTH

    def w(shape, fan_in):
        return jax.random.normal(next(ks), shape, jnp.float32) * fan_in ** -0.5

    def gain(shape):
        return 1.0 + 0.02 * jax.random.normal(next(ks), shape, jnp.float32)

    def bias(shape):
        return 0.02 * jax.random.normal(next(ks), shape, jnp.float32)

    x = jax.random.normal(next(ks), (BATCH, SEQ, D_MODEL), jnp.float32)
    offsets = jax.random.randint(next(ks), (BATCH, 1), 0, MAX_POS_OFFSET, dtype=jnp.int32)
    positions = offsets + jnp.arange(SEQ, dtype=jnp.int32)[None, :]
    u = jax.random.uniform(next(ks), (L, LRU_WIDTH), jnp.float32, 0.9, 0.999)
    a0 = u ** (1.0 / LRU_C)
    lru_lambda = jnp.log(a0) - jnp.log1p(-a0)
    return {
        'x': x,
        'positions': positions,
        'ffn1_norm': gain((L, D_MODEL)),
        'ffn1_w1': w((L, D_MODEL, 2 * D_FF), D_MODEL),
        'ffn1_w2': w((L, D_FF, D_MODEL), D_FF),
        'mix_norm': gain((L, D_MODEL)),
        'w_in': w((L, D_MODEL, D_IN), D_MODEL),
        'b_in': bias((L, D_IN)),
        'lru_conv_w': w((L, LRU_CONV_WIDTH, LRU_WIDTH), LRU_CONV_WIDTH),
        'lru_conv_b': bias((L, LRU_WIDTH)),
        'lru_w_gate': w((L, LRU_HEADS, LRU_HEAD_DIM, 2 * LRU_HEAD_DIM), LRU_HEAD_DIM),
        'lru_b_gate': bias((L, LRU_HEADS, 2 * LRU_HEAD_DIM)),
        'lru_lambda': lru_lambda,
        'lru_w_out': w((L, LRU_WIDTH, D_MODEL), LRU_WIDTH),
        'q_norm': gain((L, Q_LORA_RANK)),
        'w_uq': w((L, Q_LORA_RANK, MLA_HEADS * (QK_NOPE_DIM + QK_ROPE_DIM)), Q_LORA_RANK),
        'kv_norm': gain((L, KV_LORA_RANK)),
        'w_ukv': w((L, KV_LORA_RANK, MLA_HEADS * (QK_NOPE_DIM + V_HEAD_DIM)), KV_LORA_RANK),
        'mla_w_o': w((L, MLA_HEADS * V_HEAD_DIM, D_MODEL), MLA_HEADS * V_HEAD_DIM),
        'conv_dw_w': w((L, CONV_WIDTH, CONV_CH), CONV_WIDTH),
        'conv_dw_b': bias((L, CONV_CH)),
        'conv_ln_g': gain((L, CONV_CH)),
        'conv_ln_b': bias((L, CONV_CH)),
        'conv_w_out': w((L, CONV_CH, D_MODEL), CONV_CH),
        'conv_b_out': bias((L, D_MODEL)),
        'w_out': w((L, D_MODEL, D_MODEL), D_MODEL),
        'ffn2_norm': gain((L, D_MODEL)),
        'ffn2_w1': w((L, D_MODEL, 2 * D_FF), D_MODEL),
        'ffn2_w2': w((L, D_FF, D_MODEL), D_FF),
        'final_norm': gain((D_MODEL,)),
    }

def first_block(x, positions, ffn1_norm, ffn1_w1, ffn1_w2, mix_norm, w_in, b_in,
              lru_conv_w, lru_conv_b, lru_w_gate, lru_b_gate, lru_lambda, lru_w_out,
              q_norm, w_uq, kv_norm, w_ukv, mla_w_o,
              conv_dw_w, conv_dw_b, conv_ln_g, conv_ln_b, conv_w_out, conv_b_out,
              w_out, ffn2_norm, ffn2_w1, ffn2_w2, final_norm):
    for l in range(DEPTH):
        x = x + 0.5 * swiglu(rms_norm(x, ffn1_norm[l]), ffn1_w1[l], ffn1_w2[l])
        x = x + hybrid_mixer(
            rms_norm(x, mix_norm[l]), positions, w_in[l], b_in[l],
            lru_conv_w[l], lru_conv_b[l], lru_w_gate[l], lru_b_gate[l], lru_lambda[l], lru_w_out[l],
            q_norm[l], w_uq[l], kv_norm[l], w_ukv[l], mla_w_o[l],
            conv_dw_w[l], conv_dw_b[l], conv_ln_g[l], conv_ln_b[l], conv_w_out[l], conv_b_out[l],
            w_out[l])
        x = x + 0.5 * swiglu(rms_norm(x, ffn2_norm[l]), ffn2_w1[l], ffn2_w2[l])
    return rms_norm(x, final_norm)


HEAD_DIM = 64
FOX_HEADS = 4
NSA_HEADS = 8
NSA_KV_GROUPS = 2
DIL_HEADS = 4
MIX_WIDTH = (FOX_HEADS + NSA_HEADS + DIL_HEADS) * HEAD_DIM
DIL_PATTERNS = ((128, 1), (512, 4), (2048, 16))
ROPE_THETA_2 = 500000.0
ROPE_DIM = HEAD_DIM // 4
CMP_BLOCK = 32
CMP_STRIDE = 16
CMP_HIDDEN = 4 * HEAD_DIM
SEL_BLOCK = 64
SEL_TOPK = 16
NSA_WINDOW = 512
CONV_WIDTH_2 = 3
RMS_EPS = 1e-6
NEG_INF = -1e30
FORCE_SCORE = 1e9
ATTN_SCALE = HEAD_DIM ** -0.5
KV_W = NSA_KV_GROUPS * HEAD_DIM
IN_SPLITS = (FOX_HEADS * HEAD_DIM,) * 3 + (FOX_HEADS,) + (NSA_HEADS * HEAD_DIM,) + (KV_W,) * 6 + (3 * NSA_HEADS,) + (DIL_HEADS * HEAD_DIM,) * 3
N_IN = sum(IN_SPLITS)


def rms_norm_2(x, g):
    xf = x.astype(jnp.float32)
    y = xf * lax.rsqrt(jnp.mean(xf * xf, axis=-1, keepdims=True) + RMS_EPS)
    return (y * g.astype(jnp.float32)).astype(x.dtype)

def rope_tables_2(positions):
    half = ROPE_DIM // 2
    inv_freq = ROPE_THETA_2 ** (-2.0 * jnp.arange(half, dtype=jnp.float32) / ROPE_DIM)
    ang = positions.astype(jnp.float32)[..., None] * inv_freq
    return jnp.cos(ang)[:, :, None, :], jnp.sin(ang)[:, :, None, :]

def partial_rope(x, cos, sin):
    half = ROPE_DIM // 2
    cos = cos.astype(x.dtype)
    sin = sin.astype(x.dtype)
    x1 = x[..., :half]
    x2 = x[..., half:ROPE_DIM]
    return jnp.concatenate([x1 * cos - x2 * sin, x2 * cos + x1 * sin, x[..., ROPE_DIM:]], axis=-1)

def masked_softmax(scores, mask):
    s = jnp.where(mask, scores, NEG_INF)
    m = jnp.max(s, axis=-1, keepdims=True)
    e = jnp.where(mask, jnp.exp(s - m), 0.0)
    den = jnp.maximum(jnp.sum(e, axis=-1, keepdims=True), 1e-30)
    return e / den, m + jnp.log(den)

def sweep_query_blocks(fn, seq):
    out = lax.map(fn, jnp.arange(seq // Q_BLOCK, dtype=jnp.int32) * Q_BLOCK)
    out = jnp.moveaxis(out, 0, 1)
    return out.reshape((out.shape[0], seq) + out.shape[3:])

def fox_attention(q, k, v, log_f):
    S = q.shape[1]
    c = jnp.cumsum(log_f, axis=1)
    c_k = jnp.transpose(c, (0, 2, 1))[:, :, None, :]
    kpos = jnp.arange(S)

    def block(start):
        qb = lax.dynamic_slice_in_dim(q, start, Q_BLOCK, axis=1)
        cb = lax.dynamic_slice_in_dim(c, start, Q_BLOCK, axis=1)
        qpos = start + jnp.arange(Q_BLOCK)
        s = jnp.einsum('bqhd,bkhd->bhqk', qb, k, preferred_element_type=jnp.float32) * ATTN_SCALE
        s = s + jnp.transpose(cb, (0, 2, 1))[..., None] - c_k
        p, _ = masked_softmax(s, kpos[None, :] <= qpos[:, None])
        return jnp.einsum('bhqk,bkhd->bqhd', p.astype(v.dtype), v)

    return sweep_query_blocks(block, S)

def dilated_attention(q, k, v):
    S = q.shape[1]

    def block(start):
        qb = lax.dynamic_slice_in_dim(q, start, Q_BLOCK, axis=1)
        qpos = start + jnp.arange(Q_BLOCK)
        outs, lses = [], []
        for window, dilation in DIL_PATTERNS:
            offs = jnp.arange(window // dilation + 1) * dilation
            idx = qpos[:, None] - offs[None, :]
            valid = idx >= 0
            idx = jnp.maximum(idx, 0)
            kg = jnp.take(k, idx, axis=1)
            vg = jnp.take(v, idx, axis=1)
            s = jnp.einsum('bqhd,bqjhd->bhqj', qb, kg, preferred_element_type=jnp.float32) * ATTN_SCALE
            p, lse = masked_softmax(s, valid[None, None])
            outs.append(jnp.einsum('bhqj,bqjhd->bqhd', p.astype(v.dtype), vg))
            lses.append(lse[..., 0])
        w = jax.nn.softmax(jnp.stack(lses, 0), axis=0)
        w = jnp.transpose(w, (0, 1, 3, 2))[..., None].astype(v.dtype)
        return jnp.sum(w * jnp.stack(outs, 0), axis=0)

    return sweep_query_blocks(block, S)

def nsa_compress(kv, pos_emb, w1, w2):
    S = kv.shape[1]
    n_cmp = (S - CMP_BLOCK) // CMP_STRIDE + 1
    idx = jnp.arange(n_cmp)[:, None] * CMP_STRIDE + jnp.arange(CMP_BLOCK)[None, :]
    win = jnp.take(kv, idx, axis=1) + pos_emb[None, None, :, None, :]
    B, N, L, G, hd = win.shape
    win = jnp.transpose(win, (0, 1, 3, 2, 4)).reshape(B, N, G, L * hd)
    return jax.nn.gelu(win @ w1) @ w2

def nsa_attention(q, kc, vc, ks, vs, kw, vw, gates, cmp_pos_k, cmp_w1_k, cmp_w2_k, cmp_pos_v, cmp_w1_v, cmp_w2_v):
    B, S, H, hd = q.shape
    G = NSA_KV_GROUPS
    R = H // G
    k_cmp = nsa_compress(kc, cmp_pos_k, cmp_w1_k, cmp_w2_k)
    v_cmp = nsa_compress(vc, cmp_pos_v, cmp_w1_v, cmp_w2_v)
    n_cmp = k_cmp.shape[1]
    cmp_start = jnp.arange(n_cmp) * CMP_STRIDE
    cmp_end = cmp_start + CMP_BLOCK - 1
    n_sel = S // SEL_BLOCK
    top_k = min(SEL_TOPK, n_sel)
    sel_start = jnp.arange(n_sel) * SEL_BLOCK
    overlap = ((cmp_start[:, None] < sel_start[None, :] + SEL_BLOCK) & (cmp_start[:, None] + CMP_BLOCK > sel_start[None, :])).astype(jnp.float32)
    ks_blk = jnp.transpose(ks.reshape(B, n_sel, SEL_BLOCK, G, hd), (0, 3, 1, 2, 4))
    vs_blk = jnp.transpose(vs.reshape(B, n_sel, SEL_BLOCK, G, hd), (0, 3, 1, 2, 4))
    pad = ((0, 0), (NSA_WINDOW, 0), (0, 0), (0, 0))
    kw_pad = jnp.pad(kw, pad)
    vw_pad = jnp.pad(vw, pad)
    gather_blocks = jax.vmap(jax.vmap(lambda blocks, idx: blocks[idx]))
    blk_id = jnp.arange(n_sel)[None, :]

    def block(start):
        qb = lax.dynamic_slice_in_dim(q, start, Q_BLOCK, axis=1).reshape(B, Q_BLOCK, G, R, hd)
        gb = lax.dynamic_slice_in_dim(gates, start, Q_BLOCK, axis=1).reshape(B, Q_BLOCK, G, R, 3)
        qpos = start + jnp.arange(Q_BLOCK)
        s_c = jnp.einsum('bqgrd,bngd->bgrqn', qb, k_cmp, preferred_element_type=jnp.float32) * ATTN_SCALE
        p_c, _ = masked_softmax(s_c, cmp_end[None, :] <= qpos[:, None])
        o_c = jnp.einsum('bgrqn,bngd->bqgrd', p_c.astype(v_cmp.dtype), v_cmp)
        imp = jnp.einsum('bgrqn,nj->bgqj', p_c, overlap)
        cur = (qpos // SEL_BLOCK)[:, None]
        forced = (blk_id == 0) | (blk_id == cur) | (blk_id == cur - 1)
        future = sel_start[None, :] > qpos[:, None]
        imp = jnp.where(future, NEG_INF, jnp.where(forced, FORCE_SCORE, imp))
        _, sel = lax.top_k(imp, top_k)
        k_sel = gather_blocks(ks_blk, sel).reshape(B, G, Q_BLOCK, top_k * SEL_BLOCK, hd)
        v_sel = gather_blocks(vs_blk, sel).reshape(B, G, Q_BLOCK, top_k * SEL_BLOCK, hd)
        kpos_sel = (sel[..., None] * SEL_BLOCK + jnp.arange(SEL_BLOCK)).reshape(B, G, Q_BLOCK, top_k * SEL_BLOCK)
        mask_s = (kpos_sel <= qpos[None, None, :, None])[:, :, None]
        s_s = jnp.einsum('bqgrd,bgqkd->bgrqk', qb, k_sel, preferred_element_type=jnp.float32) * ATTN_SCALE
        p_s, _ = masked_softmax(s_s, mask_s)
        o_s = jnp.einsum('bgrqk,bgqkd->bqgrd', p_s.astype(v_sel.dtype), v_sel)
        kwb = lax.dynamic_slice_in_dim(kw_pad, start, Q_BLOCK + NSA_WINDOW, axis=1)
        vwb = lax.dynamic_slice_in_dim(vw_pad, start, Q_BLOCK + NSA_WINDOW, axis=1)
        kpos_w = (start - NSA_WINDOW + jnp.arange(Q_BLOCK + NSA_WINDOW))[None, :]
        mask_w = (kpos_w <= qpos[:, None]) & (kpos_w > qpos[:, None] - NSA_WINDOW) & (kpos_w >= 0)
        s_w = jnp.einsum('bqgrd,bkgd->bgrqk', qb, kwb, preferred_element_type=jnp.float32) * ATTN_SCALE
        p_w, _ = masked_softmax(s_w, mask_w)
        o_w = jnp.einsum('bgrqk,bkgd->bqgrd', p_w.astype(vwb.dtype), vwb)
        o = gb[..., 0:1] * o_c + gb[..., 1:2] * o_s + gb[..., 2:3] * o_w
        return o.reshape(B, Q_BLOCK, H, hd)

    return sweep_query_blocks(block, S)

def hybrid_mixer_2(h, cos, sin, w_in, b_forget, b_nsa_gate, cmp_pos_k, cmp_w1_k, cmp_w2_k, cmp_pos_v, cmp_w1_v, cmp_w2_v, w_out):
    B, S, _ = h.shape
    proj = h @ w_in
    splits = np.cumsum(IN_SPLITS)[:-1].tolist()
    (fq, fk, fv, ff, nq, kc, vc, ks, vs, kw, vw, ng, dq, dk, dv) = jnp.split(proj, splits, axis=-1)

    def heads(t, n):
        return t.reshape(B, S, n, HEAD_DIM)

    log_f = jax.nn.log_sigmoid(ff.astype(jnp.float32) + b_forget.astype(jnp.float32))
    o_fox = fox_attention(heads(fq, FOX_HEADS), heads(fk, FOX_HEADS), heads(fv, FOX_HEADS), log_f)
    rope = lambda t, n: partial_rope(heads(t, n), cos, sin)
    gates = jax.nn.sigmoid(ng + b_nsa_gate).reshape(B, S, NSA_HEADS, 3)
    o_nsa = nsa_attention(rope(nq, NSA_HEADS), rope(kc, NSA_KV_GROUPS), heads(vc, NSA_KV_GROUPS),
                          rope(ks, NSA_KV_GROUPS), heads(vs, NSA_KV_GROUPS),
                          rope(kw, NSA_KV_GROUPS), heads(vw, NSA_KV_GROUPS), gates,
                          cmp_pos_k, cmp_w1_k, cmp_w2_k, cmp_pos_v, cmp_w1_v, cmp_w2_v)
    o_dil = dilated_attention(rope(dq, DIL_HEADS), rope(dk, DIL_HEADS), heads(dv, DIL_HEADS))
    mix = jnp.concatenate([o_fox.reshape(B, S, -1), o_nsa.reshape(B, S, -1), o_dil.reshape(B, S, -1)], axis=-1)
    return mix @ w_out

def conv_ffn(h, w_up, conv_w, conv_b, w_down):
    S = h.shape[1]
    u = h @ w_up
    u_pad = jnp.pad(u, ((0, 0), (CONV_WIDTH_2 - 1, 0), (0, 0)))
    c = conv_b + u_pad[:, 0:S] * conv_w[0]
    for j in range(1, CONV_WIDTH_2):
        c = c + u_pad[:, j:j + S] * conv_w[j]
    a, b = jnp.split(c, 2, axis=-1)
    return (jax.nn.silu(a) * b) @ w_down

def second_inputs(seed: int = 0) -> dict:
    key = jax.random.key(seed)
    k = jax.random.split(key, 24)
    nrm = lambda kk, shape, scale: jax.random.normal(kk, shape, jnp.float32) * scale
    x = nrm(k[0], (BATCH, SEQ, D_MODEL), 1.0)
    offset = jax.random.randint(k[1], (BATCH, 1), 0, 1024, dtype=jnp.int32)
    positions = offset + jnp.arange(SEQ, dtype=jnp.int32)[None, :]
    return {
        'x': x,
        'positions': positions,
        'attn_pre_norm': 1.0 + nrm(k[2], (DEPTH, D_MODEL), 0.05),
        'attn_post_norm': 1.0 + nrm(k[3], (DEPTH, D_MODEL), 0.05),
        'ffn_pre_norm': 1.0 + nrm(k[4], (DEPTH, D_MODEL), 0.05),
        'ffn_post_norm': 1.0 + nrm(k[5], (DEPTH, D_MODEL), 0.05),
        'w_in': nrm(k[6], (DEPTH, D_MODEL, N_IN), D_MODEL ** -0.5),
        'b_forget': jax.random.uniform(k[7], (DEPTH, FOX_HEADS), jnp.float32, 1.0, 5.0),
        'b_nsa_gate': nrm(k[8], (DEPTH, 3 * NSA_HEADS), 0.01),
        'cmp_pos_k': nrm(k[9], (DEPTH, CMP_BLOCK, HEAD_DIM), 0.1),
        'cmp_w1_k': nrm(k[10], (DEPTH, CMP_BLOCK * HEAD_DIM, CMP_HIDDEN), (CMP_BLOCK * HEAD_DIM) ** -0.5),
        'cmp_w2_k': nrm(k[11], (DEPTH, CMP_HIDDEN, HEAD_DIM), CMP_HIDDEN ** -0.5),
        'cmp_pos_v': nrm(k[12], (DEPTH, CMP_BLOCK, HEAD_DIM), 0.1),
        'cmp_w1_v': nrm(k[13], (DEPTH, CMP_BLOCK * HEAD_DIM, CMP_HIDDEN), (CMP_BLOCK * HEAD_DIM) ** -0.5),
        'cmp_w2_v': nrm(k[14], (DEPTH, CMP_HIDDEN, HEAD_DIM), CMP_HIDDEN ** -0.5),
        'w_out': nrm(k[15], (DEPTH, MIX_WIDTH, D_MODEL), MIX_WIDTH ** -0.5),
        'w_up': nrm(k[16], (DEPTH, D_MODEL, 2 * D_FF), D_MODEL ** -0.5),
        'conv_w': nrm(k[17], (DEPTH, CONV_WIDTH_2, 2 * D_FF), CONV_WIDTH_2 ** -0.5),
        'conv_b': nrm(k[18], (DEPTH, 2 * D_FF), 0.01),
        'w_down': nrm(k[19], (DEPTH, D_FF, D_MODEL), D_FF ** -0.5),
    }

def second_block(x, positions, attn_pre_norm, attn_post_norm, ffn_pre_norm, ffn_post_norm, w_in, b_forget, b_nsa_gate,
              cmp_pos_k, cmp_w1_k, cmp_w2_k, cmp_pos_v, cmp_w1_v, cmp_w2_v, w_out, w_up, conv_w, conv_b, w_down):
    cos, sin = rope_tables_2(positions)
    for l in range(DEPTH):
        h = rms_norm_2(x, attn_pre_norm[l])
        mix = hybrid_mixer_2(h, cos, sin, w_in[l], b_forget[l], b_nsa_gate[l], cmp_pos_k[l], cmp_w1_k[l], cmp_w2_k[l],
                           cmp_pos_v[l], cmp_w1_v[l], cmp_w2_v[l], w_out[l])
        x = x + rms_norm_2(mix, attn_post_norm[l])
        h = rms_norm_2(x, ffn_pre_norm[l])
        x = x + rms_norm_2(conv_ffn(h, w_up[l], conv_w[l], conv_b[l], w_down[l]), ffn_post_norm[l])
    return x


def setup_inputs(seed=0):
    out = dict(first_inputs(seed))
    for name, value in second_inputs(seed + 1).items():
        if name != "x":
            out[name + "_2"] = value
    return out


def reference(
    x, positions, ffn1_norm, ffn1_w1, ffn1_w2, mix_norm, w_in, b_in, lru_conv_w, lru_conv_b,
    lru_w_gate, lru_b_gate, lru_lambda, lru_w_out, q_norm, w_uq, kv_norm, w_ukv, mla_w_o,
    conv_dw_w, conv_dw_b, conv_ln_g, conv_ln_b, conv_w_out, conv_b_out, w_out, ffn2_norm,
    ffn2_w1, ffn2_w2, final_norm, positions_2, attn_pre_norm_2, attn_post_norm_2,
    ffn_pre_norm_2, ffn_post_norm_2, w_in_2, b_forget_2, b_nsa_gate_2, cmp_pos_k_2, cmp_w1_k_2,
    cmp_w2_k_2, cmp_pos_v_2, cmp_w1_v_2, cmp_w2_v_2, w_out_2, w_up_2, conv_w_2, conv_b_2,
    w_down_2,
):
    x = first_block(
        x, positions, ffn1_norm, ffn1_w1, ffn1_w2, mix_norm, w_in, b_in, lru_conv_w, lru_conv_b,
        lru_w_gate, lru_b_gate, lru_lambda, lru_w_out, q_norm, w_uq, kv_norm, w_ukv, mla_w_o,
        conv_dw_w, conv_dw_b, conv_ln_g, conv_ln_b, conv_w_out, conv_b_out, w_out, ffn2_norm,
        ffn2_w1, ffn2_w2, final_norm,
    )
    return second_block(
        x, positions_2, attn_pre_norm_2, attn_post_norm_2, ffn_pre_norm_2, ffn_post_norm_2,
        w_in_2, b_forget_2, b_nsa_gate_2, cmp_pos_k_2, cmp_w1_k_2, cmp_w2_k_2, cmp_pos_v_2,
        cmp_w1_v_2, cmp_w2_v_2, w_out_2, w_up_2, conv_w_2, conv_b_2, w_down_2,
    )


_drawn_inputs = setup_inputs


def setup_inputs(seed=0):
    import zlib

    import numpy as np

    out = dict(_drawn_inputs(seed))
    spreads = {}
    factors = {'ffn1_norm': 3.328,
     'lru_b_gate': 32.303,
     'q_norm': 8.0,
     'kv_norm': 5.043,
     'conv_ln_g': 2.842,
     'ffn2_norm': 3.959,
     'b_nsa_gate_2': 8.0,
     'cmp_pos_k_2': 4.987,
     'conv_b_2': 4.937,
     'conv_ln_b': 5.925,
     'conv_b_out': 3.657}
    for name, (base, spread) in spreads.items():
        noise = np.random.default_rng([zlib.crc32(name.encode()), seed]).standard_normal(out[name].shape)
        drawn = base * np.exp(spread * noise) if base else spread * noise
        out[name] = __import__('jax').numpy.asarray(drawn.astype(out[name].dtype))
    for name, factor in factors.items():
        out[name] = (out[name] * factor).astype(out[name].dtype)
    return out
```

```python
import concourse.bass as bass
from concourse import mybir
from contextlib import ExitStack
import numpy as np

F32 = mybir.dt.float32
F32R = mybir.dt.float32r
I32 = mybir.dt.int32
ACT = mybir.ActivationFunctionType
ALU = mybir.AluOpType
AX = mybir.AxisListType

T = 256
P = 128
D = 1024
KT = D // P
DEPTH = 2
FF = 2816
FT = FF // P
HALF = FT // 2
BLOCK = P * P
RAW_SLOTS = 2
SPLIT_SLOTS = 4
AHEAD = 3
EPS = 1e-6
MASKED = -1e30
TWO_PI = 2 * np.pi

FFN_UNITS = [16] * FT + [HALF] * (2 * KT)
MIX1_UNITS = ([16] * 3
              + [16] * 4
              + [16] * 4
              + [12] * 2
              + [16]
              + [8]
              + [12] * 24
              + [16, 16, 16, 8, 8])
UNITS1 = FFN_UNITS + MIX1_UNITS + FFN_UNITS
MIX1_AT = len(FFN_UNITS)
PC_AT, PA_AT, UQ_AT, UKV_AT, LRG_AT, BR_AT, WO_AT = (MIX1_AT + n for n in (3, 7, 11, 13, 14, 15, 39))
FFN1_AT = MIX1_AT + len(MIX1_UNITS)
assert len(UNITS1) % SPLIT_SLOTS == 0

QKV_HEADS, NOPE, ROPE, VD = 8, 64, 32, 64
MLA_SCALE = (NOPE + ROPE) ** -0.5
CONV_TAPS, LRU_TAPS = 31, 4


def columns(fields):
    at, out = 0, {}
    for name, n in fields:
        out[name] = at
        at += n
    return out, at


VEC1, NVEC1 = columns([("norm0", 8), ("norm1", 8), ("norm2", 8), ("b_pb", 6), ("b_pc", 8), ("b_pa", 8), ("b_gate", 24),
                       ("lru_w", 16), ("lru_b", 4), ("lru_br", 4), ("lru_bi", 4), ("lam", 4), ("q_norm", 3),
                       ("kv_norm", 2), ("dw_w", 4 * CONV_TAPS), ("dw_b", 4), ("ln_g", 4), ("ln_b", 4), ("b_pw", 8)])
CONST, NCONST = columns([("ones", P), ("ident", P), ("causal", 384), ("freq1", 1), ("phase1", 1), ("final", 8)])


def first_steps():
    s = [("pb", i) for i in range(3)] + [("pc", i) for i in range(4)]
    s += [("pa", 0), ("stat_lat", 0), ("pa", 1), ("pa", 2), ("pa", 3)]
    s += [("uq", i) for i in range(4)] + [("uk", 0), ("uk", 1), ("uv", 0), ("uv", 1)]
    s += [("lr", 0), ("lr", 1), ("li", 0), ("li", 1)]
    s += [("S", 0)]
    for u in range(16):
        s.append(("A", u) if u < 8 else ("C", u - 8))
        if u == 3:
            s.append(("stat_mu", 0))
        if u == 5:
            s.append(("stat_ln", 0))
        if u % 2 == 0:
            s.append(("T", u // 2))
            if u // 2 + 1 < QKV_HEADS:
                s.append(("S", u // 2 + 1))
        elif u % 4 == 3:
            s.append(("V", u // 4))
    return s + [("B", t) for t in range(8)] + [("O", i) for i in range(5)]


STEPS1 = first_steps()
FREER = dict(pb="a", pc="v", pa="a", stat_lat="v", uq="v", uk="a", uv="a", lr="a", li="a", S="v", T="a", V="v",
             A="v", C="a", B="v", O="v", stat_mu="v", stat_ln="v", stat="v", up="v", down="v")
FIXED_BANK = dict(stat_lat=7, stat_mu=7, stat_ln=7, stat=7, T=6, V=7)


class Groups:

    def __init__(self, steps, freer=FREER, fixed=FIXED_BANK):
        self.mark, self.bank, self.freer = {}, {}, {}
        marks = 0
        self.freed_until, main, last, self.before = {"a": 0, "v": 0}, 0, {}, {}
        for kind, i in steps:
            g = (kind, i)
            if kind.startswith("up"):
                main, bank = i % 4, i % 4
            elif kind.startswith("down"):
                bank = 2 + i % 2
                main = 3
            elif kind == "S":
                bank = 4 + i % 2
            elif kind in fixed:
                bank = fixed[kind]
            else:
                main = (main + 1) % 4
                bank = main
            who = freer[kind if kind in freer else kind[:-1]]
            marks += 2 if kind.startswith("down") else 1
            self.mark[g], self.bank[g] = marks, bank
            self.before[g] = last.get(bank)
            if who is None:
                continue
            self.freed_until[who] += 1
            self.freer[g] = (who, self.freed_until[who])
            last[bank] = g
        self.marks, self.last = marks, last


class Signal:

    def __init__(self, sem, per, ahead=0):
        self.sem, self.per, self.ahead = sem, per, ahead

    def __call__(self, layer, n):
        return self.sem, layer * self.per + (self.ahead * self.per + n)


def layer_steps1():
    ffn = lambda w: [(f"up{w}", j) for j in range(FT)] + [(f"down{w}", t) for t in range(KT)]
    return [("stat", 0)] + ffn(0) + [("stat", 1)] + STEPS1 + [("stat", 2)] + ffn(1)


def used_marks1(mark):
    last = ["pb"] * 3, ["pc"] * 4, ["pa"] * 4
    out = [mark["up0", j] for j in range(FT)]
    out += [mark["down0", t] - 1 + half for t in range(KT) for half in range(2)]
    out += [mark[kind, i] for kinds in last for i, kind in enumerate(kinds)]
    out += [mark["uq", 1], mark["uq", 3], mark["uv", 1], mark["li", 1]]
    out += [mark[kind, t] for kind in "ACB" for t in range(KT)]
    out += [mark["O", i] for i in range(5)]
    out += [mark["up1", j] for j in range(FT)]
    out += [mark["down1", t] - 1 + half for t in range(KT) for half in range(2)]
    assert len(out) == len(UNITS1)
    return out


FOX_HEADS, NSA_HEADS, DIL_HEADS, HD = 4, 8, 4, 64
GROUPS = 2
ATTN_SCALE = HD ** -0.5
CMP_BLOCK, CMP_STRIDE = 32, 16
N_CMP = (T - CMP_BLOCK) // CMP_STRIDE + 1
SLOT = 16
DIL_PATTERNS = ((128, 1), (512, 4), (2048, 16))
ROPE2_HALF = 8
assert T // 64 <= 16 and T <= 512
VB_COLS = 288
KC, VC, NQ, KS, KW, FQ, FK, DQ, DK, FGATE = 0, 1, 2, 6, 7, 8, 10, 12, 14, 16
F_TILES = [(2 * i, 2 * i + 1) for i in range(8)] + [(16,)]
ROTATED = {0: (KC,), 1: (2, 3), 2: (4, 5), 3: (KS, KW), 6: (12, 13), 7: (14, 15)}
MIX2_ORDER = [("f", 0), ("R", 0), ("f", 1), ("R", 1), ("f", 2), ("R", 2), ("f", 3), ("R", 3), ("f", 8), ("va", 0),
              ("va", 1), ("vb", 0), ("vb", 1), ("cmp", 0), ("cmp", 1), ("cmp", 2), ("cmp", 3), ("c2", 0), ("SC", 0)]
MIX2_FILL = [("f", 4), ("f", 5), ("cum", 0), ("cum", 1), ("f", 6), ("R", 6), ("f", 7), ("R", 7)]
HEADS2 = [(kind, i, e) for i in range(4) for e in range(2) for kind in ("sel", "win")] \
    + [(kind, i, e) for kind in ("fox", "dil") for i in range(2) for e in range(2)]
LAST_OF_TILE = {n for n in range(16) if n % 4 == 3} | {n for n in range(16, 24) if n % 2}
O2_TILE = dict(fox=0, sel=2, win=2, dil=6)


def second_steps():
    s, fill = list(MIX2_ORDER), list(MIX2_FILL)
    values = lambda n: ("W" if n in LAST_OF_TILE else "V", n)
    for n in range(len(HEADS2) + 2):
        if n < len(HEADS2):
            s.append(("S", n))
        if n == 1:
            s.append(("TC", 0))
        if 0 <= n - 1 < len(HEADS2):
            s.append(("T", n - 1))
        if n - 2 >= 0:
            s.append(values(n - 2))
        if fill:
            s.append(fill.pop(0))
    return s + [("O", i) for i in range(5)]


STEPS2 = second_steps()
FREER2 = dict(f="a", R="v", va="a", vb="a", cmp="a", c2="a", SC="v", TC="a", cum="v", S="v", T="a", V=None, W="v",
              O="a", stat="v", up="v", down="a")
FIXED_BANK2 = dict(stat=7, T=6, V=7, W=7)
O2_UNITS = [(0, 1), (2, 3), (4, 5), (6,), (7,)]

UNIT_ORDER2 = [("f", 0), ("f", 1), ("f", 2), ("f", 3), ("f", 8), ("va", 0), ("va", 1), ("vb", 0), ("vb", 1), ("cmp", 0),
               ("cmp", 1), ("cmp", 2), ("cmp", 3), ("f", 4), ("f", 5), ("f", 6), ("f", 7)] + [("O", i) for i in range(5)]
UNIT_BLOCKS2 = dict(f=16, va=16, vb=4 * VB_COLS // P, cmp=16, O=16)
UNITS2 = [8 if u in (("f", 8), ("O", 3), ("O", 4)) else UNIT_BLOCKS2[u[0]] for u in UNIT_ORDER2] + FFN_UNITS
FFN2_AT = len(UNIT_ORDER2)
UNIT_OF2 = {u: n for n, u in enumerate(UNIT_ORDER2)}
assert len(UNITS2) % SPLIT_SLOTS == 0


def layer_steps2():
    return ([("stat", 0)] + STEPS2 + [("stat", 1), ("stat", 2)] + [("up0", j) for j in range(FT)]
            + [("down0", t) for t in range(KT)] + [("stat", 3)])


def used_marks2(mark):
    both = {("va", 0): ("va", 1), ("vb", 0): ("vb", 1)}
    out = [mark[both.get(u, u)] for u in UNIT_ORDER2]
    out += [mark["up0", j] for j in range(FT)]
    return out + [mark["down0", t] - 1 + half for t in range(KT) for half in range(2)]


VEC2, NVEC2 = columns([("norm0", 8), ("norm1", 8), ("norm2", 8), ("norm3", 8), ("b_forget", 1), ("b_nsa", 24),
                       ("pos_k", 16), ("pos_v", 16), ("w2k", 128), ("w2v", 128), ("conv_w", 3 * 2 * FT), ("conv_b", 2 * FT)])
CONST2, NCONST2 = columns([("perm", P), ("dil", 384), ("pick", FOX_HEADS * P), ("cmp_bias", 2 * SLOT), ("cmp_keep", 2 * SLOT),
                           ("own", NSA_HEADS), ("freq_c", 1), ("freq_s", 1), ("phase_c", 1), ("phase_s", 1)])
NVEC = max(NVEC1, NVEC2)


def build(nc, io):
    with ExitStack() as ctx:
        def sbuf(name, shape, dt=F32, stack=ctx):
            return stack.enter_context(nc.sbuf_tensor(name, shape, dt))

        raw = sbuf("raw", [P, RAW_SLOTS, 16 * P])
        w_hi = sbuf("w_hi", [P, SPLIT_SLOTS, 16 * P], F32R)
        w_lo = sbuf("w_lo", [P, SPLIT_SLOTS, 16 * P], F32R)
        x = sbuf("x", [P, KT, T])
        h_hi = sbuf("h_hi", [P, KT, T], F32R)
        h_lo = sbuf("h_lo", [P, KT, T], F32R)
        const = sbuf("const", [P, NCONST])
        vec = sbuf("vec", [P, NVEC])
        scr = sbuf("scr", [P, KT, T])
        sq = sbuf("sq", [P, 2, T])
        acc = sbuf("acc", [P, T])
        std = sbuf("std", [P, T])
        trig1 = sbuf("trig1", [P, T])
        ones = const[:, CONST["ones"]:CONST["ones"] + P]
        ident = const[:, CONST["ident"]:CONST["ident"] + P]
        causal = const[:, CONST["causal"]:CONST["causal"] + 384]

        with ExitStack() as phase:
            hid_hi = sbuf("hid_hi", [P, FT, T], F32R, phase)
            hid_lo = sbuf("hid_lo", [P, FT, T], F32R, phase)
            silu = sbuf("silu", [P, 2, T], F32, phase)
            hid = sbuf("hid", [P, 2, T], F32, phase)
            conv2 = sbuf("conv2", [P, 2, T], F32, phase)
        with ExitStack() as phase:
            with ExitStack() as early:
                q1 = sbuf("q1", [P, QKV_HEADS, T], F32, early)
                k1 = sbuf("k1", [P, QKV_HEADS, T], F32, early)
            m_hi = sbuf("m_hi", [P, KT, T], F32R, phase)
            m_lo = sbuf("m_lo", [P, KT, T], F32R, phase)
            v1 = sbuf("v1", [P, 2, QKV_HEADS * VD], F32, phase)
            glu = sbuf("glu", [P, 4, T + CONV_TAPS - 1], F32, phase)
            conv = sbuf("conv", [P, 4, T], F32, phase)
            derived = sbuf("derived", [P, 64], F32, phase)
            probs1 = sbuf("probs1", [P, 2, 384], F32, phase)
            probs_t1 = sbuf("probs_t1", [P, 2, 384], F32, phase)
            row1 = sbuf("row1", [P, 16], F32, phase)
            with ExitStack() as early:
                lat = sbuf("lat", [P, 5, T], F32, early)
                lat_hi = sbuf("lat_hi", [P, 5, T], F32R, early)
                lat_lo = sbuf("lat_lo", [P, 5, T], F32R, early)
            cv_hi = sbuf("cv_hi", [P, 4, T], F32R, phase)
            cv_lo = sbuf("cv_lo", [P, 4, T], F32R, phase)
            o1_hi = sbuf("o1_hi", [P, 4, T], F32R, phase)
            o1_lo = sbuf("o1_lo", [P, 4, T], F32R, phase)
            pad_r = sbuf("pad_r", [P, 4, T + LRU_TAPS - 1], F32, phase)
            gelu = sbuf("gelu", [P, 4, T], F32, phase)
            xa = sbuf("xa", [P, 4, T], F32, phase)
            a_t = sbuf("a_t", [P, 4, T], F32, phase)
            i_g = sbuf("i_g", [P, 4, T], F32, phase)
            with ExitStack() as early:
                xa_hi = sbuf("xa_hi", [P, 4, T], F32R, early)
                xa_lo = sbuf("xa_lo", [P, 4, T], F32R, early)
                r_g = sbuf("r_g", [P, 4, T], F32, early)
            ya_hi = sbuf("ya_hi", [P, 4, T], F32R, phase)
            ya_lo = sbuf("ya_lo", [P, 4, T], F32R, phase)
            gate = sbuf("gate", [P, 2, T], F32, phase)
            y_b = sbuf("y_b", [P, 2, T], F32, phase)

        rope_t = a_t[:].rearrange("p (e f) t -> p e (f t)", e=2)
        key_pe = i_g[:, 0]
        lat_acc = i_g[:, 1:3].rearrange("p a t -> p (a t)")
        ratio = pad_r[:, :, LRU_TAPS - 1:]
        with ExitStack() as phase:
            sbuf("spacer", [P, 52 * 256], F32, phase)
            const2 = sbuf("const2", [P, NCONST2], F32, phase)
            cos2 = sbuf("cos2", [P, T], F32, phase)
            sin2 = sbuf("sin2", [P, T], F32, phase)
            v2a = sbuf("v2a", [P, 2, 512], F32, phase)
            v2b = sbuf("v2b", [P, 2, VB_COLS], F32, phase)
            gates2 = sbuf("gates2", [P, 2, 24], F32, phase)
            h1 = sbuf("h1", [P, 4, 2 * SLOT], F32, phase)
            h_rep = sbuf("h_rep", [P, 2, 4, 2 * SLOT], F32, phase)
            k_cmp = sbuf("k_cmp", [P, 2 * SLOT], F32, phase)
            v_cmp = sbuf("v_cmp", [P, HD], F32, phase)
            v_own = sbuf("v_own", [P, NSA_HEADS, HD], F32, phase)
            p_cmp = sbuf("p_cmp", [P, 2 * NSA_HEADS, SLOT], F32, phase)
            p_cmp_t = sbuf("p_cmp_t", [P, T], F32, phase)
            row_cmp = sbuf("row_cmp", [P, 2, 2 * NSA_HEADS], F32, phase)
            fox_bias = sbuf("fox_bias", [P, FOX_HEADS, 384], F32, phase)
            probs2 = sbuf("probs2", [P, 2, 384], F32, phase)
            probs_t2 = sbuf("probs_t2", [P, 2, 384], F32, phase)
            row2 = sbuf("row2", [P, 16], F32, phase)
        with ExitStack() as phase:
            feat = sbuf("feat", [P, 17, T], F32, phase)
            win = sbuf("win", [P, 2, 512], F32, phase)
            win_hi = sbuf("win_hi", [P, 2, 512], F32R, phase)
            win_lo = sbuf("win_lo", [P, 2, 512], F32R, phase)
            o2_hi = sbuf("o2_hi", [P, 8, T], F32R, phase)
            o2_lo = sbuf("o2_lo", [P, 8, T], F32R, phase)
            decay = sbuf("decay", [FOX_HEADS, 5, T], F32, phase)

        merged = scr
        banks = [ctx.enter_context(nc.psum_tensor(f"bank{b}", [P, 512], F32)) for b in range(8)]

        def col(name, n=0, at=VEC1, rows=slice(0, P)):
            return vec[rows, at[name] + n:at[name] + n + 1]

        def signal(name, per=0, ahead=0):
            return Signal(ctx.enter_context(nc.semaphore(name)), per, ahead)

        class Stream:

            def __init__(self, tag, units, used):
                self.units, self.used = units, used
                self.raw_full = [signal(f"raw_full{s}_{tag}", 16 * len(units) // RAW_SLOTS) for s in range(RAW_SLOTS)]
                self.hi_ready = signal(f"hi_ready_{tag}", len(units))
                self.lo_ready = signal(f"lo_ready_{tag}", len(units), ahead=1)

        class Work:

            def __init__(self, tag, steps, *rules):
                self.g = Groups(steps, *rules)
                self.done_sem = signal(f"group_done_{tag}", self.g.marks, ahead=1)
                self.freed = {"v": signal(f"freed_by_vector_{tag}", self.g.freed_until["v"], ahead=1),
                              "a": signal(f"freed_by_scalar_{tag}", self.g.freed_until["a"], ahead=1)}

            def out(self, group):
                return banks[self.g.bank[group]]

            def done(self, layer, group, more=0):
                return self.done_sem(layer, self.g.mark[group] + more)

            def bank_free(self, layer, group):
                before = self.g.before[group]
                wrapped = before is None
                before = before or self.g.last[self.g.bank[group]]
                who, n = self.g.freer[before]
                s = self.freed[who]
                return s(layer, n - s.per) if wrapped else s(layer, n)

            def wait_banks_free(self, pe, layer, groups, taken=()):
                latest = {}
                for group in taken:
                    who, n = self.g.freer[group]
                    latest[who] = max(latest.get(who, n), n)
                for group in groups:
                    before = self.g.before[group]
                    wrapped = before is None
                    who, n = self.g.freer[before or self.g.last[self.g.bank[group]]]
                    latest[who] = max(latest.get(who, -10 ** 9), n - (self.freed[who].per if wrapped else 0))
                for who, n in latest.items():
                    pe.wait_ge(*self.freed[who](layer, n))

            def freed_sem(self, group):
                return self.freed[self.g.freer[group][0]].sem

            def taken(self, layer, group, more=0):
                who, n = self.g.freer[group]
                return self.freed[who](layer, n + more)

        work1 = Work("1", layer_steps1())
        first = Stream("1", UNITS1, used_marks1(work1.g.mark))
        consts_in = signal("consts_in")
        x_in = signal("x_in")
        credited = signal("credited")
        out_done = signal("out_done")
        setup_v = signal("setup_v")
        setup_p = signal("setup_p")
        trig_ready = signal("trig_ready")

        class Norms:

            def __init__(self, tag, norms, made):
                self.sq_ready = signal(f"sq_ready_{tag}", norms * KT)
                self.sq_summed = signal(f"sq_summed_{tag}", norms * KT, ahead=1)
                self.std_ready = signal(f"std_ready_{tag}", norms)
                self.normed = signal(f"normed_{tag}", made * KT)
                self.h_hi_ready = signal(f"h_hi_ready_{tag}", made * KT)
                self.h_ready = signal(f"h_ready_{tag}", made * KT)

        n1 = Norms("1", 3, 3)
        silu_ready = signal("silu_ready", 2 * FT)
        hid_hi_ready = signal("hid_hi_ready", 2 * FT)
        hid_ready = signal("hid_ready", 2 * FT)
        vec_full = signal("vec_full", 16)
        vec_free = signal("vec_free", 2, ahead=1)
        lam_ready = signal("lam_ready", 1)
        lam_exp = signal("lam_exp", 1)
        rate_ready = signal("rate_ready", 1)
        lat_ready = signal("lat_ready", 3)
        lat_summed = signal("lat_summed", 1)
        lat_std = signal("lat_std", 1)
        lat_normed = signal("lat_normed", 1)
        lat_hi_ready = signal("lat_hi_ready", 1)
        lat_split = signal("lat_split", 1)
        key_terms = signal("key_terms", 1)
        key_rope_ready = signal("key_rope_ready", 1)
        q_nope_ready = signal("q_nope_ready", 4)
        q_ready = signal("q_ready", 4)
        sig_ready = signal("sig_ready", 4)
        xa_ready = signal("xa_ready", 1)
        xa_hi_ready = signal("xa_hi_ready", 1)
        xa_split = signal("xa_split", 1)
        decay_ready = signal("decay_ready", 1)
        ratio_ready = signal("ratio_ready", 1)
        root_ready = signal("root_ready", 1)
        ya_made = signal("ya_made", 1)
        ya_hi_ready = signal("ya_hi_ready", 1)
        ya_split = signal("ya_split", 1)
        conv_ready = signal("conv_ready", 1)
        conv_summed = signal("conv_summed", 1)
        centred = signal("centred", 1)
        centred_sq = signal("centred_sq", 1)
        dev_summed = signal("dev_summed", 1)
        ln_std = signal("ln_std", 1)
        ln_made = signal("ln_made", 1)
        cv_made = signal("cv_made", 1)
        cv_hi_ready = signal("cv_hi_ready", 1)
        cv_split = signal("cv_split", 1)
        gate_ready = signal("gate_ready", 16)
        merge_step = signal("merge_step", 24)
        x_mixed = signal("x_mixed", KT)
        m_hi_ready = signal("m_hi_ready", KT)
        m_split = signal("m_split", KT)
        max_ready = signal("max_ready", QKV_HEADS)
        exp_ready = signal("exp_ready", QKV_HEADS)
        probs_ready = signal("probs_ready", QKV_HEADS)
        o_hi_ready = signal("o_hi_ready", 4)
        work2 = Work("2", layer_steps2(), FREER2, FIXED_BANK2)
        second = Stream("2", UNITS2, used_marks2(work2.g.mark))
        n2 = Norms("2", 4, 2)
        x_final = signal("x_final")
        consts2_in = signal("consts2_in")
        turned = signal("turned")
        trig2_ready = signal("trig2_ready")
        vec2_full = signal("vec2_full", 16)
        vec2_free = signal("vec2_free", 2, ahead=1)
        x_new = signal("x_new", 2 * KT)
        rotated = signal("rotated", 6)
        win_cleared = signal("win_cleared", 1)
        win_copied = signal("win_copied", 1)
        win_made = signal("win_made", 1)
        win_hi_ready = signal("win_hi_ready", 1)
        win_split = signal("win_split", 1)
        gate_sums = signal("gate_sums", 1)
        gates_ready = signal("gates_ready", 1)
        rep_ready = signal("rep_ready", 1)
        own_ready = signal("own_ready", 1)
        cmp_shifted = signal("cmp_shifted", 1)
        cmp_exp = signal("cmp_exp", 1)
        cmp_ready = signal("cmp_ready", 1)
        forget_in = signal("forget_in", 1)
        forget_abs = signal("forget_abs", 1)
        forget_exp = signal("forget_exp", 1)
        decay_summed = signal("decay_summed", 1)
        max2_ready = signal("max2_ready", len(HEADS2))
        exp2_ready = signal("exp2_ready", len(HEADS2))
        probs2_ready = signal("probs2_ready", len(HEADS2))
        o2_hi_ready = signal("o2_hi_ready", 8)
        last_tap_ready = signal("last_tap_ready", FT)
        hid2_made = signal("hid2_made", FT)
        silu2_ready = signal("silu2_ready", FT)
        hid2_hi_ready = signal("hid2_hi_ready", FT)
        hid2_ready = signal("hid2_ready", FT)

        def load_unit(sp, st, l, s, src, more=0):
            n = st.units[s] * P
            sp.wait_ge(*st.lo_ready(l, more + (s - RAW_SLOTS + 1)))
            sp.dma_start(raw[:, s % RAW_SLOTS, 0:n], src).then_inc(st.raw_full[s % RAW_SLOTS].sem, 16)

        def split_hi(act, st, work, l, s, more=0, half=0, floor=0):
            n, before = st.units[s] * P, s - SPLIT_SLOTS
            act.wait_ge(*st.raw_full[s % RAW_SLOTS](l, half * 16 + 16 * (s // RAW_SLOTS + 1)))
            if before >= 0 or floor:
                act.wait_ge(*work.done_sem(l, more + max(st.used[before] if before >= 0 else 0, floor)))
            else:
                act.wait_ge(*work.done_sem(l, st.used[before] - work.g.marks))
            act.activation(w_hi[:, s % SPLIT_SLOTS, 0:n], raw[:, s % RAW_SLOTS, 0:n], ACT.Copy).then_inc(st.hi_ready.sem, 1)

        def split_lo(dve, st, l, s, more=0):
            n = st.units[s] * P
            dve.wait_ge(*st.hi_ready(l, more + (s + 1)))
            dve.tensor_tensor(w_lo[:, s % SPLIT_SLOTS, 0:n], raw[:, s % RAW_SLOTS, 0:n],
                              w_hi[:, s % SPLIT_SLOTS, 0:n].bitcast(F32), ALU.subtract).then_inc(st.lo_ready.sem, 1)

        class Splitter:

            def __init__(self, one, units):
                self.one, self.next, self.units = one, 0, units

            def until(self, s):
                while self.next <= min(s, self.units - 1):
                    self.one(self.next)
                    self.next += 1

        def product(pe, out, s, block, x_hi, x_lo, start, stop, rows=P):
            hi = w_hi[:, s % SPLIT_SLOTS, block * P:block * P + rows]
            lo = w_lo[:, s % SPLIT_SLOTS, block * P:block * P + rows]
            pe.matmul(out, hi, x_hi, start=start, stop=False)
            pe.matmul(out, hi, x_lo, start=False, stop=False)
            return pe.matmul(out, lo, x_hi, start=False, stop=stop)

        def tokens_product(pe, out, s, at, width, x_hi, x_lo, start, stop):
            hi = w_hi[:, s % SPLIT_SLOTS, at:at + width]
            lo = w_lo[:, s % SPLIT_SLOTS, at:at + width]
            pe.matmul(out, x_hi, hi, start=start, stop=False)
            pe.matmul(out, x_lo, hi, start=False, stop=False)
            return pe.matmul(out, x_hi, lo, start=False, stop=stop)

        def norm_pe(pe, work, nm, l, n):
            pe.wait_ge(*nm.sq_summed(l, KT * n + KT))
            pe.wait_ge(*work.bank_free(l, ("stat", n)))
            pe.matmul(work.out(("stat", n))[:, 0:T], ones, acc[:], start=True, stop=True).then_inc(work.done_sem.sem, 1)

        def norm_act_root(act, work, nm, l, n):
            act.wait_ge(*work.taken(l, ("stat", n)))
            act.activation(std[:], std[:], ACT.Sqrt).then_inc(nm.std_ready.sem, 1)

        def norm_act_split(act, nm, l, m):
            for t in range(KT):
                act.wait_ge(*nm.normed(l, KT * m + t + 1))
                act.activation(h_hi[:, t], scr[:, t], ACT.Copy).then_inc(nm.h_hi_ready.sem, 1)

        def norm_dve_scale(dve, work, nm, l, n):
            dve.wait_ge(*work.done(l, ("stat", n)))
            dve.tensor_scalar(std[:], work.out(("stat", n))[:, 0:T], 1.0 / D, EPS, ALU.mult,
                              ALU.add).then_inc(work.freed_sem(("stat", n)), 1)
            dve.wait_ge(*nm.std_ready(l, n + 1))
            dve.reciprocal(std[:], std[:])
            dve.drain()

        def norm_dve(dve, work, nm, l, n, m, gains):
            norm_dve_scale(dve, work, nm, l, n)
            for t in range(KT):
                dve.scalar_tensor_tensor(scr[:, t], x[:, t], gains(t), std[:], ALU.mult, ALU.mult).then_inc(nm.normed.sem, 1)
            for t in range(KT):
                dve.wait_ge(*nm.h_hi_ready(l, KT * m + t + 1))
                dve.tensor_tensor(h_lo[:, t], scr[:, t], h_hi[:, t].bitcast(F32), ALU.subtract).then_inc(nm.h_ready.sem, 1)

        def square(act, nm, l, k, src, parity):
            act.wait_ge(*nm.sq_summed(l, k - 2))
            act.activation(sq[:, parity], src, ACT.Square).then_inc(nm.sq_ready.sem, 1)

        def sum_squares(pool, nm, l, first_k):
            pool.drain()
            pool.wait_ge(*nm.sq_ready(l, first_k + 1))
            pool.tensor_tensor(acc[:], sq[:, 0], sq[:, 1], ALU.add).then_inc(nm.sq_summed.sem, 2)
            for t in range(2, KT):
                pool.drain()
                pool.wait_ge(*nm.sq_ready(l, first_k + t))
                pool.tensor_tensor(acc[:], acc[:], sq[:, t % 2], ALU.add).then_inc(nm.sq_summed.sem, 1)

        def ffn_pe(pe, st, work, nm, l, w, at, m, hidden):
            up, down = f"up{w}", f"down{w}"

            def up_unit(j, more):
                s = at + j
                pe.wait_ge(*st.lo_ready(l, more + (s + 1)))
                out = banks[j % 4]
                for half in range(2):
                    for k in range(KT):
                        if not isinstance(more, int) or j or half:
                            pass
                        else:
                            pe.wait_ge(*nm.h_ready(l, KT * m + k + 1))
                        last = product(pe, out[:, half * T:half * T + T], s, half * KT + k, h_hi[:, k], h_lo[:, k],
                                       k == 0, k == KT - 1)
                last.then_inc(work.done_sem.sem, 1)

            work.wait_banks_free(pe, l, [(up, j) for j in range(4)])
            for j in range(2):
                up_unit(j, 0)
            with pe.Fori(0, 5) as it:
                for u in range(4):
                    pe.wait_ge(*work.taken(l, (up, 0), it * 4 + (2 + u - 4)))
                    up_unit(2 + u, it * 4)
            with pe.Fori(0, KT // 2) as it:
                for g in range(2):
                    if work.g.freer[down, 0][0] != "v":
                        pe.wait_ge(*work.taken(l, (up, FT - 1)))
                    pe.wait_ge(*work.taken(l, (down, 0), it * 2 + (g - 2)))
                    for half in range(2):
                        s = at + FT + 2 * g + half
                        pe.wait_ge(*st.lo_ready(l, it * 4 + (s + 1)))
                        pe.wait_ge(*hidden(l, w * FT + (half + 1) * HALF - 3 * half))
                        for b in range(HALF):
                            k = half * HALF + b
                            if k >= FT - 3:
                                pe.wait_ge(*hidden(l, w * FT + k + 1))
                            last = product(pe, banks[2 + g][:, 0:T], s, b, hid_hi[:, k], hid_lo[:, k],
                                           k == 0, k == FT - 1)
                        last.then_inc(work.done_sem.sem, 1)

        def ffn_act(act, l, w, at, n, split):
            up, down, st, work = f"up{w}", f"down{w}", first, work1

            def gated(j, more, parity, split_next):
                bank = banks[j % 4]
                act.wait_ge(*work.done(l, (up, 0), more + j))
                act.activation(silu[:, parity], bank[:, 0:T], ACT.Silu).then_inc(silu_ready.sem, 1)
                split_next()
                act.wait_ge(*work.taken(l, (up, 0), more + j))
                act.activation(hid_hi[:, more + j], hid[:, parity], ACT.Copy).then_inc(hid_hi_ready.sem, 1)

            floor = work.g.mark[up, 0] - 1
            with act.Fori(0, 4) as it:
                for u in range(4):
                    gated(u, it * 4, u % 2, lambda: split_hi(act, st, work, l, at + u + AHEAD, it * 4, it * 2, floor))
            split.next = at + 16 + AHEAD
            for j in range(16, FT):
                gated(j, 0, j % 2, lambda: split.until(at + j + AHEAD))
            base = at + FT + AHEAD

            def residual(t, more):
                act.wait_ge(*work.taken(l, (down, 0), more + t))
                square(act, n1, l, more + (KT * (n + 1) + t + 1), x[:, more + t], t % 2)

            with act.Fori(0, 3) as it:
                for g in range(2):
                    for e in range(2):
                        split_hi(act, st, work, l, base + 2 * g + e, it * 4, it * 2)
                    residual(g, it * 2)
            split.next = base + 12
            for t in range(6, KT):
                split.until(base + 2 * t + 1)
                residual(t, 0)

        def ffn_dve(dve, l, w, at, n, split):
            up, down, st, work = f"up{w}", f"down{w}", first, work1

            def gated(j, more, parity, split_next):
                bank = banks[j % 4]
                dve.wait_ge(*silu_ready(l, more + (w * FT + j + 1)))
                dve.tensor_tensor(hid[:, parity], silu[:, parity], bank[:, T:2 * T], ALU.mult).then_inc(work.freed["v"].sem, 1)
                split_next()
                dve.wait_ge(*hid_hi_ready(l, more + (w * FT + j + 1)))
                dve.tensor_tensor(hid_lo[:, more + j], hid[:, parity], hid_hi[:, more + j].bitcast(F32),
                                  ALU.subtract).then_inc(hid_ready.sem, 1)

            with dve.Fori(0, 4) as it:
                for u in range(4):
                    gated(u, it * 4, u % 2, lambda: split_lo(dve, st, l, at + u + AHEAD, it * 4))
            split.next = at + 16 + AHEAD
            for j in range(16, FT):
                gated(j, 0, j % 2, lambda: split.until(at + j + AHEAD))
            base = at + FT + AHEAD

            def residual(t, more):
                dve.wait_ge(*work.done(l, (down, 0), more * 2 + 2 * t))
                dve.scalar_tensor_tensor(x[:, more + t], banks[2 + t % 2][:, 0:T], 0.5, x[:, more + t], ALU.mult,
                                         ALU.add).then_inc(work.freed["v"].sem, 1)

            with dve.Fori(0, 3) as it:
                for g in range(2):
                    for e in range(2):
                        split_lo(dve, st, l, base + 2 * g + e, it * 4)
                    residual(g, it * 2)
            split.next = base + 12
            for t in range(6, KT):
                split.until(base + 2 * t + 1)
                residual(t, 0)

        def load_loop(sp, st, l, src, at, count, size):
            with sp.Fori(0, count // 2) as it:
                for u in range(2):
                    load_unit(sp, st, l, at + u, src[it * 2 + u], it * 2)

        def scores_pe(pe, work, l, g, q, k):
            pe.wait_ge(*work.bank_free(l, g))
            out = work.out(g)
            pe.matmul(out[:, 0:P], q[:, 0:P], k[:, 0:P], start=True, stop=True)
            pe.matmul(out[:, P:3 * P], q[:, P:2 * P], k[:, 0:2 * P], start=True, stop=True).then_inc(work.done_sem.sem, 1)

        def transpose_pe(pe, work, l, g, ready, probs, parity):
            pe.wait_ge(*ready)
            pe.wait_ge(*work.bank_free(l, g))
            for b in range(3):
                last = pe.transpose(work.out(g)[:, b * P:(b + 1) * P], probs[:, parity, b * P:(b + 1) * P], ident)
            last.then_inc(work.done_sem.sem, 1)

        def values_pe(pe, out, v, probs_t, parity, start=True):
            pe.matmul(out, v[0], probs_t[:, parity, 0:T], start=start, stop=False, skip_group_check=not start)
            return pe.matmul(out[:, P:T], v[1], probs_t[:, parity, T:T + P], start=False, stop=True,
                             skip_group_check=not start)

        def softmax_dve_max(dve, work, l, g, scale, bias, probs, row, parity, signal_):
            dve.wait_ge(*work.done(l, g))
            dve.scalar_tensor_tensor(probs[:, parity, :], work.out(g)[:, 0:384], scale, bias, ALU.mult,
                                     ALU.add).then_inc(work.freed_sem(g), 1)
            dve.drain()
            dve.tensor_reduce(row[:, 8 * parity:8 * parity + 1], probs[:, parity, 0:P], AX.X, ALU.max, negate=True)
            dve.tensor_reduce(row[:, 8 * parity + 1:8 * parity + 2], probs[:, parity, P:384], AX.X, ALU.max,
                              negate=True).then_inc(signal_.sem, 1)

        def softmax_act_exp(act, probs, row, parity, ready, signal_):
            act.wait_ge(*ready)
            act.activation(probs[:, parity, 0:P], probs[:, parity, 0:P], ACT.Exp, bias=row[:, 8 * parity:8 * parity + 1],
                           accum_out=row[:, 8 * parity + 2:8 * parity + 3])
            act.activation(probs[:, parity, P:384], probs[:, parity, P:384], ACT.Exp,
                           bias=row[:, 8 * parity + 1:8 * parity + 2],
                           accum_out=row[:, 8 * parity + 3:8 * parity + 4]).then_inc(signal_.sem, 1)

        def softmax_dve_norm(dve, probs, row, parity, ready, signal_, gates=None):
            dve.wait_ge(*ready)
            inv = row[:, 8 * parity + 4:8 * parity + 6]
            dve.reciprocal(inv, row[:, 8 * parity + 2:8 * parity + 4])
            dve.drain()
            if gates is not None:
                dve.tensor_tensor(inv, inv, gates, ALU.mult)
                dve.drain()
            dve.tensor_scalar(probs[:, parity, 0:P], probs[:, parity, 0:P], row[:, 8 * parity + 4:8 * parity + 5], None, ALU.mult)
            dve.tensor_scalar(probs[:, parity, P:384], probs[:, parity, P:384], row[:, 8 * parity + 5:8 * parity + 6],
                              None, ALU.mult).then_inc(signal_.sem, 1)

        UNIT_OF = {("pb", i): MIX1_AT + i for i in range(3)} | {("pc", i): PC_AT + i for i in range(4)} \
            | {("pa", i): PA_AT + i for i in range(4)} | {("uq", i): UQ_AT + i // 2 for i in range(4)} \
            | {(k, i): UKV_AT for k in ("uk", "uv") for i in range(2)} \
            | {(k, i): LRG_AT for k in ("lr", "li") for i in range(2)} \
            | {(k, t): BR_AT + KT * n + t for n, k in enumerate("ACB") for t in range(KT)} \
            | {("O", i): WO_AT + i for i in range(5)}
        BRANCH_VEC = dict(A=0, C=16, B=8)
        O_TILES = [(0, 1), (2, 3), (4, 5), (6,), (7,)]

        def mixer1_pe(pe, l):
            st, work = first, work1
            for kind, i in STEPS1:
                g = (kind, i)
                s = UNIT_OF.get(g)
                out = work.out(g)
                if kind in ("stat_lat", "stat_mu", "stat_ln"):
                    ready = dict(stat_lat=lat_summed, stat_mu=conv_summed, stat_ln=dev_summed)[kind]
                    pe.wait_ge(*ready(l, 1))
                    pe.wait_ge(*work.bank_free(l, g))
                    if kind == "stat_lat":
                        pe.matmul(out[:, 0:2 * T], ones, lat_acc, start=True, stop=True).then_inc(work.done_sem.sem, 1)
                    else:
                        pe.matmul(out[:, 0:T], ones, acc[:], start=True, stop=True).then_inc(work.done_sem.sem, 1)
                    continue
                if kind == "S":
                    pe.wait_ge(*q_ready(l, i // 2 + 1))
                    if i == 0:
                        pe.wait_ge(*key_rope_ready(l, 1))
                        pe.wait_ge(*work.taken(l, ("uk", 1)))
                    scores_pe(pe, work, l, g, q1[0:NOPE + ROPE, i], k1[0:NOPE + ROPE, i])
                    continue
                if kind == "T":
                    transpose_pe(pe, work, l, g, probs_ready(l, i + 1), probs1, i % 2)
                    continue
                if kind == "V":
                    pe.wait_ge(*work.taken(l, ("T", 2 * i + 1)))
                    pe.wait_ge(*work.bank_free(l, g))
                    if i == 0:
                        pe.wait_ge(*work.taken(l, ("uv", 1)))
                    for e in range(2):
                        h = 2 * i + e
                        last = values_pe(pe, out[64 * e:64 * e + 64, 0:T],
                                         [v1[:, m, h * VD:(h + 1) * VD] for m in range(2)], probs_t1, e)
                    last.then_inc(work.done_sem.sem, 1)
                    continue
                pe.wait_ge(*st.lo_ready(l, s + 1))
                pe.wait_ge(*work.bank_free(l, g))
                if kind in ("pb", "pc", "pa"):
                    for half in range(2):
                        for k in range(KT):
                            if g == ("pb", 0) and half == 0:
                                pe.wait_ge(*n1.h_ready(l, KT + k + 1))
                            last = product(pe, out[:, half * T:half * T + T], s, half * KT + k, h_hi[:, k], h_lo[:, k],
                                           k == 0, k == KT - 1)
                elif kind == "uq":
                    pe.wait_ge(*lat_split(l, 1))
                    for half in range(2):
                        for k in range(3):
                            last = product(pe, out[:, half * T:half * T + T], s, 6 * (i % 2) + 3 * half + k, lat_hi[:, k],
                                           lat_lo[:, k], k == 0, k == 2)
                elif kind == "uk":
                    for half in range(2):
                        for k in range(2):
                            last = product(pe, out[:, half * T:half * T + T], s, 4 * i + 2 * half + k, lat_hi[:, 3 + k],
                                           lat_lo[:, 3 + k], k == 0, k == 1)
                elif kind == "uv":
                    for k in range(2):
                        last = tokens_product(pe, out[:, 0:512], s, 8 * P + 512 * k, 512, lat_hi[:, 3 + k, i * P:(i + 1) * P],
                                              lat_lo[:, 3 + k, i * P:(i + 1) * P], k == 0, k == 1)
                elif kind in ("lr", "li"):
                    pe.wait_ge(*xa_split(l, 1))
                    for half in range(2):
                        t = 2 * i + half
                        last = product(pe, out[:, half * T:half * T + T], s, (4 if kind == "li" else 0) + t, xa_hi[:, t],
                                       xa_lo[:, t], True, True)
                elif kind in ("A", "C", "B"):
                    for k in range(KT):
                        product(pe, out[:, 0:T], s, k, h_hi[:, k], h_lo[:, k], k == 0, k == KT - 1)
                    y_hi, y_lo = dict(A=(ya_hi, ya_lo), C=(cv_hi, cv_lo), B=(o1_hi, o1_lo))[kind]
                    if i == 0:
                        pe.wait_ge(*(ya_split(l, 1) if kind == "A" else cv_split(l, 1) if kind == "C"
                                     else work.taken(l, ("V", 3))))
                    for k in range(4):
                        last = product(pe, out[:, T:2 * T], s, KT + k, y_hi[:, k], y_lo[:, k], k == 0, k == 3)
                elif kind == "O":
                    for half, t in enumerate(O_TILES[i]):
                        for k in range(KT):
                            if t == 0:
                                pe.wait_ge(*m_split(l, k + 1))
                            last = product(pe, out[:, half * T:half * T + T], s, half * KT + k, m_hi[:, k], m_lo[:, k],
                                           k == 0, k == KT - 1)
                last.then_inc(work.done_sem.sem, 1)

        def lam_root_act(act, l):
            act.wait_ge(*lam_ready(l, 1))
            act.activation(derived[:, 28:32], derived[:, 24:28], ACT.Exp, scale=-1.0).then_inc(lam_exp.sem, 1)

        def mixer1_act(act, l, split):
            st, work = first, work1
            for kind, i in STEPS1:
                g = (kind, i)
                out = work.out(g)
                if g in UNIT_OF:
                    split.until(UNIT_OF[g] + AHEAD)
                if kind == "pb":
                    act.wait_ge(*work.done(l, g))
                    for half in range(2):
                        t, src = 2 * i + half, out[:, half * T:half * T + T]
                        if t < 5:
                            act.activation(scr[:, t], src, ACT.Square, bias=col("b_pb", t))
                            last = act.activation(lat[:, t], src, ACT.Identity, bias=col("b_pb", t))
                        else:
                            act.activation(key_pe[64:P], src[64:P], ACT.Identity,
                                           bias=col("b_pb", 5, rows=slice(64, P))).then_inc(work.freed_sem(g), 1)
                            last = None
                    if last is not None:
                        last.then_inc(work.freed_sem(g), 1)
                elif kind == "pc":
                    act.wait_ge(*work.done(l, g))
                    if i >= 2:
                        act.wait_ge(*work.taken(l, ("pc", i - 2)))
                    act.activation(gate[:, i % 2], out[:, T:2 * T], ACT.Sigmoid, bias=col("b_pc", 4 + i)).then_inc(sig_ready.sem, 1)
                    if i == 3:
                        lam_root_act(act, l)
                elif kind == "pa":
                    act.wait_ge(*work.done(l, g))
                    act.activation(pad_r[:, i, LRU_TAPS - 1:], out[:, 0:T], ACT.Identity, bias=col("b_pa", i))
                    act.activation(gelu[:, i], out[:, T:2 * T], ACT.Gelu_apprx_tanh,
                                   bias=col("b_pa", 4 + i)).then_inc(work.freed_sem(g), 1)
                    if i == 1:
                        act.wait_ge(*work.taken(l, ("stat_lat", 0)))
                        act.activation(lat_acc, lat_acc, ACT.Sqrt).then_inc(lat_std.sem, 1)
                        act.wait_ge(*lat_normed(l, 1))
                        act.activation(lat_hi[:], lat[:], ACT.Copy).then_inc(lat_hi_ready.sem, 1)
                    if i == 3:
                        act.wait_ge(*xa_ready(l, 1))
                        act.activation(xa_hi[:], xa[:], ACT.Copy).then_inc(xa_hi_ready.sem, 1)
                elif kind == "uq":
                    act.wait_ge(*work.done(l, g))
                    act.activation(q1[0:64, 2 * i:2 * i + 2], out[0:64, :].rearrange("p (h t) -> p h t", h=2),
                                   ACT.Copy).then_inc(q_nope_ready.sem, 1)
                elif kind == "uk":
                    act.wait_ge(*work.done(l, g))
                    for e in range(2):
                        last = act.activation(k1[0:64, 4 * i + e:4 * i + 4:2],
                                              out[64 * e:64 * e + 64, :].rearrange("p (h t) -> p h t", h=2), ACT.Copy)
                    last.then_inc(work.freed_sem(g), 1)
                elif kind == "uv":
                    act.wait_ge(*work.done(l, g))
                    act.activation(v1[:, i], out[:, :], ACT.Copy).then_inc(work.freed_sem(g), 1)
                elif kind in ("lr", "li"):
                    act.wait_ge(*work.done(l, g))
                    into, bias = (r_g, "lru_br") if kind == "lr" else (i_g, "lru_bi")
                    for half in range(2):
                        t = 2 * i + half
                        last = act.activation(into[:, t], out[:, half * T:half * T + T], ACT.Sigmoid, bias=col(bias, t))
                    last.then_inc(work.freed_sem(g), 1)
                    if g == ("li", 1):
                        act.drain()
                        act.wait_ge(*q_ready(l, 4))
                        act.wait_ge(*rate_ready(l, 1))
                        for t in range(4):
                            act.activation(a_t[:, t], r_g[:, t], ACT.Exp, scale=derived[:, 32 + t:33 + t])
                        for t in range(4):
                            last = act.activation(r_g[:, t], r_g[:, t], ACT.Tanh, scale=derived[:, 32 + t:33 + t])
                        last.then_inc(decay_ready.sem, 1)
                        act.wait_ge(*ratio_ready(l, 1))
                        act.activation(r_g[:], r_g[:], ACT.Sqrt).then_inc(root_ready.sem, 1)
                        act.wait_ge(*ya_made(l, 1))
                        act.activation(ya_hi[:], xa[:], ACT.Copy).then_inc(ya_hi_ready.sem, 1)
                elif kind == "S":
                    softmax_act_exp(act, probs1, row1, i % 2, max_ready(l, i + 1), exp_ready)
                elif kind == "T":
                    act.wait_ge(*work.done(l, g))
                    if i >= 2:
                        act.wait_ge(*work.done(l, ("V", i // 2 - 1)))
                    act.activation(probs_t1[:, i % 2, :], out[:, 0:384], ACT.Copy).then_inc(work.freed_sem(g), 1)
                elif kind == "V":
                    act.wait_ge(*work.done(l, g))
                    act.activation(o1_hi[:, i], out[:, 0:T], ACT.Copy).then_inc(o_hi_ready.sem, 1)
                elif kind in ("A", "C", "B"):
                    n = "ACB".index(kind) * KT + i
                    act.wait_ge(*work.done(l, g))
                    if n >= 2:
                        act.wait_ge(*merge_step(l, n - 1))
                    last = act.activation(gate[:, i % 2], out[:, 0:T], ACT.Tanh, scale=0.5,
                                          bias=derived[:, BRANCH_VEC[kind] + i:BRANCH_VEC[kind] + i + 1])
                    if kind == "C":
                        act.activation(y_b[:, i % 2], out[:, T:2 * T], ACT.Identity,
                                       bias=col("b_pw", i)).then_inc(work.freed_sem(g), 1)
                    else:
                        last.then_inc(gate_ready.sem, 1)
                    if kind == "B":
                        act.wait_ge(*merge_step(l, n + 1))
                        act.activation(m_hi[:, i], merged[:, i], ACT.Copy).then_inc(m_hi_ready.sem, 1)
                elif kind == "stat_ln":
                    act.wait_ge(*work.taken(l, g))
                    act.activation(std[:], std[:], ACT.Sqrt).then_inc(ln_std.sem, 1)
                    act.wait_ge(*ln_made(l, 1))
                    for t in range(4):
                        last = act.activation(conv[:, t], conv[:, t], ACT.Silu, scale=col("ln_g", t), bias=col("ln_b", t))
                    act.drain()
                    act.activation(cv_hi[:], conv[:], ACT.Copy).then_inc(cv_hi_ready.sem, 1)
                elif kind == "stat_mu":
                    act.wait_ge(*centred(l, 1))
                    act.activation(i_g[:], conv[:], ACT.Square).then_inc(centred_sq.sem, 1)
                elif kind == "O":
                    for t in O_TILES[i]:
                        act.wait_ge(*x_mixed(l, t + 1))
                        square(act, n1, l, KT * 2 + t + 1, x[:, t], t % 2)

        def log1p_series(dve, e, out, s, s2):
            dve.tensor_scalar(s, e, 2.0, None, ALU.add)
            dve.drain()
            dve.reciprocal(s, s)
            dve.drain()
            dve.tensor_tensor(s, s, e, ALU.mult)
            dve.drain()
            dve.tensor_tensor(s2, s, s, ALU.mult)
            dve.drain()
            dve.tensor_scalar(out, s2, 1.0 / 17, 1.0 / 15, ALU.mult, ALU.add)
            for n in (13, 11, 9, 7, 5, 3, 1):
                dve.drain()
                dve.tensor_tensor(out, out, s2, ALU.mult)
                dve.drain()
                dve.tensor_scalar(out, out, 1.0 / n, None, ALU.add)
            dve.drain()
            dve.tensor_tensor(out, out, s, ALU.mult)
            dve.drain()
            dve.tensor_scalar(out, out, 2.0, None, ALU.mult)
            dve.drain()

        def mixer1_dve(dve, l, split):
            st, work = first, work1

            def taps():
                for j in range(CONV_TAPS):
                    dve.drain()
                    for t in range(4):
                        w = col("dw_w", CONV_TAPS * t + j)
                        if j == 0:
                            last = dve.tensor_scalar(conv[:, t], glu[:, t, 0:T], w, col("dw_b", t), ALU.mult, ALU.add)
                        else:
                            last = dve.scalar_tensor_tensor(conv[:, t], glu[:, t, j:j + T], w, conv[:, t], ALU.mult, ALU.add)
                        if j == CONV_TAPS - 1 and t == 3:
                            last.then_inc(conv_ready.sem, 1)
                        yield

            dve.memset(glu[:, :, 0:CONV_TAPS - 1], 0.0)
            dve.memset(pad_r[:, :, 0:LRU_TAPS - 1], 0.0)
            tap = taps()

            def convolve(n):
                for _ in range(n):
                    next(tap, None)

            for kind, i in STEPS1:
                g = (kind, i)
                out = work.out(g)
                if g in UNIT_OF:
                    split.until(UNIT_OF[g] + AHEAD)
                if kind == "pb" and i == 0:
                    dve.tensor_scalar(derived[:, 0:24], vec[:, VEC1["b_gate"]:VEC1["b_gate"] + 24], 0.5, None, ALU.mult)
                    lam = vec[:, VEC1["lam"]:VEC1["lam"] + 4]
                    dve.tensor_scalar(derived[:, 36:40], lam, -1.0, None, ALU.mult)
                    dve.drain()
                    dve.tensor_tensor(derived[:, 24:28], derived[:, 36:40], lam, ALU.max).then_inc(lam_ready.sem, 1)
                elif kind == "pb" and i == 2:
                    dve.wait_ge(*work.taken(l, ("pb", 2)))
                    dve.tensor_tensor(rope_t[64:96, 0, 0:T], key_pe[64:96], trig1[64:96], ALU.mult)
                    dve.tensor_tensor(rope_t[64:96, 1, 0:T], key_pe[96:128], trig1[96:128], ALU.mult).then_inc(key_terms.sem, 1)
                elif kind == "pc":
                    dve.wait_ge(*sig_ready(l, i + 1))
                    dve.scalar_tensor_tensor(glu[:, i, CONV_TAPS - 1:], out[:, 0:T], col("b_pc", i), gate[:, i % 2],
                                             ALU.add, ALU.mult).then_inc(work.freed_sem(g), 1)
                    if i == 3:
                        dve.wait_ge(*lam_exp(l, 1))
                        log1p_series(dve, derived[:, 28:32], derived[:, 40:44], derived[:, 44:48], derived[:, 48:52])
                        dve.tensor_scalar(derived[:, 36:40], derived[:, 36:40], 0.0, None, ALU.max)
                        dve.drain()
                        dve.tensor_tensor(derived[:, 40:44], derived[:, 40:44], derived[:, 36:40], ALU.add)
                        dve.drain()
                        dve.tensor_scalar(derived[:, 32:36], derived[:, 40:44], -8.0, None, ALU.mult).then_inc(rate_ready.sem, 1)
                elif kind == "stat_lat":
                    dve.wait_ge(*work.done(l, g))
                    dve.tensor_scalar(lat_acc[:, 0:T], out[:, 0:T], 1.0 / 384, EPS, ALU.mult, ALU.add)
                    dve.tensor_scalar(lat_acc[:, T:2 * T], out[:, T:2 * T], 1.0 / 256, EPS, ALU.mult,
                                      ALU.add).then_inc(work.freed_sem(g), 1)
                    convolve(8)
                elif kind == "pa" and i == 1:
                    dve.wait_ge(*lat_std(l, 1))
                    dve.reciprocal(lat_acc, lat_acc)
                    dve.drain()
                    for t in range(5):
                        gain = col("q_norm", t) if t < 3 else col("kv_norm", t - 3)
                        r = lat_acc[:, 0:T] if t < 3 else lat_acc[:, T:2 * T]
                        last = dve.scalar_tensor_tensor(lat[:, t], lat[:, t], gain, r, ALU.mult, ALU.mult)
                    last.then_inc(lat_normed.sem, 1)
                    dve.wait_ge(*lat_hi_ready(l, 1))
                    dve.tensor_tensor(lat_lo[:], lat[:], lat_hi[:].bitcast(F32), ALU.subtract).then_inc(lat_split.sem, 1)
                elif kind == "pa" and i == 3:
                    dve.wait_ge(*work.taken(l, ("pa", 3)))
                    for j in range(LRU_TAPS):
                        for t in range(4):
                            w = col("lru_w", LRU_TAPS * t + j)
                            if j == 0:
                                last = dve.tensor_scalar(xa[:, t], pad_r[:, t, 0:T], w, col("lru_b", t), ALU.mult, ALU.add)
                            else:
                                last = dve.scalar_tensor_tensor(xa[:, t], pad_r[:, t, j:j + T], w, xa[:, t], ALU.mult, ALU.add)
                        if j < LRU_TAPS - 1:
                            dve.drain()
                    last.then_inc(xa_ready.sem, 1)
                    dve.wait_ge(*xa_hi_ready(l, 1))
                    dve.tensor_tensor(xa_lo[:], xa[:], xa_hi[:].bitcast(F32), ALU.subtract).then_inc(xa_split.sem, 1)
                elif kind == "uq":
                    if i == 0:
                        dve.wait_ge(*key_rope_ready(l, 1))
                    dve.wait_ge(*q_nope_ready(l, i + 1))
                    view = out[:, :].rearrange("p (h t) -> p h t", h=2)
                    a, b = (rope_t[64:96, e, :].rearrange("p (h t) -> p h t", h=2) for e in range(2))
                    dve.tensor_tensor(a, view[64:96], trig1[64:96].unsqueeze(1).to_broadcast([32, 2, T]), ALU.mult)
                    dve.tensor_tensor(b, view[96:128], trig1[96:128].unsqueeze(1).to_broadcast([32, 2, T]),
                                      ALU.mult).then_inc(work.freed_sem(g), 1)
                    dve.drain()
                    dve.tensor_tensor(q1[64:96, 2 * i:2 * i + 2], a, b, ALU.add).then_inc(q_ready.sem, 1)
                    convolve(6)
                elif kind in ("uk", "uv", "lr"):
                    convolve(8)
                elif g == ("li", 1):
                    dve.wait_ge(*decay_ready(l, 1))
                    dve.tensor_scalar(ratio, r_g[:], -1.0, 1.0, ALU.mult, ALU.add)
                    dve.drain()
                    dve.reciprocal(ratio, ratio)
                    dve.tensor_tensor(i_g[:], i_g[:], xa[:], ALU.mult)
                    dve.drain()
                    dve.scalar_tensor_tensor(r_g[:], r_g[:], -2.0, ratio, ALU.mult, ALU.mult).then_inc(ratio_ready.sem, 1)
                    dve.wait_ge(*root_ready(l, 1))
                    dve.tensor_tensor(i_g[:], i_g[:], r_g[:], ALU.mult)
                    dve.drain()
                    for t in range(4):
                        dve.tensor_tensor_scan(xa[:, t], a_t[:, t], i_g[:, t], 0.0, ALU.mult, ALU.add)
                    dve.drain()
                    dve.tensor_tensor(xa[:], xa[:], gelu[:], ALU.mult).then_inc(ya_made.sem, 1)
                    dve.wait_ge(*ya_hi_ready(l, 1))
                    dve.tensor_tensor(ya_lo[:], xa[:], ya_hi[:].bitcast(F32), ALU.subtract).then_inc(ya_split.sem, 1)
                elif kind == "S":
                    if i >= 2:
                        dve.wait_ge(*work.done(l, ("T", i - 2)))
                    softmax_dve_max(dve, work, l, g, MLA_SCALE, causal, probs1, row1, i % 2, max_ready)
                    convolve(10)
                    softmax_dve_norm(dve, probs1, row1, i % 2, exp_ready(l, i + 1), probs_ready)
                elif kind == "V":
                    dve.wait_ge(*o_hi_ready(l, i + 1))
                    dve.tensor_tensor(o1_lo[:, i], out[:, 0:T], o1_hi[:, i].bitcast(F32), ALU.subtract).then_inc(work.freed_sem(g), 1)
                elif kind in ("A", "C", "B"):
                    n = "ACB".index(kind) * KT + i
                    if kind == "A":
                        dve.wait_ge(*gate_ready(l, i + 1))
                        dve.scalar_tensor_tensor(merged[:, i], gate[:, i % 2], 1.0, out[:, T:2 * T], ALU.add,
                                                 ALU.mult).then_inc(work.freed_sem(g), 1)
                        convolve(10)
                        dve.drain().then_inc(merge_step.sem, 1)
                    else:
                        if kind == "C":
                            dve.wait_ge(*work.taken(l, g))
                            dve.scalar_tensor_tensor(sq[:, i % 2], gate[:, i % 2], 1.0, y_b[:, i % 2], ALU.add, ALU.mult)
                        else:
                            dve.wait_ge(*gate_ready(l, KT + i + 1))
                            dve.scalar_tensor_tensor(sq[:, i % 2], gate[:, i % 2], 1.0, out[:, T:2 * T], ALU.add,
                                                     ALU.mult).then_inc(work.freed_sem(g), 1)
                        dve.drain()
                        dve.tensor_tensor(merged[:, i], merged[:, i], sq[:, i % 2], ALU.add).then_inc(merge_step.sem, 1)
                        if kind == "B":
                            dve.wait_ge(*m_hi_ready(l, i + 1))
                            dve.tensor_tensor(m_lo[:, i], merged[:, i], m_hi[:, i].bitcast(F32),
                                              ALU.subtract).then_inc(m_split.sem, 1)
                elif kind == "stat_mu":
                    dve.wait_ge(*work.done(l, g))
                    dve.tensor_scalar(std[:], out[:, 0:T], 1.0 / 512, None, ALU.mult).then_inc(work.freed_sem(g), 1)
                    dve.drain()
                    dve.tensor_tensor(conv[:], conv[:], std[:].unsqueeze(1).to_broadcast([P, 4, T]),
                                      ALU.subtract).then_inc(centred.sem, 1)
                elif kind == "stat_ln":
                    dve.wait_ge(*work.done(l, g))
                    dve.tensor_scalar(std[:], out[:, 0:T], 1.0 / 512, EPS, ALU.mult, ALU.add).then_inc(work.freed_sem(g), 1)
                    dve.wait_ge(*ln_std(l, 1))
                    dve.reciprocal(std[:], std[:])
                    dve.drain()
                    dve.tensor_tensor(conv[:], conv[:], std[:].unsqueeze(1).to_broadcast([P, 4, T]),
                                      ALU.mult).then_inc(ln_made.sem, 1)
                    dve.wait_ge(*cv_hi_ready(l, 1))
                    dve.tensor_tensor(cv_lo[:], conv[:], cv_hi[:].bitcast(F32), ALU.subtract).then_inc(cv_split.sem, 1)
                elif kind == "O":
                    dve.wait_ge(*work.done(l, g))
                    for half, t in enumerate(O_TILES[i]):
                        last = dve.scalar_tensor_tensor(x[:, t], out[:, half * T:half * T + T], 0.5, x[:, t], ALU.mult,
                                                        ALU.add).then_inc(x_mixed.sem, 1)
                    dve.drain().then_inc(work.freed_sem(g), 1)
                if g == ("A", 2):
                    convolve(4 * CONV_TAPS)

        def mixer1_pool(pool, l):
            pool.drain()
            pool.wait_ge(*work1.taken(l, ("pb", 2)))
            pool.tensor_tensor(lat_acc[:, 0:T], scr[:, 0], scr[:, 1], ALU.add)
            pool.tensor_tensor(lat_acc[:, T:2 * T], scr[:, 3], scr[:, 4], ALU.add)
            pool.drain()
            pool.tensor_tensor(lat_acc[:, 0:T], lat_acc[:, 0:T], scr[:, 2], ALU.add).then_inc(lat_summed.sem, 1)
            pool.drain()
            pool.wait_ge(*key_terms(l, 1))
            pool.tensor_tensor(k1[64:96], rope_t[64:96, 0, 0:T].unsqueeze(1).to_broadcast([32, QKV_HEADS, T]),
                               rope_t[64:96, 1, 0:T].unsqueeze(1).to_broadcast([32, QKV_HEADS, T]),
                               ALU.add).then_inc(key_rope_ready.sem, 1)
            for src, ready, said in ((conv, conv_ready, conv_summed), (i_g, centred_sq, dev_summed)):
                pool.drain()
                pool.wait_ge(*ready(l, 1))
                pool.tensor_tensor(acc[:], src[:, 0], src[:, 1], ALU.add)
                for t in range(2, 4):
                    pool.drain()
                    last = pool.tensor_tensor(acc[:], acc[:], src[:, t], ALU.add)
                last.then_inc(said.sem, 1)

        def c2(name, n=0, rows=slice(0, P), width=1):
            return const2[rows, CONST2[name] + n:CONST2[name] + n + width]

        def v2(name, n=0, rows=slice(0, P), width=1):
            return vec[rows, bass.ds(n + VEC2[name], width)]

        def head2(n):
            kind, i, e = HEADS2[n]
            rows = slice(64 * e, 64 * e + 64)
            if kind in ("sel", "win"):
                keys, at = (KS, 0) if kind == "sel" else (KW, GROUPS * HD)
                head = i + 4 * e
                values = [v2b[:, m, at + e * HD:at + (e + 1) * HD] for m in range(2)]
                return rows, NQ + i, keys, values, causal, gates2[:, :, 3 * head + (1 if kind == "sel" else 2)]
            head = 2 * i + e
            q, k, at, bias = (FQ, FK, 0, fox_bias[:, head]) if kind == "fox" else (DQ, DK, 256, c2("dil", width=384))
            return rows, q + i, k + i, [v2a[:, m, at + head * HD:at + (head + 1) * HD] for m in range(2)], bias, None

        ROTATED_ORDER = list(ROTATED)
        qk_rot = sq[:].rearrange("p a t -> p (a t)")

        def mixer2_pe(pe, l):
            st, work = second, work2
            for kind, i in STEPS2:
                g = (kind, i)
                out = work.out(g)
                opens = kind not in ("V", "W") or (HEADS2[i][2] == 0 and HEADS2[i][0] != "win")
                reads = {"R": [("f", i)], "SC": [("c2", 0)], "S": [("f", 5)] if i == 16 else [], "V": [("T", i)],
                         "W": [("T", i)], "O": [last_in_tile(0)] if i == 0 else []}.get(kind, [])
                work.wait_banks_free(pe, l, [g] if opens else [], reads)
                if g in UNIT_OF2:
                    s = UNIT_OF2[g]
                    pe.wait_ge(*st.lo_ready(l, s + 1))
                if kind == "f":
                    for half, t in enumerate(F_TILES[i]):
                        for k in range(KT):
                            if g == ("f", 0) and half == 0:
                                pe.wait_ge(*n2.h_ready(l, k + 1))
                            last = product(pe, out[:, half * T:half * T + T], s, half * KT + k, h_hi[:, k], h_lo[:, k],
                                           k == 0, k == KT - 1)
                elif kind == "R":
                    for half, t in enumerate(ROTATED[i]):
                        last = pe.matmul(out[:, half * T:half * T + T], c2("perm", width=P), feat[:, t], start=True, stop=True)
                elif kind in ("va", "vb"):
                    s = UNIT_OF2[kind, 0]
                    pe.wait_ge(*st.lo_ready(l, s + 2))
                    width = 512 if kind == "va" else VB_COLS
                    for k in range(KT):
                        last = tokens_product(pe, out[:, 0:width], s + k // 4, (k % 4) * width, width,
                                              h_hi[:, k, i * P:(i + 1) * P], h_lo[:, k, i * P:(i + 1) * P], k == 0, k == KT - 1)
                elif kind == "cmp":
                    pe.wait_ge(*win_split(l, 1))
                    for j in range(16):
                        cols_ = slice(32 * j, 32 * j + 32)
                        last = product(pe, out[:, 0:32], s, j, win_hi[:, i // 2, cols_], win_lo[:, i // 2, cols_], j == 0, j == 15)
                elif kind == "c2":
                    pe.wait_ge(*rep_ready(l, 1))
                    for e in range(GROUPS):
                        rows = slice(64 * e, 64 * e + 64)
                        for t in range(2):
                            pe.matmul(out[rows, 0:SLOT], v2("w2k", HD * t, width=HD), h1[:, t, SLOT * e:SLOT * e + SLOT],
                                      start=t == 0, stop=t == 1)
                    for t in range(2):
                        last = pe.matmul(out[:, P:P + HD], h_rep[:, t].rearrange("p a c -> p (a c)"), v2("w2v", HD * t, width=HD),
                                         start=t == 0, stop=t == 1)
                elif kind == "SC":
                    pe.wait_ge(*rotated(l, 3))
                    for q in range(2):
                        for tile in range(4):
                            at = 2 * SLOT * (4 * q + tile)
                            last = pe.matmul(out[:, at:at + 2 * SLOT], feat[:, NQ + tile, q * P:(q + 1) * P], k_cmp[:],
                                             start=True, stop=True)
                elif kind == "TC":
                    pe.wait_ge(*cmp_ready(l, 1))
                    for q in range(2):
                        last = pe.transpose(out[:, q * P:(q + 1) * P], p_cmp[:, 8 * q:8 * q + 8].rearrange("p h n -> p (h n)"), ident)
                elif kind == "cum":
                    pe.wait_ge(*decay_summed(l, 1))
                    for half in range(2):
                        last = pe.matmul(out[:, half * T:half * T + T], c2("pick", P * (2 * i + half), slice(0, FOX_HEADS), P),
                                         decay[:, 3], start=True, stop=True)
                elif kind == "S":
                    rows, q, k, _, _, _ = head2(i)
                    need = {0: 4, 20: 6}.get(i)
                    if need:
                        pe.wait_ge(*rotated(l, need))
                    out = work.out(g)
                    pe.matmul(out[:, 0:P], feat[rows, q, 0:P], feat[rows, k, 0:P], start=True, stop=True)
                    last = pe.matmul(out[:, P:3 * P], feat[rows, q, P:2 * P], feat[rows, k], start=True, stop=True)
                elif kind == "T":
                    pe.wait_ge(*probs2_ready(l, i + 1))
                    for b in range(3):
                        last = pe.transpose(out[:, b * P:(b + 1) * P], probs2[:, i % 2, b * P:(b + 1) * P], ident)
                elif kind in ("V", "W"):
                    what, tile, e = HEADS2[i]
                    nsa = what in ("sel", "win")
                    if what == "sel" and e == 0:
                        pe.wait_ge(*own_ready(l, 1))
                        pe.matmul(out[:, 0:T], v_tile(tile), p_cmp_t[:], start=True, stop=False, skip_group_check=True)
                    values = head2(i)[3]
                    into = out[64 * e:64 * e + 64, 0:T]
                    pe.matmul(into, values[0], probs_t2[:, i % 2, 0:T], start=not nsa, stop=False, skip_group_check=nsa)
                    last = pe.matmul(into[:, P:T], values[1], probs_t2[:, i % 2, T:T + P], start=False, stop=True,
                                     skip_group_check=nsa)
                elif kind == "O":
                    for half, t in enumerate(O2_UNITS[i]):
                        for k in range(KT):
                            if t == 0 and k:
                                pe.wait_ge(*work.taken(l, last_in_tile(k)))
                            last = product(pe, out[:, half * T:half * T + T], s, half * KT + k, o2_hi[:, k], o2_lo[:, k],
                                           k == 0, k == KT - 1)
                last.then_inc(work.done_sem.sem, 1)

        v_tile = lambda i: v_own[:, 2 * i:2 * i + 2].rearrange("p e d -> p (e d)")

        def last_in_tile(k):
            n = {0: 17, 1: 19, 2: 3, 3: 7, 4: 11, 5: 15, 6: 21, 7: 23}[k]
            return ("W", n)

        def tile_of(n):
            kind, i, _ = HEADS2[n]
            return O2_TILE[kind] + i

        TILE_DONE = sorted(LAST_OF_TILE)

        def win_views(tile, par, e):
            v = feat[64 * e:64 * e + 64, tile].rearrange("p (n j a) -> p a j n", j=8, a=2)
            return v[:, par, :, 0:N_CMP], v[:, par, :, 1:N_CMP + 1]

        def mixer2_act(act, l, split):
            st, work = second, work2
            for kind, i in STEPS2:
                g = (kind, i)
                out = work.out(g)
                if g in UNIT_OF2:
                    split.until(UNIT_OF2[g] + AHEAD)
                if kind in ("f", "va", "vb", "cmp", "c2", "TC", "T", "W", "O"):
                    act.wait_ge(*work.done(l, g))
                if kind == "f":
                    if i == 8:
                        act.activation(decay[:, 0], out[0:FOX_HEADS, 0:T], ACT.Identity,
                                       bias=v2("b_forget", rows=slice(0, FOX_HEADS))).then_inc(work.freed_sem(g), 1)
                    else:
                        act.activation(feat[:, 2 * i:2 * i + 2].rearrange("p a t -> p (a t)"), out[:, :],
                                       ACT.Copy).then_inc(work.freed_sem(g), 1)
                elif g == ("R", 0):
                    act.wait_ge(*win_cleared(l, 1))
                    act.wait_ge(*rotated(l, 1))
                    for which, tile in enumerate((KC, VC)):
                        for par in range(2):
                            for e in range(GROUPS):
                                for upper, src in enumerate(win_views(tile, par, e)):
                                    dst = win[64 * par:64 * par + 64, which].rearrange("p (j c) -> p j c", c=32)
                                    last = act.activation(dst[:, 8 * upper:8 * upper + 8, SLOT * e:SLOT * e + N_CMP], src, ACT.Copy)
                    last.then_inc(win_copied.sem, 1)
                elif g == ("R", 1):
                    act.wait_ge(*win_made(l, 1))
                    act.activation(win_hi[:], win[:], ACT.Copy).then_inc(win_hi_ready.sem, 1)
                elif kind == "va":
                    act.activation(v2a[:, i], out[:, :], ACT.Copy).then_inc(work.freed_sem(g), 1)
                elif kind == "vb":
                    act.activation(v2b[:, i], out[:, 0:VB_COLS], ACT.Copy).then_inc(work.freed_sem(g), 1)
                    if i == 1:
                        act.wait_ge(*gate_sums(l, 1))
                        act.activation(gates2[:], gates2[:], ACT.Sigmoid).then_inc(gates_ready.sem, 1)
                elif kind == "cmp":
                    act.activation(h1[:, i], out[:, 0:32], ACT.Gelu_apprx_tanh).then_inc(work.freed_sem(g), 1)
                elif kind == "c2":
                    act.activation(v_cmp[:], out[:, P:P + HD], ACT.Copy)
                    act.activation(k_cmp[0:64, 0:SLOT], out[0:64, 0:SLOT], ACT.Copy)
                    act.activation(k_cmp[64:P, SLOT:2 * SLOT], out[64:P, 0:SLOT], ACT.Copy).then_inc(work.freed_sem(g), 1)
                    act.wait_ge(*forget_abs(l, 1))
                    act.activation(decay[:, 2], decay[:, 1], ACT.Exp, scale=-1.0).then_inc(forget_exp.sem, 1)
                elif kind == "SC":
                    act.wait_ge(*cmp_shifted(l, 1))
                    act.activation(p_cmp[:], p_cmp[:], ACT.Exp).then_inc(cmp_exp.sem, 1)
                elif kind == "TC":
                    act.activation(p_cmp_t[:], out[:, 0:T], ACT.Copy).then_inc(work.freed_sem(g), 1)
                elif kind == "S":
                    softmax_act_exp(act, probs2, row2, i % 2, max2_ready(l, i + 1), exp2_ready)
                elif kind == "T":
                    if i >= 2:
                        act.wait_ge(*work.done(l, ("W" if i - 2 in LAST_OF_TILE else "V", i - 2)))
                    act.activation(probs_t2[:, i % 2, :], out[:, 0:384], ACT.Copy).then_inc(work.freed_sem(g), 1)
                elif kind == "W":
                    act.activation(o2_hi[:, tile_of(i)], out[:, 0:T], ACT.Copy).then_inc(o2_hi_ready.sem, 1)
                elif kind == "O":
                    for half, t in enumerate(O2_UNITS[i]):
                        src = out[:, half * T:half * T + T]
                        square(act, n2, l, KT + t + 1, src, t % 2)
                        last = act.activation(scr[:, t], src, ACT.Copy)
                    last.then_inc(work.freed_sem(g), 1)

        def mixer2_dve(dve, l, split):
            st, work = second, work2
            dve.memset(k_cmp[:], 0.0)
            dve.memset(win[:], 0.0).then_inc(win_cleared.sem, 1)
            for kind, i in STEPS2:
                g = (kind, i)
                out = work.out(g)
                if g in UNIT_OF2:
                    split.until(UNIT_OF2[g] + AHEAD)
                if kind == "R":
                    tiles = ROTATED[i]
                    n, width = len(tiles), len(tiles) * T
                    part = feat[:, tiles[0]:tiles[0] + n]
                    wide = lambda table: table[:].unsqueeze(1).to_broadcast([P, n, T])
                    rot = qk_rot[:, 0:width].rearrange("p (a t) -> p a t", t=T)
                    dve.drain()
                    dve.wait_ge(*work.done(l, g))
                    dve.tensor_tensor(rot, out[:, 0:width].rearrange("p (a t) -> p a t", t=T), wide(sin2), ALU.mult).then_inc(work.freed_sem(g), 1)
                    dve.tensor_tensor(part, part, wide(cos2), ALU.mult)
                    dve.drain()
                    dve.tensor_tensor(part, part, rot, ALU.add).then_inc(rotated.sem, 1)
                    if i == 1:
                        dve.wait_ge(*win_copied(l, 1))
                        for which, name in enumerate(("pos_k", "pos_v")):
                            w = win[:, which].rearrange("p (j c) -> p j c", c=32)
                            last = dve.tensor_tensor(w, w, v2(name, width=16).unsqueeze(2).to_broadcast([P, 16, 32]), ALU.add)
                        last.then_inc(win_made.sem, 1)
                        dve.wait_ge(*win_hi_ready(l, 1))
                        dve.tensor_tensor(win_lo[:], win[:], win_hi[:].bitcast(F32), ALU.subtract).then_inc(win_split.sem, 1)
                elif g == ("f", 8):
                    dve.wait_ge(*work.taken(l, g))
                    dve.tensor_scalar(decay[:, 1], decay[:, 0], -1.0, None, ALU.mult)
                    dve.drain()
                    dve.tensor_tensor(decay[:, 1], decay[:, 1], decay[:, 0], ALU.max).then_inc(forget_abs.sem, 1)
                elif g == ("vb", 1):
                    dve.wait_ge(*work.taken(l, g))
                    bias = v2("b_nsa", width=24).unsqueeze(1).to_broadcast([P, 2, 24])
                    dve.tensor_tensor(gates2[:], v2b[:, :, 256:280], bias, ALU.add).then_inc(gate_sums.sem, 1)
                elif g == ("cmp", 3):
                    dve.wait_ge(*work.taken(l, g))
                    for t in range(2):
                        last = dve.tensor_copy(h_rep[:, t], h1[:, 2 + t].unsqueeze(1).to_broadcast([P, 4, 2 * SLOT]))
                    last.then_inc(rep_ready.sem, 1)
                elif kind == "c2":
                    dve.wait_ge(*work.taken(l, g))
                    dve.tensor_tensor(v_own[:], v_cmp[:].unsqueeze(1).to_broadcast([P, NSA_HEADS, HD]),
                                      c2("own", width=NSA_HEADS).unsqueeze(2).to_broadcast([P, NSA_HEADS, HD]),
                                      ALU.mult).then_inc(own_ready.sem, 1)
                    dve.wait_ge(*forget_exp(l, 1))
                    log1p_series(dve, decay[:, 2], decay[:, 4], decay[:, 1], decay[:, 3])
                    dve.scalar_tensor_tensor(decay[:, 1], decay[:, 0], 0.0, decay[:, 4], ALU.min, ALU.subtract)
                    dve.memset(decay[:, 2], 0.0)
                    dve.drain()
                    dve.tensor_tensor_scan(decay[:, 3], decay[:, 1], decay[:, 2], 0.0, ALU.add, ALU.add).then_inc(decay_summed.sem, 1)
                elif kind == "SC":
                    dve.wait_ge(*work.done(l, g))
                    per_q = lambda ap, q: ap[:, 8 * q:8 * q + 8]
                    mask = lambda name, q: c2(name, SLOT * q, width=SLOT).unsqueeze(1).to_broadcast([P, NSA_HEADS, SLOT])
                    src = out[:, 0:2 * NSA_HEADS * SLOT].rearrange("p (h n) -> p h n", n=SLOT)
                    spread = lambda r: row_cmp[:, r].unsqueeze(2).to_broadcast([P, 2 * NSA_HEADS, SLOT])
                    for q in range(2):
                        last = dve.scalar_tensor_tensor(per_q(p_cmp, q), per_q(src, q), ATTN_SCALE, mask("cmp_bias", q), ALU.mult, ALU.add)
                    last.then_inc(work.freed_sem(g), 1)
                    dve.drain()
                    dve.tensor_reduce(row_cmp[:, 0], p_cmp[:], AX.X, ALU.max)
                    dve.drain()
                    dve.tensor_tensor(p_cmp[:], p_cmp[:], spread(0), ALU.subtract).then_inc(cmp_shifted.sem, 1)
                    dve.wait_ge(*cmp_exp(l, 1))
                    for q in range(2):
                        dve.tensor_tensor(per_q(p_cmp, q), per_q(p_cmp, q), mask("cmp_keep", q), ALU.mult)
                    dve.drain()
                    dve.tensor_reduce(row_cmp[:, 0], p_cmp[:], AX.X, ALU.add)
                    dve.drain()
                    dve.tensor_scalar(row_cmp[:, 0], row_cmp[:, 0], 1e-30, None, ALU.max)
                    dve.drain()
                    dve.reciprocal(row_cmp[:, 1], row_cmp[:, 0])
                    dve.drain()
                    dve.wait_ge(*gates_ready(l, 1))
                    heads = lambda r: row_cmp[:, r].rearrange("p (q i e) -> p q i e", q=2, e=2)
                    for q in range(2):
                        dve.tensor_tensor(heads(0)[:, q], heads(1)[:, q],
                                          gates2[:, q].rearrange("p (e i b) -> p i e b", e=2, b=3)[:, :, :, 0], ALU.mult)
                    dve.drain()
                    dve.tensor_tensor(p_cmp[:], p_cmp[:], spread(0), ALU.mult).then_inc(cmp_ready.sem, 1)
                elif kind == "cum":
                    dve.wait_ge(*work.done(l, g))
                    for half in range(2):
                        h = 2 * i + half
                        c = out[:, half * T:half * T + T]
                        dve.tensor_tensor(fox_bias[:, h, 0:P], causal[:, 0:P], c[:, 0:P], ALU.subtract)
                        last = dve.tensor_tensor(fox_bias[:, h, P:384], causal[:, P:384], c, ALU.subtract)
                    last.then_inc(work.freed_sem(g), 1)
                elif kind == "S":
                    bias, gate_ = head2(i)[4:]
                    if i >= 2:
                        dve.wait_ge(*work.done(l, ("T", i - 2)))
                    softmax_dve_max(dve, work, l, g, ATTN_SCALE, bias, probs2, row2, i % 2, max2_ready)
                elif kind == "W":
                    n = TILE_DONE.index(i)
                    dve.wait_ge(*o2_hi_ready(l, n + 1))
                    dve.tensor_tensor(o2_lo[:, tile_of(i)], out[:, 0:T], o2_hi[:, tile_of(i)].bitcast(F32),
                                      ALU.subtract).then_inc(work.freed_sem(g), 1)
                nxt = STEPS2.index(g) + 1
                if nxt < len(STEPS2) and STEPS2[nxt][0] == "T":
                    n = STEPS2[nxt][1]
                    softmax_dve_norm(dve, probs2, row2, n % 2, exp2_ready(l, n + 1), probs2_ready, head2(n)[5])

        def post_norm_dve(dve, l, n, m, gains):
            norm_dve_scale(dve, work2, n2, l, n)
            for t in range(KT):
                dve.scalar_tensor_tensor(scr[:, t], scr[:, t], gains(t), std[:], ALU.mult, ALU.mult)
            dve.drain()
            for t in range(KT):
                dve.tensor_tensor(x[:, t], x[:, t], scr[:, t], ALU.add).then_inc(x_new.sem, 1)

        def post_norm_act(act, l, n, m):
            norm_act_root(act, work2, n2, l, n)
            for t in range(KT):
                act.wait_ge(*x_new(l, KT * m + t + 1))
                square(act, n2, l, KT * (n + 1) + t + 1, x[:, t], t % 2)

        def ffn2_act(act, l, split):
            up, down, st, work, at = "up0", "down0", second, work2, FFN2_AT
            floor = work.g.mark[up, 0] - 1
            wcol = lambda j, half, tap: v2("conv_w", j + tap * 2 * FT + half * FT)
            bcol = lambda j, half: v2("conv_b", j + half * FT)

            def gated(j, more, parity, split_next):
                out = banks[j % 4]
                act.wait_ge(*work.done(l, (up, 0), more + j))
                act.activation(silu[:, parity], out[:, 0:T], ACT.Identity, scale=wcol(more + j, 0, 2), bias=bcol(more + j, 0))
                act.activation(conv2[:, parity], out[:, T:2 * T], ACT.Identity, scale=wcol(more + j, 1, 2),
                               bias=bcol(more + j, 1)).then_inc(last_tap_ready.sem, 1)
                split_next()
                act.wait_ge(*work.taken(l, (up, 0), more + j))
                act.activation(silu[:, parity], silu[:, parity], ACT.Silu).then_inc(silu2_ready.sem, 1)
                act.wait_ge(*hid2_made(l, more + (j + 1)))
                act.activation(hid_hi[:, more + j], hid[:, parity], ACT.Copy).then_inc(hid2_hi_ready.sem, 1)

            with act.Fori(0, 4) as it:
                for u in range(4):
                    gated(u, it * 4, u % 2, lambda: split_hi(act, st, work, l, at + u + AHEAD, it * 4, it * 2, floor))
            split.next = at + 16 + AHEAD
            for j in range(16, FT):
                gated(j, 0, j % 2, lambda: split.until(at + j + AHEAD))
            base = at + FT + AHEAD

            def output(t, more):
                act.wait_ge(*work.done(l, (down, 0), more * 2 + 2 * t))
                square(act, n2, l, more + (KT * 3 + t + 1), banks[2 + t % 2][:, 0:T], t % 2)
                act.activation(scr[:, more + t], banks[2 + t % 2][:, 0:T], ACT.Copy).then_inc(work.freed["a"].sem, 1)

            with act.Fori(0, 3) as it:
                for g in range(2):
                    for e in range(2):
                        split_hi(act, st, work, l, base + 2 * g + e, it * 4, it * 2)
                    output(g, it * 2)
            split.next = base + 12
            for t in range(6, KT):
                split.until(base + 2 * t + 1)
                output(t, 0)

        def ffn2_dve(dve, l, split):
            up, st, work, at = "up0", second, work2, FFN2_AT
            wcol = lambda j, half, tap: v2("conv_w", j + tap * 2 * FT + half * FT)

            def gated(j, more, parity, split_next):
                out = banks[j % 4]
                dve.wait_ge(*last_tap_ready(l, more + (j + 1)))
                for back in (1, 2):
                    for half, into in enumerate((silu, conv2)):
                        part = into[:, parity, back:T]
                        last = dve.scalar_tensor_tensor(part, out[:, half * T:half * T + T - back], wcol(more + j, half, 2 - back),
                                                        part, ALU.mult, ALU.add)
                    if back == 1:
                        dve.drain()
                last.then_inc(work.freed["v"].sem, 1)
                split_next()
                dve.wait_ge(*silu2_ready(l, more + (j + 1)))
                dve.tensor_tensor(hid[:, parity], silu[:, parity], conv2[:, parity], ALU.mult).then_inc(hid2_made.sem, 1)
                dve.wait_ge(*hid2_hi_ready(l, more + (j + 1)))
                dve.tensor_tensor(hid_lo[:, more + j], hid[:, parity], hid_hi[:, more + j].bitcast(F32),
                                  ALU.subtract).then_inc(hid2_ready.sem, 1)

            with dve.Fori(0, 4) as it:
                for u in range(4):
                    gated(u, it * 4, u % 2, lambda: split_lo(dve, st, l, at + u + AHEAD, it * 4))
            split.next = at + 16 + AHEAD
            for j in range(16, FT):
                gated(j, 0, j % 2, lambda: split.until(at + j + AHEAD))
            base = at + FT + AHEAD
            with dve.Fori(0, 3) as it:
                for u in range(4):
                    split_lo(dve, st, l, base + u, it * 4)
            split.next = base + 12
            split.until(len(st.units) - 1)

        MAGIC = 1.5 * 2 ** 23

        def rotary_dve(dve, table, pos, whole, freq, phase, done):
            dve.tensor_scalar(table, pos, freq, None, ALU.mult)
            dve.drain()
            dve.tensor_scalar(whole, table, phase, 1.0 / TWO_PI, ALU.add, ALU.mult)
            dve.drain()
            dve.tensor_scalar(whole, whole, MAGIC, None, ALU.add)
            dve.drain()
            dve.tensor_scalar(whole, whole, -MAGIC, None, ALU.add)
            for part in (6.28125, 0.0019350051879882812, 3.019915981956753e-07):
                dve.drain()
                dve.scalar_tensor_tensor(table, whole, -part, table, ALU.mult, ALU.add)
            dve.drain()
            dve.tensor_scalar(table, table, phase, 3.1415925, ALU.add, ALU.min)
            dve.drain()
            dve.tensor_scalar(table, table, -3.1415925, None, ALU.max).then_inc(done.sem, 1)

        pos_i = scr[:, 0].bitcast(I32)
        freq1 = const[:, CONST["freq1"]:CONST["freq1"] + 1]
        phase1 = const[:, CONST["phase1"]:CONST["phase1"] + 1]
        final_gain = lambda t: const[:, CONST["final"] + t:CONST["final"] + t + 1]
        xv = lambda ap: ap.rearrange("p (k t) -> p k t", k=KT)
        w1_rows = io["w1"].shape[1]

        def stream(w, units, at, l, count=1):
            start = sum(units[:at]) * BLOCK
            n = units[at] * BLOCK
            view = w[l, start:start + n * count].rearrange("(u p n) -> u p n", p=P, n=units[at] * P)
            return view

        block = ctx.enter_context(nc.Block())

        @block.sync
        def _(sp):
            sp.dma_start(const[:], io["const"]).then_inc(consts_in.sem, 16)
            sp.dma_start(x[:], xv(io["x"])).then_inc(x_in.sem, 16)
            sp.dma_start(pos_i, io["pos1"].to_broadcast([P, T])).then_inc(x_in.sem, 16)
            with sp.Fori(0, DEPTH) as l:
                sp.wait_ge(*vec_free(l, 0))
                sp.dma_start(vec[:, 0:NVEC1], io["vec1"][l]).then_inc(vec_full.sem, 16)
                for at in (0, FFN1_AT):
                    if at:
                        for s in range(MIX1_AT, FFN1_AT):
                            load_unit(sp, first, l, s, stream(io["w1"], UNITS1, s, l)[0])
                    load_loop(sp, first, l, stream(io["w1"], UNITS1, at, l, FT), at, FT, 16)
                    load_loop(sp, first, l, stream(io["w1"], UNITS1, at + FT, l, 2 * KT), at + FT, 2 * KT, HALF)
            sp.wait_ge(*x_final(0, KT))
            sp.dma_start(const2[:], io["const2"]).then_inc(consts2_in.sem, 16)
            sp.dma_start(pos_i, io["pos2"].to_broadcast([P, T])).then_inc(consts2_in.sem, 16)
            sp.wait_ge(*vec_free(DEPTH, 0))
            sp.wait_ge(*first.lo_ready(DEPTH - 1, len(UNITS1)))
            with sp.Fori(0, DEPTH) as l:
                sp.wait_ge(*vec2_free(l, 0))
                sp.dma_start(vec[:, 0:NVEC2], io["vec2"][l]).then_inc(vec2_full.sem, 16)
                for s in range(FFN2_AT):
                    load_unit(sp, second, l, s, stream(io["w2"], UNITS2, s, l)[0])
                load_loop(sp, second, l, stream(io["w2"], UNITS2, FFN2_AT, l, FT), FFN2_AT, FT, 16)
                load_loop(sp, second, l, stream(io["w2"], UNITS2, FFN2_AT + FT, l, 2 * KT), FFN2_AT + FT, 2 * KT, HALF)
            for t in range(0, KT, 2):
                sp.wait_ge(*x_new(DEPTH - 1, KT + t + 2))
                sp.dma_start(xv(io["out"])[:, t:t + 2], x[:, t:t + 2]).then_inc(out_done.sem, 16)
            sp.wait_ge(out_done.sem, 16 * KT // 2)

        @block.tensor
        def _(pe):
            pe.wait_ge(consts_in.sem, 16)
            with pe.Fori(0, DEPTH) as l:
                norm_pe(pe, work1, n1, l, 0)
                ffn_pe(pe, first, work1, n1, l, 0, 0, 0, hid_ready)
                norm_pe(pe, work1, n1, l, 1)
                mixer1_pe(pe, l)
                norm_pe(pe, work1, n1, l, 2)
                ffn_pe(pe, first, work1, n1, l, 1, FFN1_AT, 2, hid_ready)
            norm_pe(pe, work1, n1, DEPTH, 0)
            with pe.Fori(0, DEPTH) as l:
                norm_pe(pe, work2, n2, l, 0)
                mixer2_pe(pe, l)
                norm_pe(pe, work2, n2, l, 1)
                norm_pe(pe, work2, n2, l, 2)
                ffn_pe(pe, second, work2, n2, l, 0, FFN2_AT, 1, hid2_ready)
                norm_pe(pe, work2, n2, l, 3)

        @block.scalar
        def _(act):
            def one(l):
                return lambda s: split_hi(act, first, work1, l, s)
            act.wait_ge(setup_v.sem, 1)
            act.activation(trig1[:], trig1[:], ACT.Sin).then_inc(trig_ready.sem, 1)
            act.wait_ge(x_in.sem, 32)
            for t in range(KT):
                square(act, n1, 0, t + 1, x[:, t], t % 2)
            with act.Fori(0, DEPTH) as l:
                act.wait_ge(*vec_full(l, 16))
                split = Splitter(one(l), len(UNITS1))
                split.until(0)
                norm_act_root(act, work1, n1, l, 0)
                norm_act_split(act, n1, l, 0)
                split.until(AHEAD - 1)
                ffn_act(act, l, 0, 0, 0, split)
                norm_act_root(act, work1, n1, l, 1)
                norm_act_split(act, n1, l, 1)
                mixer1_act(act, l, split)
                norm_act_root(act, work1, n1, l, 2)
                norm_act_split(act, n1, l, 2)
                ffn_act(act, l, 1, FFN1_AT, 2, split)
                act.drain().then_inc(vec_free.sem, 1)
            norm_act_root(act, work1, n1, DEPTH, 0)
            for t in range(KT):
                act.wait_ge(*x_final(0, t + 1))
                square(act, n2, 0, t + 1, x[:, t], t % 2)
            act.wait_ge(*turned(0, 2))
            act.activation(cos2[:], cos2[:], ACT.Sin)
            act.activation(sin2[:], sin2[:], ACT.Sin).then_inc(trig2_ready.sem, 1)
            with act.Fori(0, DEPTH) as l:
                act.wait_ge(*vec2_full(l, 16))
                split = Splitter(lambda s: split_hi(act, second, work2, l, s), len(UNITS2))
                split.until(0)
                norm_act_root(act, work2, n2, l, 0)
                norm_act_split(act, n2, l, 0)
                split.until(AHEAD - 1)
                mixer2_act(act, l, split)
                post_norm_act(act, l, 1, 0)
                norm_act_root(act, work2, n2, l, 2)
                norm_act_split(act, n2, l, 1)
                ffn2_act(act, l, split)
                post_norm_act(act, l, 3, 1)
                act.drain().then_inc(vec2_free.sem, 1)

        @block.vector
        def _(dve):
            def one(l):
                return lambda s: split_lo(dve, first, l, s)
            for s in (first.lo_ready, work1.done_sem, work1.freed["v"], work1.freed["a"], n1.sq_summed, vec_free,
                      second.lo_ready, work2.done_sem, work2.freed["v"], work2.freed["a"], n2.sq_summed, vec2_free):
                dve.sem_inc(s.sem, s.per)
            dve.wait_ge(consts_in.sem, 16)
            dve.wait_ge(x_in.sem, 32)
            dve.tensor_copy(scr[:, 1], pos_i)
            dve.drain()
            rotary_dve(dve, trig1[:], scr[:, 1], scr[:, 2], freq1, phase1, setup_v)
            with dve.Fori(0, DEPTH) as l:
                dve.wait_ge(*vec_full(l, 16))
                split = Splitter(one(l), len(UNITS1))
                split.until(0)
                norm_dve(dve, work1, n1, l, 0, 0, lambda t: col("norm0", t))
                split.until(AHEAD - 1)
                ffn_dve(dve, l, 0, 0, 0, split)
                norm_dve(dve, work1, n1, l, 1, 1, lambda t: col("norm1", t))
                mixer1_dve(dve, l, split)
                norm_dve(dve, work1, n1, l, 2, 2, lambda t: col("norm2", t))
                ffn_dve(dve, l, 1, FFN1_AT, 2, split)
                dve.drain().then_inc(vec_free.sem, 1)
            norm_dve_scale(dve, work1, n1, DEPTH, 0)
            for t in range(KT):
                dve.scalar_tensor_tensor(x[:, t], x[:, t], final_gain(t), std[:], ALU.mult, ALU.mult).then_inc(x_final.sem, 1)
            dve.wait_ge(consts2_in.sem, 32)
            dve.drain()
            dve.tensor_copy(scr[:, 1], pos_i)
            dve.drain()
            rotary_dve(dve, cos2[:], scr[:, 1], scr[:, 2], c2("freq_c"), c2("phase_c"), turned)
            dve.drain()
            rotary_dve(dve, sin2[:], scr[:, 1], scr[:, 2], c2("freq_s"), c2("phase_s"), turned)
            dve.wait_ge(*trig2_ready(0, 1))
            with dve.Fori(0, DEPTH) as l:
                dve.wait_ge(*vec2_full(l, 16))
                split = Splitter(lambda s: split_lo(dve, second, l, s), len(UNITS2))
                split.until(0)
                norm_dve(dve, work2, n2, l, 0, 0, lambda t: v2("norm0", t))
                split.until(AHEAD - 1)
                mixer2_dve(dve, l, split)
                post_norm_dve(dve, l, 1, 0, lambda t: v2("norm1", t))
                norm_dve(dve, work2, n2, l, 2, 1, lambda t: v2("norm2", t))
                ffn2_dve(dve, l, split)
                post_norm_dve(dve, l, 3, 1, lambda t: v2("norm3", t))
                dve.drain().then_inc(vec2_free.sem, 1)

        @block.gpsimd
        def _(pool):
            sum_squares(pool, n1, 0, 1)
            with pool.Fori(0, DEPTH) as l:
                sum_squares(pool, n1, l, KT + 1)
                mixer1_pool(pool, l)
                sum_squares(pool, n1, l, 2 * KT + 1)
                sum_squares(pool, n1, l, 3 * KT + 1)
            sum_squares(pool, n2, 0, 1)
            with pool.Fori(0, DEPTH) as l:
                for n in range(1, 5):
                    sum_squares(pool, n2, l, KT * n + 1)


def tile_blocks(w, rows=None):
    k, c = w.shape
    return w.reshape(k // P, P, c).transpose(1, 0, 2).reshape(P, -1)


def unit(*parts):
    return np.concatenate(parts, axis=1).ravel()


def ffn_units(w1, w2, inner=FF):
    out = []
    for j in range(FT):
        out.append(unit(tile_blocks(w1[:, j * P:(j + 1) * P]), tile_blocks(w1[:, FF + j * P:FF + (j + 1) * P])))
    for t in range(KT):
        for half in range(2):
            out.append(unit(tile_blocks(w2[half * HALF * P:(half + 1) * HALF * P, t * P:(t + 1) * P])))
    return out


def tiles_of(w, tiles):
    return unit(*(tile_blocks(w[:, t * P:(t + 1) * P]) for t in tiles))


def pe_swapped(w):
    return np.concatenate([w, w[..., 16:32], w[..., 0:16]], axis=-1)


def mixer1_units(i, l):
    w = i["w_in"][l]
    pa, pb, pc, pg = np.split(w, [1024, 1696, 2720], axis=1)
    out = []
    key = np.concatenate([np.zeros((D, 64), w.dtype), pe_swapped(pb[:, 640:672])], axis=1)
    lat = np.concatenate([pb[:, 0:640], key], axis=1)
    out += [tiles_of(lat, (2 * n, 2 * n + 1)) for n in range(3)]
    out += [tiles_of(pc, (n, 4 + n)) for n in range(4)]
    out += [tiles_of(pa, (n, 4 + n)) for n in range(4)]
    uq = i["w_uq"][l].reshape(384, QKV_HEADS, NOPE + ROPE)
    uq = np.concatenate([uq[..., :NOPE], pe_swapped(uq[..., NOPE:])], axis=-1)
    out += [unit(*(tile_blocks(uq[:, 4 * n + h]) for h in range(4))) for n in range(2)]
    ukv = i["w_ukv"][l].reshape(256, QKV_HEADS, NOPE + VD)
    uk = np.ascontiguousarray(ukv[..., :NOPE]).reshape(256, -1)
    uv = np.ascontiguousarray(ukv[..., NOPE:]).reshape(256, -1)
    out.append(unit(*(tile_blocks(uk[:, c * P:(c + 1) * P]) for c in range(4)), tile_blocks(uv)))
    gates = []
    for part in range(2):
        for t in range(4):
            b = np.zeros((P, P), w.dtype)
            for e in range(2):
                b[64 * e:64 * e + 64, 64 * e:64 * e + 64] = i["lru_w_gate"][l, 2 * t + e, :, 64 * part:64 * part + 64]
            gates.append(b)
    out.append(unit(*gates))
    for branch, name in ((0, "lru_w_out"), (2, "conv_w_out"), (1, "mla_w_o")):
        g = pg[:, branch * D:(branch + 1) * D]
        y = i[name][l]
        out += [unit(tile_blocks(g[:, t * P:(t + 1) * P]), tile_blocks(y[:, t * P:(t + 1) * P])) for t in range(KT)]
    out += [tiles_of(i["w_out"][l], ts) for ts in ((0, 1), (2, 3), (4, 5), (6,), (7,))]
    return out


def stack_units(layers):
    return np.stack([np.concatenate(units) for units in layers])


def cols(v):
    return v.reshape(-1, P).T


def vec1_of(i, l):
    b = i["b_in"][l]
    kpe = np.concatenate([np.zeros(64, b.dtype), pe_swapped(b[1664:1696])])
    gb = i["lru_b_gate"][l]
    by = dict(norm0=cols(i["ffn1_norm"][l]), norm1=cols(i["mix_norm"][l]), norm2=cols(i["ffn2_norm"][l]),
              b_pb=cols(np.concatenate([b[1024:1664], kpe])), b_pc=cols(b[1696:2720]), b_pa=cols(b[0:1024]),
              b_gate=cols(b[2720:]), lru_b=cols(i["lru_conv_b"][l]),
              lru_w=i["lru_conv_w"][l].T.reshape(4, P, LRU_TAPS).transpose(1, 0, 2).reshape(P, -1),
              lru_br=cols(np.ascontiguousarray(gb[:, 0:64]).ravel()), lru_bi=cols(np.ascontiguousarray(gb[:, 64:128]).ravel()),
              lam=cols(i["lru_lambda"][l]), q_norm=cols(i["q_norm"][l]), kv_norm=cols(i["kv_norm"][l]),
              dw_w=i["conv_dw_w"][l].T.reshape(4, P, CONV_TAPS).transpose(1, 0, 2).reshape(P, -1),
              dw_b=cols(i["conv_dw_b"][l]), ln_g=cols(i["conv_ln_g"][l]), ln_b=cols(i["conv_ln_b"][l]),
              b_pw=cols(i["conv_b_out"][l]))
    out = np.concatenate([by[name] for name in VEC1], axis=1)
    assert out.shape == (P, NVEC1)
    return out


def causal_bias():
    q, k = np.arange(P)[:, None], np.arange(P)[None, :]
    tri = np.where(k <= q, 0.0, MASKED)
    return np.concatenate([tri, np.zeros((P, P)), tri], axis=1)


def const_of(i):
    freq, phase = np.zeros((P, 1)), np.zeros((P, 1))
    inv = 10000.0 ** (-np.arange(0, ROPE, 2, dtype=np.float64) / ROPE)
    freq[64:128, 0] = np.concatenate([inv, inv, -inv, inv])
    phase[64:96] = np.pi / 2
    parts = dict(ones=np.ones((P, P)), ident=np.eye(P), causal=causal_bias(), freq1=freq, phase1=phase)
    parts = {k: v.astype(np.float32) for k, v in parts.items()}
    parts["final"] = cols(i["final_norm"])
    return np.concatenate([parts[k] for k in CONST], axis=1)


def mixer2_units(i, l):
    names = ("fq", "fk", "fv", "ff", "nq", "kc", "vc", "ks", "vs", "kw", "vw", "ng", "dq", "dk", "dv")
    widths = (256, 256, 256, 4, 512, 128, 128, 128, 128, 128, 128, 24, 256, 256, 256)
    w = dict(zip(names, np.split(i["w_in_2"][l], np.cumsum(widths)[:-1], axis=1)))
    nq = w["nq"].reshape(D, 2, 4, HD).transpose(0, 2, 1, 3).reshape(D, 512)
    pad = lambda a, n: np.concatenate([a, np.zeros((D, n - a.shape[1]), a.dtype)], axis=1)
    tiles = np.concatenate([w["kc"], w["vc"], nq, w["ks"], w["kw"], w["fq"], w["fk"], w["dq"], w["dk"], pad(w["ff"], P)], axis=1)
    va = np.concatenate([w["fv"], w["dv"]], axis=1)
    vb = pad(np.concatenate([w["vs"], w["vw"], w["ng"]], axis=1), VB_COLS)
    out_rows = i["w_out_2"][l]
    nsa = out_rows[256:768].reshape(2, 4, HD, D).transpose(1, 0, 2, 3).reshape(512, D)
    out_rows = np.concatenate([out_rows[:256], nsa, out_rows[768:]], axis=0)
    out = []
    for kind, n in UNIT_ORDER2:
        if kind == "f":
            out.append(tiles_of(tiles, F_TILES[n]))
        elif kind in ("va", "vb"):
            out.append(unit(tile_blocks((va if kind == "va" else vb)[512 * n:512 * n + 512])))
        elif kind == "cmp":
            w1 = i["cmp_w1_k_2" if n < 2 else "cmp_w1_v_2"][l]
            out.append(unit(tile_blocks(w1[:, P * (n % 2):P * (n % 2) + P])))
        else:
            out.append(tiles_of(out_rows, O2_UNITS[n]))
    assert [o.size // BLOCK for o in out] == UNITS2[:FFN2_AT]
    return out


def vec2_of(i, l):
    pos = lambda a: a.reshape(16, 2 * HD).T
    by = dict(norm0=cols(i["attn_pre_norm_2"][l]), norm1=cols(i["attn_post_norm_2"][l]), norm2=cols(i["ffn_pre_norm_2"][l]),
              norm3=cols(i["ffn_post_norm_2"][l]),
              b_forget=np.concatenate([i["b_forget_2"][l], np.zeros(P - FOX_HEADS, np.float32)])[:, None],
              b_nsa=np.tile(i["b_nsa_gate_2"][l][None], (P, 1)), pos_k=pos(i["cmp_pos_k_2"][l]), pos_v=pos(i["cmp_pos_v_2"][l]),
              w2k=tile_blocks(i["cmp_w2_k_2"][l]), w2v=tile_blocks(i["cmp_w2_v_2"][l]),
              conv_w=np.concatenate([cols(i["conv_w_2"][l, tap]) for tap in range(3)], axis=1), conv_b=cols(i["conv_b_2"][l]))
    out = np.concatenate([by[name] for name in VEC2], axis=1)
    assert out.shape == (P, NVEC2)
    return out


def const2_of():
    p = np.arange(P)
    perm = np.zeros((P, P))
    for m in p:
        if m % HD < 2 * ROPE2_HALF:
            perm[m + ROPE2_HALF if m % HD < ROPE2_HALF else m - ROPE2_HALF, m] = 1
    q, k = np.arange(T)[:, None], np.arange(T)[None, :]
    back = q - k
    times = sum(((back >= 0) & (back <= w) & (back % d == 0)).astype(int) for w, d in DIL_PATTERNS)
    dil = np.where(times > 0, np.log(np.maximum(times, 1)), MASKED)
    dil = np.concatenate([dil[:P, :P], dil[P:]], axis=1)
    pick = np.zeros((P, FOX_HEADS, P))
    for h in range(FOX_HEADS):
        pick[h, h] = 1
    n = np.arange(SLOT)
    keep = np.stack([(n[None] < N_CMP) & (n[None] * CMP_STRIDE + CMP_BLOCK - 1 <= (p + P * half)[:, None]) for half in range(2)], axis=1)
    own = np.zeros((P, NSA_HEADS))
    for head in range(NSA_HEADS):
        own[SLOT * head:SLOT * head + SLOT, head] = 1
    inv = 500000.0 ** (-2.0 * np.arange(ROPE2_HALF) / (2 * ROPE2_HALF))
    d = p % HD
    freq = np.where(d < 2 * ROPE2_HALF, inv[d % ROPE2_HALF], 0.0)
    parts = dict(perm=perm, dil=dil, pick=pick.reshape(P, -1), cmp_bias=np.where(keep, 0.0, MASKED).reshape(P, -1),
                 cmp_keep=keep.reshape(P, -1), own=own, freq_c=freq[:, None], freq_s=np.where(d < ROPE2_HALF, -freq, freq)[:, None],
                 phase_c=np.full((P, 1), np.pi / 2), phase_s=np.zeros((P, 1)))
    return np.concatenate([parts[name].astype(np.float32) for name in CONST2], axis=1)


def kernel(**i):
    import concourse.bacc as bacc
    from concourse.bass_utils import run_bass_kernel_spmd as run

    i = {name: np.asarray(a) for name, a in i.items()}
    nc = bacc.Bacc("TRN2", target_bir_lowering=False, num_devices=1)
    arrays = {
        "x": np.ascontiguousarray(i["x"][0].T.reshape(KT, P, T).transpose(1, 0, 2)).reshape(P, -1),
        "pos1": np.ascontiguousarray(i["positions"]),
        "pos2": np.ascontiguousarray(i["positions_2"]),
        "const": const_of(i),
        "const2": const2_of(),
        "vec1": np.stack([vec1_of(i, l) for l in range(DEPTH)]),
        "vec2": np.stack([vec2_of(i, l) for l in range(DEPTH)]),
        "w1": stack_units([ffn_units(i["ffn1_w1"][l], i["ffn1_w2"][l]) + mixer1_units(i, l)
                           + ffn_units(i["ffn2_w1"][l], i["ffn2_w2"][l]) for l in range(DEPTH)]),
        "w2": stack_units([mixer2_units(i, l) + ffn_units(i["w_up_2"][l], i["w_down_2"][l]) for l in range(DEPTH)]),
    }
    io = {n: nc.dram_tensor("in_" + n, a.shape, mybir.dt.from_np(a.dtype), kind="ExternalInput").ap() for n, a in arrays.items()}
    io["out"] = nc.dram_tensor("out", (P, KT * T), F32, kind="ExternalOutput").ap()
    build(nc, io)
    r = run(nc, [{"in_" + n: a for n, a in arrays.items()}], core_ids=[0])
    got = r.results[0]["out"]
    return np.ascontiguousarray(got.reshape(P, KT, T).transpose(2, 1, 0)).reshape(1, T, D)
```

```python
import concourse.bass as bass
from concourse import mybir
from contextlib import ExitStack
import numpy as np

F32 = mybir.dt.float32
F32R = mybir.dt.float32r
I32 = mybir.dt.int32
ACT = mybir.ActivationFunctionType
ALU = mybir.AluOpType
AX = mybir.AxisListType

T = 256
P = 128
D = 1024
KT = D // P
DEPTH = 2
FF = 2816
FT = FF // P
HALF = FT // 2
BLOCK = P * P
RAW_SLOTS = 2
SPLIT_SLOTS = 4
AHEAD = 3
EPS = 1e-6
MASKED = -1e30
TWO_PI = 2 * np.pi
LOG_EXP = "natural_log_exp_and_others"
SILU = "silu_and_others"

FFN_UNITS = [16] * FT + [HALF] * (2 * KT)
UNIT_ORDER1 = ([("pa", i) for i in range(4)]
               + [("pb", 0), ("pb", 1), ("lr", 0), ("pb", 2)]
               + [("pc", i) for i in range(4)]
               + [("uq", 0), ("uq", 2), ("uk", 0)]
               + [(kind, t) for kind in "ABC" for t in range(KT)]
               + [("O", i) for i in range(5)])
UNIT_BLOCKS1 = dict(pa=16, pb=16, lr=8, pc=16, uq=12, uk=16, A=12, B=12, C=12, O=16)
MIX1_UNITS = [8 if u in (("O", 3), ("O", 4)) else UNIT_BLOCKS1[u[0]] for u in UNIT_ORDER1]
UNITS1 = FFN_UNITS + MIX1_UNITS + FFN_UNITS
MIX1_AT = len(FFN_UNITS)
FFN1_AT = MIX1_AT + len(MIX1_UNITS)
assert len(UNITS1) % SPLIT_SLOTS == 0

QKV_HEADS, NOPE, ROPE, VD = 8, 64, 32, 64
MLA_SCALE = (NOPE + ROPE) ** -0.5
CONV_TAPS, LRU_TAPS = 31, 4


def columns(fields):
    at, out = 0, {}
    for name, n in fields:
        out[name] = at
        at += n
    return out, at


VEC1, NVEC1 = columns([("norm0", 8), ("norm1", 8), ("norm2", 8), ("b_pb", 6), ("b_pc", 8), ("b_pa", 8), ("b_gate", 24),
                       ("lru_w", 16), ("lru_b", 4), ("lru_br", 4), ("lru_bi", 4), ("lam", 4), ("q_norm", 3),
                       ("kv_norm", 2), ("dw_w", 4 * CONV_TAPS), ("dw_b", 4), ("ln_g", 4), ("ln_b", 4), ("b_pw", 8)])
CONST, NCONST = columns([("ones", P), ("ident", P), ("causal", 384), ("freq1", 1), ("phase1", 1), ("eps", 1), ("tiny", 1), ("final", 8),
                         ("freq_c", 1), ("freq_s", 1), ("phase_c", 1), ("phase_s", 1)])


def first_steps():
    s = [("pa", i) for i in range(4)] + [("pb", 0), ("pb", 1)]
    s += [("lr", 0), ("lr", 1), ("li", 0), ("li", 1)]
    s += [("pb", 2), ("pc", 0), ("pc", 1), ("stat_lat", 0), ("pc", 2), ("pc", 3)]
    s += [("uq", i) for i in range(4)] + [("uk", 0), ("uk", 1), ("uv", 0), ("uv", 1)]
    s += [("S", 0), ("S", 1)]
    for u in range(8):
        s.append(("A", u))
        if u and u % 2 == 0:
            s.append(("V", u // 2 - 1))
        s.append(("T", u))
        if u + 2 < QKV_HEADS:
            s.append(("S", u + 2))
    s.append(("V", 3))
    for u in range(8):
        s.append(("B", u))
        if u == MU_AFTER:
            s.append(("stat_mu", 0))
        if u == LN_AFTER:
            s.append(("stat_ln", 0))
    return s + [("C", t) for t in range(8)] + [("O", i) for i in range(5)]


MU_AFTER, LN_AFTER = 4, 6
STEPS1 = first_steps()
EVAC1 = list(STEPS1)
EVAC1.remove(("stat_lat", 0))
EVAC1.insert(EVAC1.index(("pc", 0)), ("stat_lat", 0))
FREER = dict(pb="a", pc="v", pa="a", stat_lat="a", uq="v", uk="a", uv="a", lr="a", li="a", S="v", T="a", V="v",
             A="v", C="a", B="v", O="v", stat_mu="v", stat_ln="a", stat="a", up="v", down="v")
FIXED_BANK = dict(stat_lat=7, stat_mu=7, stat_ln=7, stat=7, T=6, V=7)


class Groups:

    def __init__(self, steps, freer=FREER, fixed=FIXED_BANK):
        self.mark, self.bank, self.freer = {}, {}, {}
        marks = 0
        self.freed_until, main, last, self.before = {"a": 0, "v": 0}, 0, {}, {}
        for kind, i in steps:
            g = (kind, i)
            if kind.startswith("up"):
                main, bank = i % 4, i % 4
            elif kind.startswith("down"):
                bank = 2 + i % 2
                main = 3
            elif kind == "S":
                bank = 4 + i % 2
            elif kind in fixed:
                bank = fixed[kind]
            else:
                main = (main + 1) % 4
                bank = main
            who = freer[kind if kind in freer else kind[:-1]]
            marks += 2 if kind.startswith("down") else 1
            self.mark[g], self.bank[g] = marks, bank
            self.before[g] = last.get(bank)
            if who is None:
                continue
            self.freed_until[who] += 1
            self.freer[g] = (who, self.freed_until[who])
            last[bank] = g
        self.marks, self.last = marks, last


class Signal:

    def __init__(self, sem, per, ahead=0):
        self.sem, self.per, self.ahead = sem, per, ahead

    def __call__(self, layer, n):
        return self.sem, layer * self.per + (self.ahead * self.per + n)


def layer_steps1():
    ffn = lambda w: [(f"up{w}", j) for j in range(FT)] + [(f"down{w}", t) for t in range(KT)]
    return [("stat", 0)] + ffn(0) + [("stat", 1)] + STEPS1 + [("stat", 2)] + ffn(1)


def used_marks1(mark):
    out = [mark["up0", j] for j in range(FT)]
    out += [mark["down0", t] - 1 + half for t in range(KT) for half in range(2)]
    last = {("lr", 0): ("li", 1), ("uq", 0): ("uq", 1), ("uq", 2): ("uq", 3), ("uk", 0): ("uv", 1)}
    out += [mark[last.get(u, u)] for u in UNIT_ORDER1]
    out += [mark["up1", j] for j in range(FT)]
    out += [mark["down1", t] - 1 + half for t in range(KT) for half in range(2)]
    assert len(out) == len(UNITS1)
    return out


FOX_HEADS, NSA_HEADS, DIL_HEADS, HD = 4, 8, 4, 64
GROUPS = 2
ATTN_SCALE = HD ** -0.5
CMP_BLOCK, CMP_STRIDE = 32, 16
N_CMP = (T - CMP_BLOCK) // CMP_STRIDE + 1
SLOT = 16
DIL_PATTERNS = ((128, 1), (512, 4), (2048, 16))
ROPE2_HALF = 8
assert T // 64 <= 16 and T <= 512
VB_COLS = 288
KC, VC, NQ, KS, KW, FQ, FK, DQ, DK, FGATE = 0, 1, 2, 6, 7, 8, 10, 12, 14, 16
F_TILES = [(2 * i, 2 * i + 1) for i in range(8)] + [(16,)]
ROTATED = {0: (KC,), 1: (2, 3), 2: (4, 5), 3: (KS, KW), 6: (12, 13), 7: (14, 15)}
MIX2_ORDER = [("f", 0), ("R", 0), ("f", 1), ("R", 1), ("f", 2), ("R", 2), ("f", 3), ("R", 3), ("f", 8), ("va", 0),
              ("va", 1), ("vb", 0), ("vb", 1), ("cmp", 0), ("cmp", 1), ("cmp", 2), ("cmp", 3), ("c2", 0), ("SC", 0)]
MIX2_FILL = [("f", 4), ("f", 5), ("cum", 0), ("cum", 1), ("f", 6), ("R", 6), ("f", 7), ("R", 7)]
HEADS2 = [(kind, i, e) for i in range(4) for e in range(2) for kind in ("sel", "win")] \
    + [(kind, i, e) for kind in ("fox", "dil") for i in range(2) for e in range(2)]
LAST_OF_TILE = {n for n in range(16) if n % 4 == 3} | {n for n in range(16, 24) if n % 2}
O2_TILE = dict(fox=0, sel=2, win=2, dil=6)


def second_steps():
    s, fill = list(MIX2_ORDER), list(MIX2_FILL)
    values = lambda n: ("W" if n in LAST_OF_TILE else "V", n)
    for n in range(len(HEADS2) + 2):
        if n < len(HEADS2):
            s.append(("S", n))
        if n == 1:
            s.append(("TC", 0))
        if 0 <= n - 1 < len(HEADS2):
            s.append(("T", n - 1))
        if n - 2 >= 0:
            s.append(values(n - 2))
        if fill:
            s.append(fill.pop(0))
    return s + [("O", i) for i in range(5)]


STEPS2 = second_steps()
FREER2 = dict(f="a", R="v", va="a", vb="a", cmp="a", c2="a", SC="v", TC="a", cum="v", S="v", T="a", V=None, W="v",
              O="a", stat="a", up="v", down="a")
FIXED_BANK2 = dict(stat=7, T=6, V=7, W=7)
O2_UNITS = [(0, 1), (2, 3), (4, 5), (6,), (7,)]

UNIT_ORDER2 = [("f", 0), ("f", 1), ("f", 2), ("f", 3), ("f", 8), ("va", 0), ("va", 1), ("vb", 0), ("vb", 1), ("cmp", 0),
               ("cmp", 1), ("cmp", 2), ("cmp", 3), ("f", 4), ("f", 5), ("f", 6), ("f", 7)] + [("O", i) for i in range(5)]
UNIT_BLOCKS2 = dict(f=16, va=16, vb=4 * VB_COLS // P, cmp=16, O=16)
UNITS2 = [8 if u in (("f", 8), ("O", 3), ("O", 4)) else UNIT_BLOCKS2[u[0]] for u in UNIT_ORDER2] + FFN_UNITS
FFN2_AT = len(UNIT_ORDER2)
UNIT_OF2 = {u: n for n, u in enumerate(UNIT_ORDER2)}
assert len(UNITS2) % SPLIT_SLOTS == 0


def layer_steps2():
    return ([("stat", 0)] + STEPS2 + [("stat", 1), ("stat", 2)] + [("up0", j) for j in range(FT)]
            + [("down0", t) for t in range(KT)] + [("stat", 3)])


def used_marks2(mark):
    both = {("va", 0): ("va", 1), ("vb", 0): ("vb", 1)}
    out = [mark[both.get(u, u)] for u in UNIT_ORDER2]
    out += [mark["up0", j] for j in range(FT)]
    return out + [mark["down0", t] - 1 + half for t in range(KT) for half in range(2)]


VEC2, NVEC2 = columns([("norm0", 8), ("norm1", 8), ("norm2", 8), ("norm3", 8), ("b_forget", 1), ("b_nsa", 24),
                       ("pos_k", 16), ("pos_v", 16), ("w2k", 128), ("w2v", 128), ("conv_w", 3 * 2 * FT), ("conv_b", 2 * FT)])
CONST2, NCONST2 = columns([("perm", P), ("dil", 384), ("pick", FOX_HEADS * P), ("cmp_bias", 2 * SLOT), ("cmp_keep", 2 * SLOT),
                           ("own", NSA_HEADS)])
NVEC = max(NVEC1, NVEC2)


def build(nc, io):
    with ExitStack() as ctx:
        def sbuf(name, shape, dt=F32, stack=ctx):
            return stack.enter_context(nc.sbuf_tensor(name, shape, dt))

        raw = sbuf("raw", [P, RAW_SLOTS, 16 * P])
        w_hi = sbuf("w_hi", [P, SPLIT_SLOTS, 16 * P], F32R)
        w_lo = sbuf("w_lo", [P, SPLIT_SLOTS, 16 * P], F32R)
        x = sbuf("x", [P, KT, T])
        h_hi = sbuf("h_hi", [P, KT, T], F32R)
        h_lo = sbuf("h_lo", [P, KT, T], F32R)
        const = sbuf("const", [P, NCONST])
        vec = sbuf("vec", [P, NVEC])
        scr = sbuf("scr", [P, KT, T])
        sq = sbuf("sq", [P, 2, T])
        acc = sbuf("acc", [P, T])
        std = sbuf("std", [P, T])
        trig1 = sbuf("trig1", [P, T])
        cos2 = sbuf("cos2", [P, T])
        sin2 = sbuf("sin2", [P, T])
        ones = const[:, CONST["ones"]:CONST["ones"] + P]
        ident = const[:, CONST["ident"]:CONST["ident"] + P]
        causal = const[:, CONST["causal"]:CONST["causal"] + 384]

        eps_col = const[:, CONST["eps"]:CONST["eps"] + 1]
        tiny_col = const[:, CONST["tiny"]:CONST["tiny"] + 1]

        with ExitStack() as phase:
            hid_hi = sbuf("hid_hi", [P, FT, T], F32R, phase)
            hid_lo = sbuf("hid_lo", [P, FT, T], F32R, phase)
            silu = sbuf("silu", [P, 2, T], F32, phase)
            hid = sbuf("hid", [P, 2, T], F32, phase)
            conv2 = sbuf("conv2", [P, 2, T], F32, phase)
        with ExitStack() as phase:
            with ExitStack() as early:
                q1 = sbuf("q1", [P, QKV_HEADS, T], F32, early)
                k1 = sbuf("k1", [P, QKV_HEADS, T], F32, early)
            m_hi = sbuf("m_hi", [P, KT, T], F32R, phase)
            m_lo = sbuf("m_lo", [P, KT, T], F32R, phase)
            v1 = sbuf("v1", [P, 2, QKV_HEADS * VD], F32, phase)
            glu = sbuf("glu", [P, 4, T + CONV_TAPS - 1], F32, phase)
            conv = sbuf("conv", [P, 4, T], F32, phase)
            derived = sbuf("derived", [P, 64], F32, phase)
            probs1 = sbuf("probs1", [P, 2, 384], F32, phase)
            probs_t1 = sbuf("probs_t1", [P, 2, 384], F32, phase)
            row1 = sbuf("row1", [P, 16], F32, phase)
            with ExitStack() as early:
                lat = sbuf("lat", [P, 5, T], F32, early)
                lat_hi = sbuf("lat_hi", [P, 5, T], F32R, early)
                lat_lo = sbuf("lat_lo", [P, 5, T], F32R, early)
            cv_hi = sbuf("cv_hi", [P, 4, T], F32R, phase)
            cv_lo = sbuf("cv_lo", [P, 4, T], F32R, phase)
            o1_hi = sbuf("o1_hi", [P, 4, T], F32R, phase)
            o1_lo = sbuf("o1_lo", [P, 4, T], F32R, phase)
            pad_r = sbuf("pad_r", [P, 4, T + LRU_TAPS - 1], F32, phase)
            gelu = sbuf("gelu", [P, 4, T], F32, phase)
            xa = sbuf("xa", [P, 4, T], F32, phase)
            a_t = sbuf("a_t", [P, 4, T], F32, phase)
            i_g = sbuf("i_g", [P, 4, T], F32, phase)
            with ExitStack() as early:
                xa_hi = sbuf("xa_hi", [P, 4, T], F32R, early)
                xa_lo = sbuf("xa_lo", [P, 4, T], F32R, early)
                r_g = sbuf("r_g", [P, 4, T], F32, early)
            ya_hi = sbuf("ya_hi", [P, 4, T], F32R, phase)
            ya_lo = sbuf("ya_lo", [P, 4, T], F32R, phase)
            gate = sbuf("gate", [P, 2, T], F32, phase)
            y_b = sbuf("y_b", [P, 2, T], F32, phase)

        rope_t = a_t[:].rearrange("p (e f) t -> p e (f t)", e=2)
        key_pe = q1[:, 5]
        lat_acc = q1[:, 6:8].rearrange("p a t -> p (a t)")
        ratio = pad_r[:, :, LRU_TAPS - 1:]
        with ExitStack() as phase:
            sbuf("spacer", [P, 52 * 256], F32, phase)
            const2 = sbuf("const2", [P, NCONST2], F32, phase)
            v2a = sbuf("v2a", [P, 2, 512], F32, phase)
            v2b = sbuf("v2b", [P, 2, VB_COLS], F32, phase)
            gates2 = sbuf("gates2", [P, 2, 24], F32, phase)
            h1 = sbuf("h1", [P, 4, 2 * SLOT], F32, phase)
            h_rep = sbuf("h_rep", [P, 2, 4, 2 * SLOT], F32, phase)
            k_cmp = sbuf("k_cmp", [P, 2 * SLOT], F32, phase)
            v_cmp = sbuf("v_cmp", [P, HD], F32, phase)
            v_own = sbuf("v_own", [P, NSA_HEADS, HD], F32, phase)
            p_cmp = sbuf("p_cmp", [P, 2 * NSA_HEADS, SLOT], F32, phase)
            p_cmp_t = sbuf("p_cmp_t", [P, T], F32, phase)
            row_cmp = sbuf("row_cmp", [P, 2, 2 * NSA_HEADS], F32, phase)
            fox_bias = sbuf("fox_bias", [P, FOX_HEADS, 384], F32, phase)
            probs2 = sbuf("probs2", [P, 2, 384], F32, phase)
            probs_t2 = sbuf("probs_t2", [P, 2, 384], F32, phase)
            row2 = sbuf("row2", [P, 16], F32, phase)
        with ExitStack() as phase:
            feat = sbuf("feat", [P, 17, T], F32, phase)
            win = sbuf("win", [P, 2, 512], F32, phase)
            win_hi = sbuf("win_hi", [P, 2, 512], F32R, phase)
            win_lo = sbuf("win_lo", [P, 2, 512], F32R, phase)
            o2_hi = sbuf("o2_hi", [P, 8, T], F32R, phase)
            o2_lo = sbuf("o2_lo", [P, 8, T], F32R, phase)
            decay = sbuf("decay", [FOX_HEADS, 5, T], F32, phase)

        merged = scr
        banks = [ctx.enter_context(nc.psum_tensor(f"bank{b}", [P, 512], F32)) for b in range(8)]

        def col(name, n=0, at=VEC1, rows=slice(0, P)):
            return vec[rows, at[name] + n:at[name] + n + 1]

        def signal(name, per=0, ahead=0):
            return Signal(ctx.enter_context(nc.semaphore(name)), per, ahead)

        class Stream:

            def __init__(self, tag, units, used):
                self.units, self.used = units, used
                self.raw_full = [signal(f"raw_full{s}_{tag}", 16 * len(units) // RAW_SLOTS) for s in range(RAW_SLOTS)]
                self.hi_ready = signal(f"hi_ready_{tag}", len(units))
                self.lo_ready = signal(f"lo_ready_{tag}", len(units), ahead=1)

        class Work:

            def __init__(self, tag, steps, *rules):
                self.g = Groups(steps, *rules)
                self.done_sem = signal(f"group_done_{tag}", self.g.marks, ahead=1)
                self.freed = {"v": signal(f"freed_by_vector_{tag}", self.g.freed_until["v"], ahead=1),
                              "a": signal(f"freed_by_scalar_{tag}", self.g.freed_until["a"], ahead=1)}

            def out(self, group):
                return banks[self.g.bank[group]]

            def done(self, layer, group, more=0):
                return self.done_sem(layer, self.g.mark[group] + more)

            def bank_free(self, layer, group):
                before = self.g.before[group]
                wrapped = before is None
                before = before or self.g.last[self.g.bank[group]]
                who, n = self.g.freer[before]
                s = self.freed[who]
                return s(layer, n - s.per) if wrapped else s(layer, n)

            def wait_banks_free(self, pe, layer, groups, taken=()):
                latest = {}
                for group in taken:
                    who, n = self.g.freer[group]
                    latest[who] = max(latest.get(who, n), n)
                for group in groups:
                    before = self.g.before[group]
                    wrapped = before is None
                    who, n = self.g.freer[before or self.g.last[self.g.bank[group]]]
                    latest[who] = max(latest.get(who, -10 ** 9), n - (self.freed[who].per if wrapped else 0))
                for who, n in latest.items():
                    pe.wait_ge(*self.freed[who](layer, n))

            def freed_sem(self, group):
                return self.freed[self.g.freer[group][0]].sem

            def taken(self, layer, group, more=0):
                who, n = self.g.freer[group]
                return self.freed[who](layer, n + more)

        work1 = Work("1", layer_steps1())
        first = Stream("1", UNITS1, used_marks1(work1.g.mark))
        consts_in = signal("consts_in")
        x_in = signal("x_in")
        credited = signal("credited")
        out_done = signal("out_done")
        turned = signal("turned")
        trig_ready = signal("trig_ready")

        class Norms:

            def __init__(self, tag, norms, made):
                self.sq_ready = signal(f"sq_ready_{tag}", norms * KT)
                self.sq_summed = signal(f"sq_summed_{tag}", norms * KT, ahead=1)
                self.std_ready = signal(f"std_ready_{tag}", norms)
                self.normed = signal(f"normed_{tag}", made * KT)
                self.h_hi_ready = signal(f"h_hi_ready_{tag}", made * KT)
                self.h_ready = signal(f"h_ready_{tag}", made * KT)

        n1 = Norms("1", 3, 3)
        silu_ready = signal("silu_ready", 2 * FT)
        hid_hi_ready = signal("hid_hi_ready", 2 * FT)
        hid_ready = signal("hid_ready", 2 * FT)
        vec_full = signal("vec_full", 16)
        vec_free = signal("vec_free", 2, ahead=1)
        lam_ready = signal("lam_ready", 1)
        lam_exp = signal("lam_exp", 1)
        rate_ready = signal("rate_ready", 1)
        lat_std = signal("lat_std", 1)
        lat_normed = signal("lat_normed", 1)
        lat_hi_ready = signal("lat_hi_ready", 1)
        lat_split = signal("lat_split", 1)
        key_terms = signal("key_terms", 1)
        key_rope_ready = signal("key_rope_ready", 1)
        q_nope_ready = signal("q_nope_ready", 4)
        q_ready = signal("q_ready", 4)
        sig_ready = signal("sig_ready", 4)
        xa_ready = signal("xa_ready", 1)
        xa_hi_ready = signal("xa_hi_ready", 1)
        xa_split = signal("xa_split", 1)
        decay_ready = signal("decay_ready", 1)
        ratio_ready = signal("ratio_ready", 1)
        root_ready = signal("root_ready", 1)
        ya_made = signal("ya_made", 1)
        ya_hi_ready = signal("ya_hi_ready", 1)
        ya_split = signal("ya_split", 1)
        conv_ready = signal("conv_ready", 1)
        centred = signal("centred", 1)
        centred_sq = signal("centred_sq", 1)
        ln_std = signal("ln_std", 1)
        ln_made = signal("ln_made", 1)
        cv_hi_ready = signal("cv_hi_ready", 1)
        cv_split = signal("cv_split", 1)
        gate_ready = signal("gate_ready", 16)
        merge_step = signal("merge_step", 24)
        x_mixed = signal("x_mixed", KT)
        m_hi_ready = signal("m_hi_ready", KT)
        m_split = signal("m_split", KT)
        max_ready = signal("max_ready", QKV_HEADS)
        exp_ready = signal("exp_ready", QKV_HEADS)
        sums_ready = signal("sums_ready", QKV_HEADS)
        probs_ready = signal("probs_ready", QKV_HEADS)
        o_hi_ready = signal("o_hi_ready", 4)
        work2 = Work("2", layer_steps2(), FREER2, FIXED_BANK2)
        second = Stream("2", UNITS2, used_marks2(work2.g.mark))
        n2 = Norms("2", 4, 2)
        consts2_in = signal("consts2_in")
        trig2_ready = signal("trig2_ready")
        vec2_full = signal("vec2_full", 16)
        vec2_free = signal("vec2_free", 2, ahead=1)
        x_new = signal("x_new", 2 * KT)
        rotated = signal("rotated", 6)
        win_cleared = signal("win_cleared", 1)
        win_copied = signal("win_copied", 1)
        win_made = signal("win_made", 1)
        win_hi_ready = signal("win_hi_ready", 1)
        win_split = signal("win_split", 1)
        gate_sums = signal("gate_sums", 1)
        gates_ready = signal("gates_ready", 1)
        rep_ready = signal("rep_ready", 1)
        own_ready = signal("own_ready", 1)
        cmp_shifted = signal("cmp_shifted", 1)
        cmp_exp = signal("cmp_exp", 1)
        cmp_ready = signal("cmp_ready", 1)
        forget_abs = signal("forget_abs", 1)
        forget_exp = signal("forget_exp", 1)
        decay_summed = signal("decay_summed", 1)
        max2_ready = signal("max2_ready", len(HEADS2))
        exp2_ready = signal("exp2_ready", len(HEADS2))
        sums2_ready = signal("sums2_ready", len(HEADS2))
        probs2_ready = signal("probs2_ready", len(HEADS2))
        o2_hi_ready = signal("o2_hi_ready", 8)
        last_tap_ready = signal("last_tap_ready", FT)
        hid2_made = signal("hid2_made", FT)
        silu2_ready = signal("silu2_ready", FT)
        hid2_hi_ready = signal("hid2_hi_ready", FT)
        hid2_ready = signal("hid2_ready", FT)

        def load_unit(sp, st, l, s, src, more=0):
            n = st.units[s] * P
            sp.wait_ge(*st.lo_ready(l, more + (s - RAW_SLOTS + 1)))
            sp.dma_start(raw[:, s % RAW_SLOTS, 0:n], src).then_inc(st.raw_full[s % RAW_SLOTS].sem, 16)

        def split_hi(act, st, work, l, s, more=0, half=0, floor=0):
            n, before = st.units[s] * P, s - SPLIT_SLOTS
            act.wait_ge(*st.raw_full[s % RAW_SLOTS](l, half * 16 + 16 * (s // RAW_SLOTS + 1)))
            if before >= 0 or floor:
                act.wait_ge(*work.done_sem(l, more + max(st.used[before] if before >= 0 else 0, floor)))
            else:
                act.wait_ge(*work.done_sem(l, st.used[before] - work.g.marks))
            act.activation(w_hi[:, s % SPLIT_SLOTS, 0:n], raw[:, s % RAW_SLOTS, 0:n], ACT.Copy).then_inc(st.hi_ready.sem, 1)

        def split_lo(dve, st, l, s, more=0):
            n = st.units[s] * P
            dve.wait_ge(*st.hi_ready(l, more + (s + 1)))
            dve.tensor_tensor(w_lo[:, s % SPLIT_SLOTS, 0:n], raw[:, s % RAW_SLOTS, 0:n],
                              w_hi[:, s % SPLIT_SLOTS, 0:n].bitcast(F32), ALU.subtract).then_inc(st.lo_ready.sem, 1)

        class Splitter:

            def __init__(self, one, units):
                self.one, self.next, self.units = one, 0, units

            def until(self, s):
                while self.next <= min(s, self.units - 1):
                    self.one(self.next)
                    self.next += 1

        def product(pe, out, s, block, x_hi, x_lo, start, stop, rows=P):
            hi = w_hi[:, s % SPLIT_SLOTS, block * P:block * P + rows]
            lo = w_lo[:, s % SPLIT_SLOTS, block * P:block * P + rows]
            pe.matmul(out, hi, x_hi, start=start, stop=False)
            pe.matmul(out, hi, x_lo, start=False, stop=False)
            return pe.matmul(out, lo, x_hi, start=False, stop=stop)

        def first_products(pe, nm, l, m, outs):
            for k in range(KT):
                pe.wait_ge(*nm.h_hi_ready(l, KT * m + k + 1))
                for out, s, block in outs:
                    at = slice((block + k) * P, (block + k + 1) * P)
                    pe.matmul(out, w_hi[:, s % SPLIT_SLOTS, at], h_hi[:, k], start=k == 0, stop=False)
                    pe.matmul(out, w_lo[:, s % SPLIT_SLOTS, at], h_hi[:, k], start=False, stop=False)
            for k in range(KT):
                pe.wait_ge(*nm.h_ready(l, KT * m + k + 1))
                for out, s, block in outs:
                    at = slice((block + k) * P, (block + k + 1) * P)
                    pe.matmul(out, w_hi[:, s % SPLIT_SLOTS, at], h_lo[:, k], start=False, stop=k == KT - 1)

        def tokens_product(pe, out, s, at, width, x_hi, x_lo, start, stop):
            hi = w_hi[:, s % SPLIT_SLOTS, at:at + width]
            lo = w_lo[:, s % SPLIT_SLOTS, at:at + width]
            pe.matmul(out, x_hi, hi, start=start, stop=False)
            pe.matmul(out, x_lo, hi, start=False, stop=False)
            return pe.matmul(out, x_hi, lo, start=False, stop=stop)

        def norm_pe(pe, work, nm, l, n):
            pe.wait_ge(*nm.sq_summed(l, KT * n + KT))
            pe.wait_ge(*work.bank_free(l, ("stat", n)))
            out = work.out(("stat", n))[:, 0:T]
            pe.matmul(out, ones, acc[:], start=True, stop=False)
            pe.wait_ge(*nm.sq_ready(l, KT * n + KT))
            pe.matmul(out, ones, sq[:, (KT - 1) % 2], start=False, stop=True).then_inc(work.done_sem.sem, 1)

        def norm_pe_direct(pe, work, nm, l, n):
            pe.wait_ge(*work.bank_free(l, ("stat", n)))
            for t in range(KT):
                pe.wait_ge(*nm.sq_ready(l, KT * n + t + 1))
                last = pe.matmul(work.out(("stat", n))[:, 0:T], ones, sq[:, t % 2], start=t == 0, stop=t == KT - 1)
                if t < KT - 1:
                    last.then_inc(nm.sq_summed.sem, 2 if t == KT - 2 else 1)
            last.then_inc(work.done_sem.sem, 1)

        def norm_act_root(act, work, nm, l, n):
            act.preload_act_table_set(LOG_EXP)
            act.wait_ge(*work.done(l, ("stat", n)))
            act.activation(std[:], work.out(("stat", n))[:, 0:T], ACT.Ln, scale=1.0 / D, bias=eps_col)
            act.drain().then_inc(work.freed_sem(("stat", n)), 1)
            act.activation(std[:], std[:], ACT.Exp, scale=-0.5).then_inc(nm.std_ready.sem, 1)

        def norm_act_split(act, nm, l, m):
            for t in range(KT):
                act.wait_ge(*nm.normed(l, KT * m + t + 1))
                act.activation(h_hi[:, t], scr[:, t], ACT.Copy).then_inc(nm.h_hi_ready.sem, 1)

        def norm_dve(dve, nm, l, n, m, gains):
            dve.wait_ge(*nm.std_ready(l, n + 1))
            for t in range(KT):
                dve.scalar_tensor_tensor(scr[:, t], x[:, t], gains(t), std[:], ALU.mult, ALU.mult).then_inc(nm.normed.sem, 1)
            for t in range(KT):
                dve.wait_ge(*nm.h_hi_ready(l, KT * m + t + 1))
                dve.tensor_tensor(h_lo[:, t], scr[:, t], h_hi[:, t].bitcast(F32), ALU.subtract).then_inc(nm.h_ready.sem, 1)

        def square(act, nm, l, k, src, parity):
            act.wait_ge(*nm.sq_summed(l, k - 2))
            act.activation(sq[:, parity], src, ACT.Square).then_inc(nm.sq_ready.sem, 1)

        def sum_squares(pool, nm, l, first_k):
            pool.drain()
            pool.wait_ge(*nm.sq_ready(l, first_k + 1))
            pool.tensor_tensor(acc[:], sq[:, 0], sq[:, 1], ALU.add).then_inc(nm.sq_summed.sem, 2)
            for t in range(2, KT - 1):
                pool.drain()
                pool.wait_ge(*nm.sq_ready(l, first_k + t))
                pool.tensor_tensor(acc[:], acc[:], sq[:, t % 2], ALU.add).then_inc(nm.sq_summed.sem, 2 if t == KT - 2 else 1)

        def ffn_pe(pe, st, work, nm, l, w, at, m, hidden):
            up, down = f"up{w}", f"down{w}"

            def up_unit(j, more, halves=(0, 1)):
                s = at + j
                pe.wait_ge(*st.lo_ready(l, more + (s + 1)))
                out = banks[j % 4]
                for half in halves:
                    for k in range(KT):
                        last = product(pe, out[:, half * T:half * T + T], s, half * KT + k, h_hi[:, k], h_lo[:, k],
                                       k == 0, k == KT - 1)
                last.then_inc(work.done_sem.sem, 1)

            work.wait_banks_free(pe, l, [(up, j) for j in range(4)])
            ready = 2 if at else 1
            pe.wait_ge(*st.lo_ready(l, at + ready))
            first_products(pe, nm, l, m, [(banks[j][:, 0:T], at + j, 0) for j in range(ready)])
            for j in range(2):
                up_unit(j, 0, halves=range(j < ready, 2))
            with pe.Fori(0, 5) as it:
                for u in range(4):
                    pe.wait_ge(*work.taken(l, (up, 0), it * 4 + (2 + u - 4)))
                    up_unit(2 + u, it * 4)
            with pe.Fori(0, KT // 2) as it:
                for g in range(2):
                    if work.g.freer[down, 0][0] != "v":
                        pe.wait_ge(*work.taken(l, (up, FT - 1)))
                    pe.wait_ge(*work.taken(l, (down, 0), it * 2 + (g - 2)))
                    for half in range(2):
                        s = at + FT + 2 * g + half
                        pe.wait_ge(*st.lo_ready(l, it * 4 + (s + 1)))
                        pe.wait_ge(*hidden(l, w * FT + (half + 1) * HALF - 3 * half))
                        for b in range(HALF):
                            k = half * HALF + b
                            if k >= FT - 3:
                                pe.wait_ge(*hidden(l, w * FT + k + 1))
                            last = product(pe, banks[2 + g][:, 0:T], s, b, hid_hi[:, k], hid_lo[:, k],
                                           k == 0, k == FT - 1)
                        last.then_inc(work.done_sem.sem, 1)

        def ffn_act(act, l, w, at, n, split):
            up, down, st, work = f"up{w}", f"down{w}", first, work1

            def gated(j, more, parity, split_next):
                bank = banks[j % 4]
                act.wait_ge(*work.done(l, (up, 0), more + j))
                act.activation(silu[:, parity], bank[:, 0:T], ACT.Silu).then_inc(silu_ready.sem, 1)
                split_next()
                act.wait_ge(*work.taken(l, (up, 0), more + j))
                act.activation(hid_hi[:, more + j], hid[:, parity], ACT.Copy).then_inc(hid_hi_ready.sem, 1)

            floor = work.g.mark[up, 0] - 1
            with act.Fori(0, 4) as it:
                for u in range(4):
                    gated(u, it * 4, u % 2, lambda: split_hi(act, st, work, l, at + u + AHEAD, it * 4, it * 2, floor))
            split.next = at + 16 + AHEAD
            for j in range(16, FT):
                gated(j, 0, j % 2, lambda: split.until(at + j + AHEAD))
            base = at + FT + AHEAD

            def residual(t, more):
                act.wait_ge(*work.taken(l, (down, 0), more + t))
                square(act, n1, l, more + (KT * (n + 1) + t + 1), x[:, more + t], t % 2)

            with act.Fori(0, 3) as it:
                for g in range(2):
                    for e in range(2):
                        split_hi(act, st, work, l, base + 2 * g + e, it * 4, it * 2)
                    residual(g, it * 2)
            split.next = base + 12
            split.until(base + 2 * 6 + 1)
            residual(6, 0)
            split.until(base + 2 * 7)
            residual(7, 0)

        def ffn_dve(dve, l, w, at, n, split):
            up, down, st, work = f"up{w}", f"down{w}", first, work1

            def gated(j, more, parity, split_next):
                bank = banks[j % 4]
                dve.wait_ge(*silu_ready(l, more + (w * FT + j + 1)))
                dve.tensor_tensor(hid[:, parity], silu[:, parity], bank[:, T:2 * T], ALU.mult).then_inc(work.freed["v"].sem, 1)
                split_next()
                dve.wait_ge(*hid_hi_ready(l, more + (w * FT + j + 1)))
                dve.tensor_tensor(hid_lo[:, more + j], hid[:, parity], hid_hi[:, more + j].bitcast(F32),
                                  ALU.subtract).then_inc(hid_ready.sem, 1)

            with dve.Fori(0, 4) as it:
                for u in range(4):
                    gated(u, it * 4, u % 2, lambda: split_lo(dve, st, l, at + u + AHEAD, it * 4))
            split.next = at + 16 + AHEAD
            for j in range(16, FT):
                gated(j, 0, j % 2, lambda: split.until(at + j + AHEAD))
            base = at + FT + AHEAD

            def residual(t, more):
                dve.wait_ge(*work.done(l, (down, 0), more * 2 + 2 * t))
                dve.scalar_tensor_tensor(x[:, more + t], banks[2 + t % 2][:, 0:T], 0.5, x[:, more + t], ALU.mult,
                                         ALU.add).then_inc(work.freed["v"].sem, 1)

            with dve.Fori(0, 3) as it:
                for g in range(2):
                    for e in range(2):
                        split_lo(dve, st, l, base + 2 * g + e, it * 4)
                    residual(g, it * 2)
            split.next = base + 12
            split.until(base + 2 * 6 + 1)
            residual(6, 0)
            split.until(base + 2 * 7)
            residual(7, 0)

        def load_loop(sp, st, l, src, at, count, size):
            with sp.Fori(0, count // 2) as it:
                for u in range(2):
                    load_unit(sp, st, l, at + u, src[it * 2 + u], it * 2)

        def scores_pe(pe, work, l, g, q, k):
            pe.wait_ge(*work.bank_free(l, g))
            out = work.out(g)
            pe.matmul(out[:, 0:P], q[:, 0:P], k[:, 0:P], start=True, stop=True)
            pe.matmul(out[:, P:3 * P], q[:, P:2 * P], k[:, 0:2 * P], start=True, stop=True).then_inc(work.done_sem.sem, 1)

        def transpose_pe(pe, work, l, g, ready, probs, parity):
            pe.wait_ge(*ready)
            pe.wait_ge(*work.bank_free(l, g))
            for b in range(3):
                last = pe.transpose(work.out(g)[:, b * P:(b + 1) * P], probs[:, parity, b * P:(b + 1) * P], ident)
            last.then_inc(work.done_sem.sem, 1)

        def values_pe(pe, out, v, probs_t, parity, start=True):
            pe.matmul(out, v[0], probs_t[:, parity, 0:T], start=start, stop=False, skip_group_check=not start)
            return pe.matmul(out[:, P:T], v[1], probs_t[:, parity, T:T + P], start=False, stop=True,
                             skip_group_check=not start)

        def softmax_dve_max(dve, work, l, g, scale, bias, probs, row, parity, signal_):
            dve.wait_ge(*work.done(l, g))
            dve.scalar_tensor_tensor(probs[:, parity, :], work.out(g)[:, 0:384], scale, bias, ALU.mult,
                                     ALU.add).then_inc(work.freed_sem(g), 1)
            dve.drain()
            dve.tensor_reduce(row[:, 8 * parity:8 * parity + 1], probs[:, parity, 0:P], AX.X, ALU.max, negate=True)
            dve.tensor_reduce(row[:, 8 * parity + 1:8 * parity + 2], probs[:, parity, P:384], AX.X, ALU.max,
                              negate=True).then_inc(signal_.sem, 1)

        def softmax_act_exp(act, probs, row, parity, ready, signal_):
            act.wait_ge(*ready)
            act.activation(probs[:, parity, 0:P], probs[:, parity, 0:P], ACT.Exp, bias=row[:, 8 * parity:8 * parity + 1],
                           accum_out=row[:, 8 * parity + 2:8 * parity + 3])
            act.activation(probs[:, parity, P:384], probs[:, parity, P:384], ACT.Exp,
                           bias=row[:, 8 * parity + 1:8 * parity + 2],
                           accum_out=row[:, 8 * parity + 3:8 * parity + 4]).then_inc(signal_.sem, 1)

        def softmax_dve_sums(dve, row, parity, ready, signal_, gates=None):
            dve.wait_ge(*ready)
            inv = row[:, 8 * parity + 4:8 * parity + 6]
            last = dve.reciprocal(inv, row[:, 8 * parity + 2:8 * parity + 4])
            if gates is not None:
                dve.drain()
                last = dve.tensor_tensor(inv, inv, gates, ALU.mult)
            last.then_inc(signal_.sem, 1)

        def softmax_act_norm(act, probs, row, parity, ready, signal_):
            act.wait_ge(*ready)
            act.activation(probs[:, parity, 0:P], probs[:, parity, 0:P], ACT.Identity,
                           scale=row[:, 8 * parity + 4:8 * parity + 5])
            act.activation(probs[:, parity, P:384], probs[:, parity, P:384], ACT.Identity,
                           scale=row[:, 8 * parity + 5:8 * parity + 6]).then_inc(signal_.sem, 1)

        UNIT_OF = {u: MIX1_AT + n for n, u in enumerate(UNIT_ORDER1)}
        for u, same in ((("lr", 1), ("lr", 0)), (("li", 0), ("lr", 0)), (("li", 1), ("lr", 0)), (("uq", 1), ("uq", 0)),
                        (("uq", 3), ("uq", 2)), (("uk", 1), ("uk", 0)), (("uv", 0), ("uk", 0)), (("uv", 1), ("uk", 0))):
            UNIT_OF[u] = UNIT_OF[same]
        BRANCH_VEC = dict(A=0, C=16, B=8)
        FIRST1 = STEPS1[0]
        O_TILES = [(0, 1), (2, 3), (4, 5), (6,), (7,)]

        def mixer1_pe(pe, l):
            st, work = first, work1
            for kind, i in STEPS1:
                g = (kind, i)
                s = UNIT_OF.get(g)
                out = work.out(g)
                if kind in ("stat_lat", "stat_mu", "stat_ln"):
                    if kind == "stat_lat":
                        pe.wait_ge(*work.taken(l, ("pb", 2)))
                        parts = (0, scr[:, 0:3]), (T, scr[:, 3:5])
                    elif kind == "stat_mu":
                        pe.wait_ge(*conv_ready(l, 1))
                        parts = ((0, conv),)
                    else:
                        pe.wait_ge(*centred_sq(l, 1))
                        parts = ((0, i_g),)
                    pe.wait_ge(*work.bank_free(l, g))
                    for at, src in parts:
                        n = src.shape[1]
                        for t in range(n):
                            last = pe.matmul(out[:, at:at + T], ones, src[:, t], start=t == 0, stop=t == n - 1)
                    last.then_inc(work.done_sem.sem, 1)
                    continue
                if kind == "S":
                    pe.wait_ge(*q_ready(l, i // 2 + 1))
                    if i == 0:
                        pe.wait_ge(*key_rope_ready(l, 1))
                        pe.wait_ge(*work.taken(l, ("uk", 1)))
                    scores_pe(pe, work, l, g, q1[0:NOPE + ROPE, i], k1[0:NOPE + ROPE, i])
                    continue
                if kind == "T":
                    transpose_pe(pe, work, l, g, probs_ready(l, i + 1), probs1, i % 2)
                    continue
                if kind == "V":
                    pe.wait_ge(*work.taken(l, ("T", 2 * i + 1)))
                    pe.wait_ge(*work.bank_free(l, g))
                    if i == 0:
                        pe.wait_ge(*work.taken(l, ("uv", 1)))
                    for e in range(2):
                        h = 2 * i + e
                        last = values_pe(pe, out[64 * e:64 * e + 64, 0:T],
                                         [v1[:, m, h * VD:(h + 1) * VD] for m in range(2)], probs_t1, e)
                    last.then_inc(work.done_sem.sem, 1)
                    continue
                pe.wait_ge(*st.lo_ready(l, s + 1))
                pe.wait_ge(*work.bank_free(l, g))
                if kind in ("pb", "pc", "pa"):
                    if g == FIRST1:
                        first_products(pe, n1, l, 1, [(out[:, 0:T], s, 0)])
                    for half in range(g == FIRST1, 2):
                        for k in range(KT):
                            last = product(pe, out[:, half * T:half * T + T], s, half * KT + k, h_hi[:, k], h_lo[:, k],
                                           k == 0, k == KT - 1)
                elif kind == "uq":
                    pe.wait_ge(*lat_split(l, 1))
                    for half in range(2):
                        for k in range(3):
                            last = product(pe, out[:, half * T:half * T + T], s, 6 * (i % 2) + 3 * half + k, lat_hi[:, k],
                                           lat_lo[:, k], k == 0, k == 2)
                elif kind == "uk":
                    for half in range(2):
                        for k in range(2):
                            last = product(pe, out[:, half * T:half * T + T], s, 4 * i + 2 * half + k, lat_hi[:, 3 + k],
                                           lat_lo[:, 3 + k], k == 0, k == 1)
                elif kind == "uv":
                    for k in range(2):
                        last = tokens_product(pe, out[:, 0:512], s, 8 * P + 512 * k, 512, lat_hi[:, 3 + k, i * P:(i + 1) * P],
                                              lat_lo[:, 3 + k, i * P:(i + 1) * P], k == 0, k == 1)
                elif kind in ("lr", "li"):
                    pe.wait_ge(*xa_split(l, 1))
                    for half in range(2):
                        t = 2 * i + half
                        last = product(pe, out[:, half * T:half * T + T], s, (4 if kind == "li" else 0) + t, xa_hi[:, t],
                                       xa_lo[:, t], True, True)
                elif kind in ("A", "C", "B"):
                    for k in range(KT):
                        product(pe, out[:, 0:T], s, k, h_hi[:, k], h_lo[:, k], k == 0, k == KT - 1)
                    y_hi, y_lo = dict(A=(ya_hi, ya_lo), B=(o1_hi, o1_lo), C=(cv_hi, cv_lo))[kind]
                    if i == 0:
                        pe.wait_ge(*(ya_split(l, 1) if kind == "A" else cv_split(l, 1) if kind == "C"
                                     else work.taken(l, ("V", 3))))
                    for k in range(4):
                        last = product(pe, out[:, T:2 * T], s, KT + k, y_hi[:, k], y_lo[:, k], k == 0, k == 3)
                elif kind == "O":
                    for half, t in enumerate(O_TILES[i]):
                        for k in range(KT):
                            if t == 0:
                                pe.wait_ge(*m_split(l, k + 1))
                            last = product(pe, out[:, half * T:half * T + T], s, half * KT + k, m_hi[:, k], m_lo[:, k],
                                           k == 0, k == KT - 1)
                last.then_inc(work.done_sem.sem, 1)

        def lam_root_act(act, l):
            act.wait_ge(*lam_ready(l, 1))
            act.activation(derived[:, 28:32], derived[:, 24:28], ACT.Exp, scale=-1.0).then_inc(lam_exp.sem, 1)

        def mixer1_act(act, l, split):
            st, work = first, work1
            for kind, i in EVAC1:
                g = (kind, i)
                out = work.out(g)
                if g in UNIT_OF:
                    split.until(UNIT_OF[g] + AHEAD)
                if g == ("pa", 0):
                    lam_root_act(act, l)
                if g == ("pb", 0):
                    act.wait_ge(*xa_ready(l, 1))
                    act.activation(xa_hi[:], xa[:], ACT.Copy).then_inc(xa_hi_ready.sem, 1)
                if kind == "pb":
                    act.wait_ge(*work.done(l, g))
                    for half in range(2):
                        t, src = 2 * i + half, out[:, half * T:half * T + T]
                        if t < 5:
                            act.activation(scr[:, t], src, ACT.Square, bias=col("b_pb", t))
                            last = act.activation(lat[:, t], src, ACT.Identity, bias=col("b_pb", t))
                        else:
                            act.activation(key_pe[64:P], src[64:P], ACT.Identity,
                                           bias=col("b_pb", 5, rows=slice(64, P))).then_inc(work.freed_sem(g), 1)
                            last = None
                    if last is not None:
                        last.then_inc(work.freed_sem(g), 1)
                    if i == 2:
                        act.wait_ge(*ratio_ready(l, 1))
                        act.activation(r_g[:], r_g[:], ACT.Exp, scale=0.5).then_inc(root_ready.sem, 1)
                elif kind == "stat_lat":
                    act.wait_ge(*work.done(l, g))
                    act.activation(lat_acc[:, 0:T], out[:, 0:T], ACT.Ln, scale=1.0 / 384, bias=eps_col)
                    act.activation(lat_acc[:, T:2 * T], out[:, T:2 * T], ACT.Ln, scale=1.0 / 256, bias=eps_col)
                    act.drain().then_inc(work.freed_sem(g), 1)
                    act.activation(lat_acc, lat_acc, ACT.Exp, scale=-0.5).then_inc(lat_std.sem, 1)
                    act.wait_ge(*lat_normed(l, 1))
                    act.activation(lat_hi[:], lat[:], ACT.Copy).then_inc(lat_hi_ready.sem, 1)
                    act.wait_ge(*ya_made(l, 1))
                    act.activation(ya_hi[:], xa[:], ACT.Copy).then_inc(ya_hi_ready.sem, 1)
                elif kind == "pc":
                    act.wait_ge(*work.done(l, g))
                    if i >= 2:
                        act.wait_ge(*work.taken(l, ("pc", i - 2)))
                    act.activation(gate[:, i % 2], out[:, T:2 * T], ACT.Sigmoid, bias=col("b_pc", 4 + i)).then_inc(sig_ready.sem, 1)
                elif kind == "pa":
                    act.wait_ge(*work.done(l, g))
                    act.activation(pad_r[:, i, LRU_TAPS - 1:], out[:, 0:T], ACT.Identity, bias=col("b_pa", i))
                    act.activation(gelu[:, i], out[:, T:2 * T], ACT.Gelu_apprx_tanh,
                                   bias=col("b_pa", 4 + i)).then_inc(work.freed_sem(g), 1)
                elif kind == "uq":
                    act.wait_ge(*work.done(l, g))
                    act.activation(q1[0:64, 2 * i:2 * i + 2], out[0:64, :].rearrange("p (h t) -> p h t", h=2),
                                   ACT.Copy).then_inc(q_nope_ready.sem, 1)
                elif kind == "uk":
                    act.wait_ge(*work.done(l, g))
                    for e in range(2):
                        last = act.activation(k1[0:64, 4 * i + e:4 * i + 4:2],
                                              out[64 * e:64 * e + 64, :].rearrange("p (h t) -> p h t", h=2), ACT.Copy)
                    last.then_inc(work.freed_sem(g), 1)
                elif kind == "uv":
                    act.wait_ge(*work.done(l, g))
                    act.activation(v1[:, i], out[:, :], ACT.Copy).then_inc(work.freed_sem(g), 1)
                elif kind in ("lr", "li"):
                    act.wait_ge(*work.done(l, g))
                    into, bias = (r_g, "lru_br") if kind == "lr" else (i_g, "lru_bi")
                    for half in range(2):
                        t = 2 * i + half
                        last = act.activation(into[:, t], out[:, half * T:half * T + T], ACT.Sigmoid, bias=col(bias, t))
                    last.then_inc(work.freed_sem(g), 1)
                    if g == ("li", 1):
                        act.drain()
                        act.wait_ge(*rate_ready(l, 1))
                        for t in range(4):
                            act.activation(a_t[:, t], r_g[:, t], ACT.Exp, scale=derived[:, 32 + t:33 + t])
                        for t in range(4):
                            act.activation(r_g[:, t], r_g[:, t], ACT.Tanh, scale=derived[:, 32 + t:33 + t])
                        act.preload_act_table_set(LOG_EXP)
                        act.drain()
                        act.activation(ratio, r_g[:], ACT.Ln, scale=-2.0, bias=tiny_col)
                        act.drain()
                        act.activation(r_g[:], r_g[:], ACT.Ln, scale=-1.0, bias=ones[:, 0:1]).then_inc(decay_ready.sem, 1)
                elif kind == "S":
                    softmax_act_exp(act, probs1, row1, i % 2, max_ready(l, i + 1), exp_ready)
                    softmax_act_norm(act, probs1, row1, i % 2, sums_ready(l, i + 1), probs_ready)
                elif kind == "T":
                    act.wait_ge(*work.done(l, g))
                    if i >= 2:
                        act.wait_ge(*work.done(l, ("V", i // 2 - 1)))
                    act.activation(probs_t1[:, i % 2, :], out[:, 0:384], ACT.Copy).then_inc(work.freed_sem(g), 1)
                elif kind == "V":
                    act.wait_ge(*work.done(l, g))
                    act.activation(o1_hi[:, i], out[:, 0:T], ACT.Copy).then_inc(o_hi_ready.sem, 1)
                elif kind in ("A", "B", "C"):
                    n = "ABC".index(kind) * KT + i
                    act.wait_ge(*work.done(l, g))
                    if n >= 2:
                        act.wait_ge(*merge_step(l, n - 1))
                    last = act.activation(gate[:, i % 2], out[:, 0:T], ACT.Tanh, scale=0.5,
                                          bias=derived[:, BRANCH_VEC[kind] + i:BRANCH_VEC[kind] + i + 1])
                    if kind == "C":
                        act.activation(y_b[:, i % 2], out[:, T:2 * T], ACT.Identity,
                                       bias=col("b_pw", i)).then_inc(work.freed_sem(g), 1)
                        act.wait_ge(*merge_step(l, n + 1))
                        act.activation(m_hi[:, i], merged[:, i], ACT.Copy).then_inc(m_hi_ready.sem, 1)
                    else:
                        last.then_inc(gate_ready.sem, 1)
                elif kind == "stat_ln":
                    act.preload_act_table_set(LOG_EXP)
                    act.wait_ge(*work.done(l, g))
                    act.activation(std[:], out[:, 0:T], ACT.Ln, scale=1.0 / 512, bias=eps_col)
                    act.drain().then_inc(work.freed_sem(g), 1)
                    act.activation(std[:], std[:], ACT.Exp, scale=-0.5).then_inc(ln_std.sem, 1)
                    act.preload_act_table_set(SILU)
                    act.wait_ge(*ln_made(l, 1))
                    for t in range(4):
                        act.activation(conv[:, t], conv[:, t], ACT.Silu, scale=col("ln_g", t), bias=col("ln_b", t))
                    act.drain()
                    act.activation(cv_hi[:], conv[:], ACT.Copy).then_inc(cv_hi_ready.sem, 1)
                elif kind == "stat_mu":
                    act.wait_ge(*centred(l, 1))
                    act.activation(i_g[:], conv[:], ACT.Square).then_inc(centred_sq.sem, 1)
                elif kind == "O":
                    for t in O_TILES[i]:
                        act.wait_ge(*x_mixed(l, t + 1))
                        square(act, n1, l, KT * 2 + t + 1, x[:, t], t % 2)

        def log1p_series(dve, e, out, s, s2):
            dve.tensor_scalar(s, e, 2.0, None, ALU.add)
            dve.drain()
            dve.reciprocal(s, s)
            dve.drain()
            dve.tensor_tensor(s, s, e, ALU.mult)
            dve.drain()
            dve.tensor_tensor(s2, s, s, ALU.mult)
            dve.drain()
            dve.tensor_scalar(out, s2, 1.0 / 17, 1.0 / 15, ALU.mult, ALU.add)
            for n in (13, 11, 9, 7, 5, 3, 1):
                dve.drain()
                dve.tensor_tensor(out, out, s2, ALU.mult)
                dve.drain()
                dve.tensor_scalar(out, out, 1.0 / n, None, ALU.add)
            dve.drain()
            dve.tensor_tensor(out, out, s, ALU.mult)
            dve.drain()
            dve.tensor_scalar(out, out, 2.0, None, ALU.mult)
            dve.drain()

        TAPS_AT = dict(pc=7, uq=3, uk=4, uv=4, S=2, A=4, B=9)

        def mixer1_dve(dve, l, split):
            st, work = first, work1

            def taps():
                for pair, j in ((pair, j) for pair in range(2) for j in range(CONV_TAPS)):
                    dve.drain()
                    for t in range(2 * pair, 2 * pair + 2):
                        w = col("dw_w", CONV_TAPS * t + j)
                        if j == 0:
                            last = dve.tensor_scalar(conv[:, t], glu[:, t, 0:T], w, col("dw_b", t), ALU.mult, ALU.add)
                        else:
                            last = dve.scalar_tensor_tensor(conv[:, t], glu[:, t, j:j + T], w, conv[:, t], ALU.mult, ALU.add)
                        if j == CONV_TAPS - 1 and t == 3:
                            last.then_inc(conv_ready.sem, 1)
                        yield

            dve.memset(glu[:, :, 0:CONV_TAPS - 1], 0.0)
            dve.memset(pad_r[:, :, 0:LRU_TAPS - 1], 0.0)
            tap = taps()

            def convolve(n):
                for _ in range(n):
                    next(tap, None)

            for kind, i in EVAC1:
                g = (kind, i)
                out = work.out(g)
                if g in UNIT_OF:
                    split.until(UNIT_OF[g] + AHEAD)
                if kind == "pa":
                    if i == 0:
                        lam = vec[:, VEC1["lam"]:VEC1["lam"] + 4]
                        dve.tensor_scalar(derived[:, 36:40], lam, -1.0, None, ALU.mult)
                        dve.drain()
                        dve.tensor_tensor(derived[:, 24:28], derived[:, 36:40], lam, ALU.max).then_inc(lam_ready.sem, 1)
                        dve.tensor_scalar(derived[:, 0:24], vec[:, VEC1["b_gate"]:VEC1["b_gate"] + 24], 0.5, None, ALU.mult)
                    if i == 1:
                        dve.wait_ge(*lam_exp(l, 1))
                        log1p_series(dve, derived[:, 28:32], derived[:, 40:44], derived[:, 44:48], derived[:, 48:52])
                        dve.tensor_scalar(derived[:, 36:40], derived[:, 36:40], 0.0, None, ALU.max)
                        dve.drain()
                        dve.tensor_tensor(derived[:, 40:44], derived[:, 40:44], derived[:, 36:40], ALU.add)
                        dve.drain()
                        dve.tensor_scalar(derived[:, 32:36], derived[:, 40:44], -8.0, None, ALU.mult).then_inc(rate_ready.sem, 1)
                    dve.wait_ge(*work.taken(l, g))
                    for j in range(LRU_TAPS):
                        w = col("lru_w", LRU_TAPS * i + j)
                        if j == 0:
                            dve.tensor_scalar(xa[:, i], pad_r[:, i, 0:T], w, col("lru_b", i), ALU.mult, ALU.add)
                        else:
                            dve.drain()
                            last = dve.scalar_tensor_tensor(xa[:, i], pad_r[:, i, j:j + T], w, xa[:, i], ALU.mult, ALU.add)
                    if i == 3:
                        last.then_inc(xa_ready.sem, 1)
                elif kind == "pb" and i == 0:
                    dve.wait_ge(*xa_hi_ready(l, 1))
                    dve.tensor_tensor(xa_lo[:], xa[:], xa_hi[:].bitcast(F32), ALU.subtract).then_inc(xa_split.sem, 1)
                elif g == ("li", 1):
                    dve.wait_ge(*decay_ready(l, 1))
                    dve.tensor_tensor(r_g[:], ratio, r_g[:], ALU.subtract).then_inc(ratio_ready.sem, 1)
                    dve.tensor_tensor(i_g[:], i_g[:], xa[:], ALU.mult)
                elif kind == "pb" and i == 2:
                    dve.drain()
                    dve.wait_ge(*root_ready(l, 1))
                    dve.tensor_tensor(i_g[:], i_g[:], r_g[:], ALU.mult)
                    dve.drain()
                    for t in range(4):
                        dve.tensor_tensor_scan(xa[:, t], a_t[:, t], i_g[:, t], 0.0, ALU.mult, ALU.add)
                    dve.drain()
                    dve.tensor_tensor(xa[:], xa[:], gelu[:], ALU.mult).then_inc(ya_made.sem, 1)
                elif kind == "stat_lat":
                    dve.wait_ge(*lat_std(l, 1))
                    for t in range(5):
                        gain = col("q_norm", t) if t < 3 else col("kv_norm", t - 3)
                        r = lat_acc[:, 0:T] if t < 3 else lat_acc[:, T:2 * T]
                        last = dve.scalar_tensor_tensor(lat[:, t], lat[:, t], gain, r, ALU.mult, ALU.mult)
                    last.then_inc(lat_normed.sem, 1)
                    dve.wait_ge(*lat_hi_ready(l, 1))
                    dve.tensor_tensor(lat_lo[:], lat[:], lat_hi[:].bitcast(F32), ALU.subtract).then_inc(lat_split.sem, 1)
                    dve.wait_ge(*ya_hi_ready(l, 1))
                    dve.tensor_tensor(ya_lo[:], xa[:], ya_hi[:].bitcast(F32), ALU.subtract).then_inc(ya_split.sem, 1)
                elif kind == "pc":
                    dve.wait_ge(*sig_ready(l, i + 1))
                    dve.scalar_tensor_tensor(glu[:, i, CONV_TAPS - 1:], out[:, 0:T], col("b_pc", i), gate[:, i % 2],
                                             ALU.add, ALU.mult).then_inc(work.freed_sem(g), 1)
                    if i == 1:
                        dve.tensor_tensor(rope_t[64:96, 0, 0:T], key_pe[64:96], trig1[64:96], ALU.mult)
                        dve.tensor_tensor(rope_t[64:96, 1, 0:T], key_pe[96:128], trig1[96:128], ALU.mult).then_inc(key_terms.sem, 1)
                        convolve(TAPS_AT[kind])
                    if i > 1:
                        convolve(TAPS_AT[kind])
                elif kind == "uq":
                    if i == 0:
                        dve.wait_ge(*key_rope_ready(l, 1))
                    dve.wait_ge(*q_nope_ready(l, i + 1))
                    view = out[:, :].rearrange("p (h t) -> p h t", h=2)
                    a, b = (rope_t[64:96, e, :].rearrange("p (h t) -> p h t", h=2) for e in range(2))
                    dve.tensor_tensor(a, view[64:96], trig1[64:96].unsqueeze(1).to_broadcast([32, 2, T]), ALU.mult)
                    dve.tensor_tensor(b, view[96:128], trig1[96:128].unsqueeze(1).to_broadcast([32, 2, T]),
                                      ALU.mult).then_inc(work.freed_sem(g), 1)
                    dve.drain()
                    dve.tensor_tensor(q1[64:96, 2 * i:2 * i + 2], a, b, ALU.add).then_inc(q_ready.sem, 1)
                    convolve(TAPS_AT[kind])
                elif kind in ("uk", "uv"):
                    convolve(TAPS_AT[kind])
                elif kind == "S":
                    if i >= 2:
                        dve.wait_ge(*work.done(l, ("T", i - 2)))
                    softmax_dve_max(dve, work, l, g, MLA_SCALE, causal, probs1, row1, i % 2, max_ready)
                    convolve(TAPS_AT[kind])
                    softmax_dve_sums(dve, row1, i % 2, exp_ready(l, i + 1), sums_ready)
                elif kind == "V":
                    dve.wait_ge(*o_hi_ready(l, i + 1))
                    dve.tensor_tensor(o1_lo[:, i], out[:, 0:T], o1_hi[:, i].bitcast(F32), ALU.subtract).then_inc(work.freed_sem(g), 1)
                elif kind in ("A", "B", "C"):
                    if kind == "A":
                        dve.wait_ge(*gate_ready(l, i + 1))
                        dve.scalar_tensor_tensor(merged[:, i], gate[:, i % 2], 1.0, out[:, T:2 * T], ALU.add,
                                                 ALU.mult).then_inc(work.freed_sem(g), 1)
                        convolve(TAPS_AT[kind])
                        dve.drain().then_inc(merge_step.sem, 1)
                        continue
                    if kind == "C":
                        dve.wait_ge(*work.taken(l, g))
                        dve.scalar_tensor_tensor(sq[:, i % 2], gate[:, i % 2], 1.0, y_b[:, i % 2], ALU.add, ALU.mult)
                    else:
                        dve.wait_ge(*gate_ready(l, KT + i + 1))
                        dve.scalar_tensor_tensor(sq[:, i % 2], gate[:, i % 2], 1.0, out[:, T:2 * T], ALU.add,
                                                 ALU.mult).then_inc(work.freed_sem(g), 1)
                    dve.drain()
                    dve.tensor_tensor(merged[:, i], merged[:, i], sq[:, i % 2], ALU.add).then_inc(merge_step.sem, 1)
                    if kind == "B":
                        convolve(TAPS_AT[kind] if i < MU_AFTER - 1 else 4 * CONV_TAPS)
                        if i == KT - 1:
                            dve.wait_ge(*cv_hi_ready(l, 1))
                            dve.tensor_tensor(cv_lo[:], conv[:], cv_hi[:].bitcast(F32), ALU.subtract).then_inc(cv_split.sem, 1)
                    if kind == "C":
                        dve.wait_ge(*m_hi_ready(l, i + 1))
                        dve.tensor_tensor(m_lo[:, i], merged[:, i], m_hi[:, i].bitcast(F32),
                                          ALU.subtract).then_inc(m_split.sem, 1)
                elif kind == "stat_mu":
                    dve.wait_ge(*work.done(l, g))
                    dve.tensor_scalar(std[:], out[:, 0:T], 1.0 / 512, None, ALU.mult).then_inc(work.freed_sem(g), 1)
                    dve.drain()
                    dve.tensor_tensor(conv[:], conv[:], std[:].unsqueeze(1).to_broadcast([P, 4, T]),
                                      ALU.subtract).then_inc(centred.sem, 1)
                elif kind == "stat_ln":
                    dve.wait_ge(*ln_std(l, 1))
                    dve.tensor_tensor(conv[:], conv[:], std[:].unsqueeze(1).to_broadcast([P, 4, T]),
                                      ALU.mult).then_inc(ln_made.sem, 1)
                elif kind == "O":
                    dve.wait_ge(*work.done(l, g))
                    for half, t in enumerate(O_TILES[i]):
                        last = dve.scalar_tensor_tensor(x[:, t], out[:, half * T:half * T + T], 0.5, x[:, t], ALU.mult,
                                                        ALU.add).then_inc(x_mixed.sem, 1)
                    dve.drain().then_inc(work.freed_sem(g), 1)

        def mixer1_pool(pool, l):
            pool.drain()
            pool.wait_ge(*key_terms(l, 1))
            pool.tensor_tensor(k1[64:96], rope_t[64:96, 0, 0:T].unsqueeze(1).to_broadcast([32, QKV_HEADS, T]),
                               rope_t[64:96, 1, 0:T].unsqueeze(1).to_broadcast([32, QKV_HEADS, T]),
                               ALU.add).then_inc(key_rope_ready.sem, 1)

        def c2(name, n=0, rows=slice(0, P), width=1):
            return const2[rows, CONST2[name] + n:CONST2[name] + n + width]

        def v2(name, n=0, rows=slice(0, P), width=1):
            return vec[rows, bass.ds(n + VEC2[name], width)]

        def head2(n):
            kind, i, e = HEADS2[n]
            rows = slice(64 * e, 64 * e + 64)
            if kind in ("sel", "win"):
                keys, at = (KS, 0) if kind == "sel" else (KW, GROUPS * HD)
                head = i + 4 * e
                values = [v2b[:, m, at + e * HD:at + (e + 1) * HD] for m in range(2)]
                return rows, NQ + i, keys, values, causal, gates2[:, :, 3 * head + (1 if kind == "sel" else 2)]
            head = 2 * i + e
            q, k, at, bias = (FQ, FK, 0, fox_bias[:, head]) if kind == "fox" else (DQ, DK, 256, c2("dil", width=384))
            return rows, q + i, k + i, [v2a[:, m, at + head * HD:at + (head + 1) * HD] for m in range(2)], bias, None

        ROTATED_ORDER = list(ROTATED)
        qk_rot = sq[:].rearrange("p a t -> p (a t)")

        def mixer2_pe(pe, l):
            st, work = second, work2
            for kind, i in STEPS2:
                g = (kind, i)
                out = work.out(g)
                opens = kind not in ("V", "W") or (HEADS2[i][2] == 0 and HEADS2[i][0] != "win")
                reads = {"R": [("f", i)], "SC": [("c2", 0)], "S": [("f", 5)] if i == 16 else [], "V": [("T", i)],
                         "W": [("T", i)], "O": [last_in_tile(0)] if i == 0 else []}.get(kind, [])
                work.wait_banks_free(pe, l, [g] if opens else [], reads)
                if g in UNIT_OF2:
                    s = UNIT_OF2[g]
                    pe.wait_ge(*st.lo_ready(l, s + 1))
                if g == ("f", 0):
                    first_products(pe, n2, l, 0, [(out[:, 0:T], s, 0)])
                if kind == "f":
                    for half, t in enumerate(F_TILES[i]):
                        for k in range(KT):
                            if (g, half) != (("f", 0), 0):
                                last = product(pe, out[:, half * T:half * T + T], s, half * KT + k, h_hi[:, k], h_lo[:, k],
                                               k == 0, k == KT - 1)
                elif kind == "R":
                    for half, t in enumerate(ROTATED[i]):
                        last = pe.matmul(out[:, half * T:half * T + T], c2("perm", width=P), feat[:, t], start=True, stop=True)
                elif kind in ("va", "vb"):
                    s = UNIT_OF2[kind, 0]
                    pe.wait_ge(*st.lo_ready(l, s + 2))
                    width = 512 if kind == "va" else VB_COLS
                    for k in range(KT):
                        last = tokens_product(pe, out[:, 0:width], s + k // 4, (k % 4) * width, width,
                                              h_hi[:, k, i * P:(i + 1) * P], h_lo[:, k, i * P:(i + 1) * P], k == 0, k == KT - 1)
                elif kind == "cmp":
                    pe.wait_ge(*win_split(l, 1))
                    for j in range(16):
                        cols_ = slice(32 * j, 32 * j + 32)
                        last = product(pe, out[:, 0:32], s, j, win_hi[:, i // 2, cols_], win_lo[:, i // 2, cols_], j == 0, j == 15)
                elif kind == "c2":
                    pe.wait_ge(*rep_ready(l, 1))
                    for e in range(GROUPS):
                        rows = slice(64 * e, 64 * e + 64)
                        for t in range(2):
                            pe.matmul(out[rows, 0:SLOT], v2("w2k", HD * t, width=HD), h1[:, t, SLOT * e:SLOT * e + SLOT],
                                      start=t == 0, stop=t == 1)
                    for t in range(2):
                        last = pe.matmul(out[:, P:P + HD], h_rep[:, t].rearrange("p a c -> p (a c)"), v2("w2v", HD * t, width=HD),
                                         start=t == 0, stop=t == 1)
                elif kind == "SC":
                    pe.wait_ge(*rotated(l, 3))
                    for q in range(2):
                        for tile in range(4):
                            at = 2 * SLOT * (4 * q + tile)
                            last = pe.matmul(out[:, at:at + 2 * SLOT], feat[:, NQ + tile, q * P:(q + 1) * P], k_cmp[:],
                                             start=True, stop=True)
                elif kind == "TC":
                    pe.wait_ge(*cmp_ready(l, 1))
                    for q in range(2):
                        last = pe.transpose(out[:, q * P:(q + 1) * P], p_cmp[:, 8 * q:8 * q + 8].rearrange("p h n -> p (h n)"), ident)
                elif kind == "cum":
                    pe.wait_ge(*decay_summed(l, 1))
                    for half in range(2):
                        last = pe.matmul(out[:, half * T:half * T + T], c2("pick", P * (2 * i + half), slice(0, FOX_HEADS), P),
                                         decay[:, 3], start=True, stop=True)
                elif kind == "S":
                    rows, q, k, _, _, _ = head2(i)
                    need = {0: 4, 20: 6}.get(i)
                    if need:
                        pe.wait_ge(*rotated(l, need))
                    out = work.out(g)
                    pe.matmul(out[:, 0:P], feat[rows, q, 0:P], feat[rows, k, 0:P], start=True, stop=True)
                    last = pe.matmul(out[:, P:3 * P], feat[rows, q, P:2 * P], feat[rows, k], start=True, stop=True)
                elif kind == "T":
                    pe.wait_ge(*probs2_ready(l, i + 1))
                    for b in range(3):
                        last = pe.transpose(out[:, b * P:(b + 1) * P], probs2[:, i % 2, b * P:(b + 1) * P], ident)
                elif kind in ("V", "W"):
                    what, tile, e = HEADS2[i]
                    nsa = what in ("sel", "win")
                    if what == "sel" and e == 0:
                        pe.wait_ge(*own_ready(l, 1))
                        pe.matmul(out[:, 0:T], v_tile(tile), p_cmp_t[:], start=True, stop=False, skip_group_check=True)
                    values = head2(i)[3]
                    into = out[64 * e:64 * e + 64, 0:T]
                    pe.matmul(into, values[0], probs_t2[:, i % 2, 0:T], start=not nsa, stop=False, skip_group_check=nsa)
                    last = pe.matmul(into[:, P:T], values[1], probs_t2[:, i % 2, T:T + P], start=False, stop=True,
                                     skip_group_check=nsa)
                elif kind == "O":
                    for half, t in enumerate(O2_UNITS[i]):
                        for k in range(KT):
                            if t == 0 and k:
                                pe.wait_ge(*work.taken(l, last_in_tile(k)))
                            last = product(pe, out[:, half * T:half * T + T], s, half * KT + k, o2_hi[:, k], o2_lo[:, k],
                                           k == 0, k == KT - 1)
                last.then_inc(work.done_sem.sem, 1)

        v_tile = lambda i: v_own[:, 2 * i:2 * i + 2].rearrange("p e d -> p (e d)")

        def last_in_tile(k):
            n = {0: 17, 1: 19, 2: 3, 3: 7, 4: 11, 5: 15, 6: 21, 7: 23}[k]
            return ("W", n)

        def tile_of(n):
            kind, i, _ = HEADS2[n]
            return O2_TILE[kind] + i

        TILE_DONE = sorted(LAST_OF_TILE)

        def win_views(tile, par, e):
            v = feat[64 * e:64 * e + 64, tile].rearrange("p (n j a) -> p a j n", j=8, a=2)
            return v[:, par, :, 0:N_CMP], v[:, par, :, 1:N_CMP + 1]

        def mixer2_act(act, l, split):
            st, work = second, work2
            for kind, i in STEPS2:
                g = (kind, i)
                out = work.out(g)
                if g in UNIT_OF2:
                    split.until(UNIT_OF2[g] + AHEAD)
                if kind in ("f", "va", "vb", "cmp", "c2", "TC", "T", "W", "O"):
                    act.wait_ge(*work.done(l, g))
                if kind == "f":
                    if i == 8:
                        act.activation(decay[:, 0], out[0:FOX_HEADS, 0:T], ACT.Identity,
                                       bias=v2("b_forget", rows=slice(0, FOX_HEADS))).then_inc(work.freed_sem(g), 1)
                    else:
                        act.activation(feat[:, 2 * i:2 * i + 2].rearrange("p a t -> p (a t)"), out[:, :],
                                       ACT.Copy).then_inc(work.freed_sem(g), 1)
                elif g == ("R", 0):
                    act.wait_ge(*win_cleared(l, 1))
                    act.wait_ge(*rotated(l, 1))
                    for which, tile in enumerate((KC, VC)):
                        for par in range(2):
                            for e in range(GROUPS):
                                for upper, src in enumerate(win_views(tile, par, e)):
                                    dst = win[64 * par:64 * par + 64, which].rearrange("p (j c) -> p j c", c=32)
                                    last = act.activation(dst[:, 8 * upper:8 * upper + 8, SLOT * e:SLOT * e + N_CMP], src, ACT.Copy)
                    last.then_inc(win_copied.sem, 1)
                elif g == ("R", 1):
                    act.wait_ge(*win_made(l, 1))
                    act.activation(win_hi[:], win[:], ACT.Copy).then_inc(win_hi_ready.sem, 1)
                elif kind == "va":
                    act.activation(v2a[:, i], out[:, :], ACT.Copy).then_inc(work.freed_sem(g), 1)
                elif kind == "vb":
                    act.activation(v2b[:, i], out[:, 0:VB_COLS], ACT.Copy).then_inc(work.freed_sem(g), 1)
                    if i == 1:
                        act.wait_ge(*gate_sums(l, 1))
                        act.activation(gates2[:], gates2[:], ACT.Sigmoid).then_inc(gates_ready.sem, 1)
                elif kind == "cmp":
                    act.activation(h1[:, i], out[:, 0:32], ACT.Gelu_apprx_tanh).then_inc(work.freed_sem(g), 1)
                elif kind == "c2":
                    act.activation(v_cmp[:], out[:, P:P + HD], ACT.Copy)
                    act.activation(k_cmp[0:64, 0:SLOT], out[0:64, 0:SLOT], ACT.Copy)
                    act.activation(k_cmp[64:P, SLOT:2 * SLOT], out[64:P, 0:SLOT], ACT.Copy).then_inc(work.freed_sem(g), 1)
                    act.wait_ge(*forget_abs(l, 1))
                    act.activation(decay[:, 2], decay[:, 1], ACT.Exp, scale=-1.0).then_inc(forget_exp.sem, 1)
                elif kind == "SC":
                    act.wait_ge(*cmp_shifted(l, 1))
                    act.activation(p_cmp[:], p_cmp[:], ACT.Exp).then_inc(cmp_exp.sem, 1)
                elif kind == "TC":
                    act.activation(p_cmp_t[:], out[:, 0:T], ACT.Copy).then_inc(work.freed_sem(g), 1)
                elif kind == "S":
                    softmax_act_exp(act, probs2, row2, i % 2, max2_ready(l, i + 1), exp2_ready)
                    softmax_act_norm(act, probs2, row2, i % 2, sums2_ready(l, i + 1), probs2_ready)
                elif kind == "T":
                    if i >= 2:
                        act.wait_ge(*work.done(l, ("W" if i - 2 in LAST_OF_TILE else "V", i - 2)))
                    act.activation(probs_t2[:, i % 2, :], out[:, 0:384], ACT.Copy).then_inc(work.freed_sem(g), 1)
                elif kind == "W":
                    act.activation(o2_hi[:, tile_of(i)], out[:, 0:T], ACT.Copy).then_inc(o2_hi_ready.sem, 1)
                elif kind == "O":
                    for half, t in enumerate(O2_UNITS[i]):
                        src = out[:, half * T:half * T + T]
                        square(act, n2, l, KT + t + 1, src, t % 2)
                        last = act.activation(scr[:, t], src, ACT.Identity, scale=v2("norm1", t))
                    last.then_inc(work.freed_sem(g), 1)

        def mixer2_dve(dve, l, split):
            st, work = second, work2
            dve.memset(k_cmp[:], 0.0)
            dve.memset(win[:], 0.0).then_inc(win_cleared.sem, 1)
            for kind, i in STEPS2:
                g = (kind, i)
                out = work.out(g)
                if g in UNIT_OF2:
                    split.until(UNIT_OF2[g] + AHEAD)
                if kind == "R":
                    tiles = ROTATED[i]
                    n, width = len(tiles), len(tiles) * T
                    part = feat[:, tiles[0]:tiles[0] + n]
                    wide = lambda table: table[:].unsqueeze(1).to_broadcast([P, n, T])
                    rot = qk_rot[:, 0:width].rearrange("p (a t) -> p a t", t=T)
                    dve.drain()
                    dve.wait_ge(*work.done(l, g))
                    dve.tensor_tensor(rot, out[:, 0:width].rearrange("p (a t) -> p a t", t=T), wide(sin2), ALU.mult).then_inc(work.freed_sem(g), 1)
                    dve.tensor_tensor(part, part, wide(cos2), ALU.mult)
                    dve.drain()
                    dve.tensor_tensor(part, part, rot, ALU.add).then_inc(rotated.sem, 1)
                    if i == 1:
                        dve.wait_ge(*win_copied(l, 1))
                        for which, name in enumerate(("pos_k", "pos_v")):
                            w = win[:, which].rearrange("p (j c) -> p j c", c=32)
                            last = dve.tensor_tensor(w, w, v2(name, width=16).unsqueeze(2).to_broadcast([P, 16, 32]), ALU.add)
                        last.then_inc(win_made.sem, 1)
                        dve.wait_ge(*win_hi_ready(l, 1))
                        dve.tensor_tensor(win_lo[:], win[:], win_hi[:].bitcast(F32), ALU.subtract).then_inc(win_split.sem, 1)
                elif g == ("f", 8):
                    dve.wait_ge(*work.taken(l, g))
                    dve.tensor_scalar(decay[:, 1], decay[:, 0], -1.0, None, ALU.mult)
                    dve.drain()
                    dve.tensor_tensor(decay[:, 1], decay[:, 1], decay[:, 0], ALU.max).then_inc(forget_abs.sem, 1)
                elif g == ("vb", 1):
                    dve.wait_ge(*work.taken(l, g))
                    bias = v2("b_nsa", width=24).unsqueeze(1).to_broadcast([P, 2, 24])
                    dve.tensor_tensor(gates2[:], v2b[:, :, 256:280], bias, ALU.add).then_inc(gate_sums.sem, 1)
                elif g == ("cmp", 3):
                    dve.wait_ge(*work.taken(l, g))
                    for t in range(2):
                        last = dve.tensor_copy(h_rep[:, t], h1[:, 2 + t].unsqueeze(1).to_broadcast([P, 4, 2 * SLOT]))
                    last.then_inc(rep_ready.sem, 1)
                elif kind == "c2":
                    dve.wait_ge(*work.taken(l, g))
                    dve.tensor_tensor(v_own[:], v_cmp[:].unsqueeze(1).to_broadcast([P, NSA_HEADS, HD]),
                                      c2("own", width=NSA_HEADS).unsqueeze(2).to_broadcast([P, NSA_HEADS, HD]),
                                      ALU.mult).then_inc(own_ready.sem, 1)
                    dve.wait_ge(*forget_exp(l, 1))
                    log1p_series(dve, decay[:, 2], decay[:, 4], decay[:, 1], decay[:, 3])
                    dve.scalar_tensor_tensor(decay[:, 1], decay[:, 0], 0.0, decay[:, 4], ALU.min, ALU.subtract)
                    dve.memset(decay[:, 2], 0.0)
                    dve.drain()
                    dve.tensor_tensor_scan(decay[:, 3], decay[:, 1], decay[:, 2], 0.0, ALU.add, ALU.add).then_inc(decay_summed.sem, 1)
                elif kind == "SC":
                    dve.wait_ge(*work.done(l, g))
                    per_q = lambda ap, q: ap[:, 8 * q:8 * q + 8]
                    mask = lambda name, q: c2(name, SLOT * q, width=SLOT).unsqueeze(1).to_broadcast([P, NSA_HEADS, SLOT])
                    src = out[:, 0:2 * NSA_HEADS * SLOT].rearrange("p (h n) -> p h n", n=SLOT)
                    spread = lambda r: row_cmp[:, r].unsqueeze(2).to_broadcast([P, 2 * NSA_HEADS, SLOT])
                    for q in range(2):
                        last = dve.scalar_tensor_tensor(per_q(p_cmp, q), per_q(src, q), ATTN_SCALE, mask("cmp_bias", q), ALU.mult, ALU.add)
                    last.then_inc(work.freed_sem(g), 1)
                    dve.drain()
                    dve.tensor_reduce(row_cmp[:, 0], p_cmp[:], AX.X, ALU.max)
                    dve.drain()
                    dve.tensor_tensor(p_cmp[:], p_cmp[:], spread(0), ALU.subtract).then_inc(cmp_shifted.sem, 1)
                    dve.wait_ge(*cmp_exp(l, 1))
                    for q in range(2):
                        dve.tensor_tensor(per_q(p_cmp, q), per_q(p_cmp, q), mask("cmp_keep", q), ALU.mult)
                    dve.drain()
                    dve.tensor_reduce(row_cmp[:, 0], p_cmp[:], AX.X, ALU.add)
                    dve.drain()
                    dve.tensor_scalar(row_cmp[:, 0], row_cmp[:, 0], 1e-30, None, ALU.max)
                    dve.drain()
                    dve.reciprocal(row_cmp[:, 1], row_cmp[:, 0])
                    dve.drain()
                    dve.wait_ge(*gates_ready(l, 1))
                    heads = lambda r: row_cmp[:, r].rearrange("p (q i e) -> p q i e", q=2, e=2)
                    for q in range(2):
                        dve.tensor_tensor(heads(0)[:, q], heads(1)[:, q],
                                          gates2[:, q].rearrange("p (e i b) -> p i e b", e=2, b=3)[:, :, :, 0], ALU.mult)
                    dve.drain()
                    dve.tensor_tensor(p_cmp[:], p_cmp[:], spread(0), ALU.mult).then_inc(cmp_ready.sem, 1)
                elif kind == "cum":
                    dve.wait_ge(*work.done(l, g))
                    for half in range(2):
                        h = 2 * i + half
                        c = out[:, half * T:half * T + T]
                        dve.tensor_tensor(fox_bias[:, h, 0:P], causal[:, 0:P], c[:, 0:P], ALU.subtract)
                        last = dve.tensor_tensor(fox_bias[:, h, P:384], causal[:, P:384], c, ALU.subtract)
                    last.then_inc(work.freed_sem(g), 1)
                elif kind == "S":
                    bias, gate_ = head2(i)[4:]
                    if i >= 2:
                        dve.wait_ge(*work.done(l, ("T", i - 2)))
                    softmax_dve_max(dve, work, l, g, ATTN_SCALE, bias, probs2, row2, i % 2, max2_ready)
                    softmax_dve_sums(dve, row2, i % 2, exp2_ready(l, i + 1), sums2_ready, head2(i)[5])
                elif kind == "W":
                    n = TILE_DONE.index(i)
                    dve.wait_ge(*o2_hi_ready(l, n + 1))
                    dve.tensor_tensor(o2_lo[:, tile_of(i)], out[:, 0:T], o2_hi[:, tile_of(i)].bitcast(F32),
                                      ALU.subtract).then_inc(work.freed_sem(g), 1)

        def post_norm_dve(dve, l, n, m):
            dve.wait_ge(*n2.std_ready(l, n + 1))
            pair = lambda ap, t: ap[:, t:t + 2]
            for t in range(0, KT + 2, 2):
                if t < KT:
                    dve.tensor_tensor(pair(scr, t), pair(scr, t), std[:].unsqueeze(1).to_broadcast([P, 2, T]), ALU.mult)
                if t:
                    dve.tensor_tensor(pair(x, t - 2), pair(x, t - 2), pair(scr, t - 2), ALU.add).then_inc(x_new.sem, 2)
                dve.drain()

        def squares_of_new(act, l, n):
            for t in range(KT):
                act.wait_ge(*x_new(l, n // 2 * KT + t + 1))
                square(act, n2, l, KT * n + t + 1, x[:, t], t % 2)

        def ffn2_act(act, l, split):
            up, down, st, work, at = "up0", "down0", second, work2, FFN2_AT
            floor = work.g.mark[up, 0] - 1
            wcol = lambda j, half, tap: v2("conv_w", j + tap * 2 * FT + half * FT)
            bcol = lambda j, half: v2("conv_b", j + half * FT)

            def high_part(j, more):
                act.wait_ge(*hid2_made(l, more + (j + 1)))
                act.activation(hid_hi[:, more + j], hid[:, j % 2], ACT.Copy).then_inc(hid2_hi_ready.sem, 1)

            def gated(j, more, split_next):
                out, parity = banks[j % 4], j % 2
                act.wait_ge(*work.done(l, (up, 0), more + j))
                act.activation(silu[:, parity], out[:, 0:T], ACT.Identity, scale=wcol(more + j, 0, 2), bias=bcol(more + j, 0))
                act.activation(conv2[:, parity], out[:, T:2 * T], ACT.Identity, scale=wcol(more + j, 1, 2),
                               bias=bcol(more + j, 1)).then_inc(last_tap_ready.sem, 1)
                split_next()
                if j:
                    high_part(j - 1, more)
                act.wait_ge(*work.taken(l, (up, 0), more + j))
                act.activation(silu[:, parity], silu[:, parity], ACT.Silu).then_inc(silu2_ready.sem, 1)

            for j in range(2):
                gated(j, 0, lambda: split.until(at + j + AHEAD))
            with act.Fori(0, 4) as it:
                for u in range(2, 6):
                    gated(u, it * 4, lambda: split_hi(act, st, work, l, at + u + AHEAD, it * 4, it * 2, floor))
            split.next = at + 18 + AHEAD
            for j in range(18, FT):
                gated(j, 0, lambda: split.until(at + j + AHEAD))
            high_part(FT - 1, 0)
            base = at + FT + AHEAD

            def output(t, more):
                act.wait_ge(*work.done(l, (down, 0), more * 2 + 2 * t))
                square(act, n2, l, more + (KT * 3 + t + 1), banks[2 + t % 2][:, 0:T], t % 2)
                act.activation(scr[:, more + t], banks[2 + t % 2][:, 0:T], ACT.Identity,
                               scale=v2("norm3", more + t)).then_inc(work.freed["a"].sem, 1)

            with act.Fori(0, 3) as it:
                for g in range(2):
                    for e in range(2):
                        split_hi(act, st, work, l, base + 2 * g + e, it * 4, it * 2)
                    output(g, it * 2)
            split.next = base + 12
            split.until(base + 2 * 7)
            output(6, 0)
            output(7, 0)

        def ffn2_dve(dve, l, split):
            up, st, work, at = "up0", second, work2, FFN2_AT
            wcol = lambda j, half, tap: v2("conv_w", j + tap * 2 * FT + half * FT)

            def low_part(j, more):
                dve.wait_ge(*hid2_hi_ready(l, more + (j + 1)))
                dve.tensor_tensor(hid_lo[:, more + j], hid[:, j % 2], hid_hi[:, more + j].bitcast(F32),
                                  ALU.subtract).then_inc(hid2_ready.sem, 1)

            def gated(j, more, split_next):
                out, parity = banks[j % 4], j % 2
                dve.wait_ge(*last_tap_ready(l, more + (j + 1)))
                for back in (1, 2):
                    for half, into in enumerate((silu, conv2)):
                        part = into[:, parity, back:T]
                        last = dve.scalar_tensor_tensor(part, out[:, half * T:half * T + T - back], wcol(more + j, half, 2 - back),
                                                        part, ALU.mult, ALU.add)
                    if back == 1:
                        dve.drain()
                last.then_inc(work.freed["v"].sem, 1)
                split_next()
                if j:
                    low_part(j - 1, more)
                dve.wait_ge(*silu2_ready(l, more + (j + 1)))
                dve.tensor_tensor(hid[:, parity], silu[:, parity], conv2[:, parity], ALU.mult).then_inc(hid2_made.sem, 1)

            for j in range(2):
                gated(j, 0, lambda: split.until(at + j + AHEAD))
            with dve.Fori(0, 4) as it:
                for u in range(2, 6):
                    gated(u, it * 4, lambda: split_lo(dve, st, l, at + u + AHEAD, it * 4))
            split.next = at + 18 + AHEAD
            for j in range(18, FT):
                gated(j, 0, lambda: split.until(at + j + AHEAD))
            low_part(FT - 1, 0)
            base = at + FT + AHEAD
            with dve.Fori(0, 3) as it:
                for u in range(4):
                    split_lo(dve, st, l, base + u, it * 4)
            split.next = base + 12
            split.until(len(st.units) - 1)

        MAGIC = 1.5 * 2 ** 23

        def rotary_dve(dve, table, pos, whole, freq, phase, done):
            dve.tensor_scalar(table, pos, freq, None, ALU.mult)
            dve.drain()
            dve.tensor_scalar(whole, table, phase, 1.0 / TWO_PI, ALU.add, ALU.mult)
            dve.drain()
            dve.tensor_scalar(whole, whole, MAGIC, None, ALU.add)
            dve.drain()
            dve.tensor_scalar(whole, whole, -MAGIC, None, ALU.add)
            for part in (6.28125, 0.0019350051879882812, 3.019915981956753e-07):
                dve.drain()
                dve.scalar_tensor_tensor(table, whole, -part, table, ALU.mult, ALU.add)
            dve.drain()
            dve.tensor_scalar(table, table, phase, 3.1415925, ALU.add, ALU.min)
            dve.drain()
            dve.tensor_scalar(table, table, -3.1415925, None, ALU.max).then_inc(done.sem, 1)

        pos_i = scr[:, 0].bitcast(I32)
        pos2_i = scr[:, 3].bitcast(I32)
        c1 = lambda name: const[:, CONST[name]:CONST[name] + 1]
        final_gain = lambda t: const[:, CONST["final"] + t:CONST["final"] + t + 1]
        xv = lambda ap: ap.rearrange("p (k t) -> p k t", k=KT)
        w1_rows = io["w1"].shape[1]

        def stream(w, units, at, l, count=1):
            start = sum(units[:at]) * BLOCK
            n = units[at] * BLOCK
            view = w[l, start:start + n * count].rearrange("(u p n) -> u p n", p=P, n=units[at] * P)
            return view

        block = ctx.enter_context(nc.Block())

        @block.sync
        def _(sp):
            sp.dma_start(x[:], xv(io["x"])).then_inc(x_in.sem, 16)
            sp.dma_start(const[:], io["const"]).then_inc(consts_in.sem, 16)
            sp.dma_start(pos_i, io["pos1"].to_broadcast([P, T])).then_inc(consts_in.sem, 16)
            sp.dma_start(pos2_i, io["pos2"].to_broadcast([P, T])).then_inc(consts_in.sem, 16)
            with sp.Fori(0, DEPTH) as l:
                sp.wait_ge(*vec_free(l, 0))
                sp.dma_start(vec[:, 0:NVEC1], io["vec1"][l]).then_inc(vec_full.sem, 16)
                for at in (0, FFN1_AT):
                    if at:
                        for s in range(MIX1_AT, FFN1_AT):
                            load_unit(sp, first, l, s, stream(io["w1"], UNITS1, s, l)[0])
                    load_loop(sp, first, l, stream(io["w1"], UNITS1, at, l, FT), at, FT, 16)
                    load_loop(sp, first, l, stream(io["w1"], UNITS1, at + FT, l, 2 * KT), at + FT, 2 * KT, HALF)
            sp.wait_ge(*x_new(0, KT))
            sp.dma_start(const2[:], io["const2"]).then_inc(consts2_in.sem, 16)
            sp.wait_ge(*vec_free(DEPTH, 0))
            sp.wait_ge(*first.lo_ready(DEPTH - 1, len(UNITS1)))
            with sp.Fori(0, DEPTH) as l:
                sp.wait_ge(*vec2_free(l, 0))
                sp.dma_start(vec[:, 0:NVEC2], io["vec2"][l]).then_inc(vec2_full.sem, 16)
                for s in range(FFN2_AT):
                    load_unit(sp, second, l, s, stream(io["w2"], UNITS2, s, l)[0])
                load_loop(sp, second, l, stream(io["w2"], UNITS2, FFN2_AT, l, FT), FFN2_AT, FT, 16)
                load_loop(sp, second, l, stream(io["w2"], UNITS2, FFN2_AT + FT, l, 2 * KT), FFN2_AT + FT, 2 * KT, HALF)
            for t in range(0, KT, 2):
                sp.wait_ge(*x_new(DEPTH, t + 2))
                sp.dma_start(xv(io["out"])[:, t:t + 2], x[:, t:t + 2]).then_inc(out_done.sem, 16)
            sp.wait_ge(out_done.sem, 16 * KT // 2)

        @block.tensor
        def _(pe):
            pe.wait_ge(consts_in.sem, 48)
            with pe.Fori(0, DEPTH) as l:
                norm_pe(pe, work1, n1, l, 0)
                ffn_pe(pe, first, work1, n1, l, 0, 0, 0, hid_ready)
                norm_pe(pe, work1, n1, l, 1)
                mixer1_pe(pe, l)
                norm_pe(pe, work1, n1, l, 2)
                ffn_pe(pe, first, work1, n1, l, 1, FFN1_AT, 2, hid_ready)
            norm_pe(pe, work1, n1, DEPTH, 0)
            with pe.Fori(0, DEPTH) as l:
                norm_pe_direct(pe, work2, n2, l, 0)
                mixer2_pe(pe, l)
                norm_pe(pe, work2, n2, l, 1)
                norm_pe_direct(pe, work2, n2, l, 2)
                ffn_pe(pe, second, work2, n2, l, 0, FFN2_AT, 1, hid2_ready)
                norm_pe(pe, work2, n2, l, 3)

        @block.scalar
        def _(act):
            def one(l):
                return lambda s: split_hi(act, first, work1, l, s)
            act.wait_ge(x_in.sem, 16)
            for t in range(KT):
                square(act, n1, 0, t + 1, x[:, t], t % 2)
            act.wait_ge(consts_in.sem, 48)
            act.wait_ge(*turned(0, 1))
            act.activation(trig1[:], trig1[:], ACT.Sin).then_inc(trig_ready.sem, 1)
            with act.Fori(0, DEPTH) as l:
                split = Splitter(one(l), len(UNITS1))
                split.until(0)
                norm_act_root(act, work1, n1, l, 0)
                act.wait_ge(*vec_full(l, 16))
                norm_act_split(act, n1, l, 0)
                split.until(AHEAD - 1)
                act.preload_act_table_set(SILU)
                ffn_act(act, l, 0, 0, 0, split)
                norm_act_root(act, work1, n1, l, 1)
                norm_act_split(act, n1, l, 1)
                mixer1_act(act, l, split)
                norm_act_root(act, work1, n1, l, 2)
                act.drain().then_inc(vec_free.sem, 1)
                norm_act_split(act, n1, l, 2)
                act.preload_act_table_set(SILU)
                ffn_act(act, l, 1, FFN1_AT, 2, split)
            norm_act_root(act, work1, n1, DEPTH, 0)
            act.wait_ge(*turned(0, 3))
            act.activation(cos2[:], cos2[:], ACT.Sin)
            act.activation(sin2[:], sin2[:], ACT.Sin).then_inc(trig2_ready.sem, 1)
            with act.Fori(0, DEPTH) as l:
                split = Splitter(lambda s: split_hi(act, second, work2, l, s), len(UNITS2))
                squares_of_new(act, l, 0)
                split.until(0)
                norm_act_root(act, work2, n2, l, 0)
                act.wait_ge(*vec2_full(l, 16))
                norm_act_split(act, n2, l, 0)
                split.until(AHEAD - 1)
                mixer2_act(act, l, split)
                norm_act_root(act, work2, n2, l, 1)
                squares_of_new(act, l, 2)
                norm_act_root(act, work2, n2, l, 2)
                norm_act_split(act, n2, l, 1)
                act.preload_act_table_set(SILU)
                ffn2_act(act, l, split)
                act.drain().then_inc(vec2_free.sem, 1)
                norm_act_root(act, work2, n2, l, 3)

        @block.vector
        def _(dve):
            def one(l):
                return lambda s: split_lo(dve, first, l, s)
            for s in (first.lo_ready, work1.done_sem, work1.freed["v"], work1.freed["a"], n1.sq_summed, vec_free,
                      second.lo_ready, work2.done_sem, work2.freed["v"], work2.freed["a"], n2.sq_summed, vec2_free):
                dve.sem_inc(s.sem, s.per)
            dve.wait_ge(consts_in.sem, 48)
            dve.tensor_copy(scr[:, 1], pos_i)
            dve.tensor_copy(scr[:, 4], pos2_i)
            dve.drain()
            rotary_dve(dve, trig1[:], scr[:, 1], scr[:, 2], c1("freq1"), c1("phase1"), turned)
            rotary_dve(dve, cos2[:], scr[:, 4], scr[:, 5], c1("freq_c"), c1("phase_c"), turned)
            rotary_dve(dve, sin2[:], scr[:, 4], scr[:, 6], c1("freq_s"), c1("phase_s"), turned)
            dve.wait_ge(*trig_ready(0, 1))
            dve.wait_ge(x_in.sem, 16)
            with dve.Fori(0, DEPTH) as l:
                split = Splitter(one(l), len(UNITS1))
                split.until(0)
                dve.wait_ge(*vec_full(l, 16))
                norm_dve(dve, n1, l, 0, 0, lambda t: col("norm0", t))
                split.until(AHEAD - 1)
                ffn_dve(dve, l, 0, 0, 0, split)
                norm_dve(dve, n1, l, 1, 1, lambda t: col("norm1", t))
                mixer1_dve(dve, l, split)
                norm_dve(dve, n1, l, 2, 2, lambda t: col("norm2", t))
                dve.drain().then_inc(vec_free.sem, 1)
                ffn_dve(dve, l, 1, FFN1_AT, 2, split)
            dve.wait_ge(*n1.std_ready(DEPTH, 1))
            for t in range(KT):
                dve.scalar_tensor_tensor(x[:, t], x[:, t], final_gain(t), std[:], ALU.mult, ALU.mult).then_inc(x_new.sem, 1)
            dve.wait_ge(*trig2_ready(0, 1))
            dve.wait_ge(consts2_in.sem, 16)
            with dve.Fori(0, DEPTH) as l:
                split = Splitter(lambda s: split_lo(dve, second, l, s), len(UNITS2))
                split.until(0)
                dve.wait_ge(*vec2_full(l, 16))
                norm_dve(dve, n2, l, 0, 0, lambda t: v2("norm0", t))
                split.until(AHEAD - 1)
                mixer2_dve(dve, l, split)
                post_norm_dve(dve, l, 1, 0)
                norm_dve(dve, n2, l, 2, 1, lambda t: v2("norm2", t))
                ffn2_dve(dve, l, split)
                dve.drain().then_inc(vec2_free.sem, 1)
                post_norm_dve(dve, l, 3, 1)

        @block.gpsimd
        def _(pool):
            sum_squares(pool, n1, 0, 1)
            with pool.Fori(0, DEPTH) as l:
                sum_squares(pool, n1, l, KT + 1)
                mixer1_pool(pool, l)
                sum_squares(pool, n1, l, 2 * KT + 1)
                sum_squares(pool, n1, l, 3 * KT + 1)
            with pool.Fori(0, DEPTH) as l:
                for n in (1, 3):
                    sum_squares(pool, n2, l, KT * n + 1)


def tile_blocks(w, rows=None):
    k, c = w.shape
    return w.reshape(k // P, P, c).transpose(1, 0, 2).reshape(P, -1)


def unit(*parts):
    return np.concatenate(parts, axis=1).ravel()


def ffn_units(w1, w2, inner=FF):
    out = []
    for j in range(FT):
        out.append(unit(tile_blocks(w1[:, j * P:(j + 1) * P]), tile_blocks(w1[:, FF + j * P:FF + (j + 1) * P])))
    for t in range(KT):
        for half in range(2):
            out.append(unit(tile_blocks(w2[half * HALF * P:(half + 1) * HALF * P, t * P:(t + 1) * P])))
    return out


def tiles_of(w, tiles):
    return unit(*(tile_blocks(w[:, t * P:(t + 1) * P]) for t in tiles))


def pe_swapped(w):
    return np.concatenate([w, w[..., 16:32], w[..., 0:16]], axis=-1)


def mixer1_units(i, l):
    w = i["w_in"][l]
    pa, pb, pc, pg = np.split(w, [1024, 1696, 2720], axis=1)
    key = np.concatenate([np.zeros((D, 64), w.dtype), pe_swapped(pb[:, 640:672])], axis=1)
    lat = np.concatenate([pb[:, 0:640], key], axis=1)
    uq = i["w_uq"][l].reshape(384, QKV_HEADS, NOPE + ROPE)
    uq = np.concatenate([uq[..., :NOPE], pe_swapped(uq[..., NOPE:])], axis=-1)
    ukv = i["w_ukv"][l].reshape(256, QKV_HEADS, NOPE + VD)
    uk = np.ascontiguousarray(ukv[..., :NOPE]).reshape(256, -1)
    uv = np.ascontiguousarray(ukv[..., NOPE:]).reshape(256, -1)
    gates = []
    for part in range(2):
        for t in range(4):
            b = np.zeros((P, P), w.dtype)
            for e in range(2):
                b[64 * e:64 * e + 64, 64 * e:64 * e + 64] = i["lru_w_gate"][l, 2 * t + e, :, 64 * part:64 * part + 64]
            gates.append(b)
    branches = dict(A=(0, "lru_w_out"), B=(1, "mla_w_o"), C=(2, "conv_w_out"))
    out = []
    for kind, n in UNIT_ORDER1:
        if kind == "pa":
            out.append(tiles_of(pa, (n, 4 + n)))
        elif kind == "pb":
            out.append(tiles_of(lat, (2 * n, 2 * n + 1)))
        elif kind == "lr":
            out.append(unit(*gates))
        elif kind == "pc":
            out.append(tiles_of(pc, (n, 4 + n)))
        elif kind == "uq":
            out.append(unit(*(tile_blocks(uq[:, 2 * n + h]) for h in range(4))))
        elif kind == "uk":
            out.append(unit(*(tile_blocks(uk[:, c * P:(c + 1) * P]) for c in range(4)), tile_blocks(uv)))
        elif kind in branches:
            branch, name = branches[kind]
            at = branch * D + n * P
            out.append(unit(tile_blocks(pg[:, at:at + P]), tile_blocks(i[name][l][:, n * P:(n + 1) * P])))
        else:
            out.append(tiles_of(i["w_out"][l], ((0, 1), (2, 3), (4, 5), (6,), (7,))[n]))
    assert [o.size // BLOCK for o in out] == MIX1_UNITS
    return out


def stack_units(layers):
    return np.stack([np.concatenate(units) for units in layers])


def cols(v):
    return v.reshape(-1, P).T


def vec1_of(i, l):
    b = i["b_in"][l]
    kpe = np.concatenate([np.zeros(64, b.dtype), pe_swapped(b[1664:1696])])
    gb = i["lru_b_gate"][l]
    by = dict(norm0=cols(i["ffn1_norm"][l]), norm1=cols(i["mix_norm"][l]), norm2=cols(i["ffn2_norm"][l]),
              b_pb=cols(np.concatenate([b[1024:1664], kpe])), b_pc=cols(b[1696:2720]), b_pa=cols(b[0:1024]),
              b_gate=cols(b[2720:]), lru_b=cols(i["lru_conv_b"][l]),
              lru_w=i["lru_conv_w"][l].T.reshape(4, P, LRU_TAPS).transpose(1, 0, 2).reshape(P, -1),
              lru_br=cols(np.ascontiguousarray(gb[:, 0:64]).ravel()), lru_bi=cols(np.ascontiguousarray(gb[:, 64:128]).ravel()),
              lam=cols(i["lru_lambda"][l]), q_norm=cols(i["q_norm"][l]), kv_norm=cols(i["kv_norm"][l]),
              dw_w=i["conv_dw_w"][l].T.reshape(4, P, CONV_TAPS).transpose(1, 0, 2).reshape(P, -1),
              dw_b=cols(i["conv_dw_b"][l]), ln_g=cols(i["conv_ln_g"][l]), ln_b=cols(i["conv_ln_b"][l]),
              b_pw=cols(i["conv_b_out"][l]))
    out = np.concatenate([by[name] for name in VEC1], axis=1)
    assert out.shape == (P, NVEC1)
    return out


def causal_bias():
    q, k = np.arange(P)[:, None], np.arange(P)[None, :]
    tri = np.where(k <= q, 0.0, MASKED)
    return np.concatenate([tri, np.zeros((P, P)), tri], axis=1)


def const_of(i):
    freq, phase = np.zeros((P, 1)), np.zeros((P, 1))
    inv = 10000.0 ** (-np.arange(0, ROPE, 2, dtype=np.float64) / ROPE)
    freq[64:128, 0] = np.concatenate([inv, inv, -inv, inv])
    phase[64:96] = np.pi / 2
    inv2 = 500000.0 ** (-2.0 * np.arange(ROPE2_HALF) / (2 * ROPE2_HALF))
    d = np.arange(P) % HD
    freq2 = np.where(d < 2 * ROPE2_HALF, inv2[d % ROPE2_HALF], 0.0)
    parts = dict(ones=np.ones((P, P)), ident=np.eye(P), causal=causal_bias(), freq1=freq, phase1=phase,
                 eps=np.full((P, 1), EPS), tiny=np.full((P, 1), 1e-30),
                 freq_c=freq2[:, None], freq_s=np.where(d < ROPE2_HALF, -freq2, freq2)[:, None],
                 phase_c=np.full((P, 1), np.pi / 2), phase_s=np.zeros((P, 1)))
    parts = {k: v.astype(np.float32) for k, v in parts.items()}
    parts["final"] = cols(i["final_norm"])
    return np.concatenate([parts[k] for k in CONST], axis=1)


def mixer2_units(i, l):
    names = ("fq", "fk", "fv", "ff", "nq", "kc", "vc", "ks", "vs", "kw", "vw", "ng", "dq", "dk", "dv")
    widths = (256, 256, 256, 4, 512, 128, 128, 128, 128, 128, 128, 24, 256, 256, 256)
    w = dict(zip(names, np.split(i["w_in_2"][l], np.cumsum(widths)[:-1], axis=1)))
    nq = w["nq"].reshape(D, 2, 4, HD).transpose(0, 2, 1, 3).reshape(D, 512)
    pad = lambda a, n: np.concatenate([a, np.zeros((D, n - a.shape[1]), a.dtype)], axis=1)
    tiles = np.concatenate([w["kc"], w["vc"], nq, w["ks"], w["kw"], w["fq"], w["fk"], w["dq"], w["dk"], pad(w["ff"], P)], axis=1)
    va = np.concatenate([w["fv"], w["dv"]], axis=1)
    vb = pad(np.concatenate([w["vs"], w["vw"], w["ng"]], axis=1), VB_COLS)
    out_rows = i["w_out_2"][l]
    nsa = out_rows[256:768].reshape(2, 4, HD, D).transpose(1, 0, 2, 3).reshape(512, D)
    out_rows = np.concatenate([out_rows[:256], nsa, out_rows[768:]], axis=0)
    out = []
    for kind, n in UNIT_ORDER2:
        if kind == "f":
            out.append(tiles_of(tiles, F_TILES[n]))
        elif kind in ("va", "vb"):
            out.append(unit(tile_blocks((va if kind == "va" else vb)[512 * n:512 * n + 512])))
        elif kind == "cmp":
            w1 = i["cmp_w1_k_2" if n < 2 else "cmp_w1_v_2"][l]
            out.append(unit(tile_blocks(w1[:, P * (n % 2):P * (n % 2) + P])))
        else:
            out.append(tiles_of(out_rows, O2_UNITS[n]))
    assert [o.size // BLOCK for o in out] == UNITS2[:FFN2_AT]
    return out


def vec2_of(i, l):
    pos = lambda a: a.reshape(16, 2 * HD).T
    by = dict(norm0=cols(i["attn_pre_norm_2"][l]), norm1=cols(i["attn_post_norm_2"][l]), norm2=cols(i["ffn_pre_norm_2"][l]),
              norm3=cols(i["ffn_post_norm_2"][l]),
              b_forget=np.concatenate([i["b_forget_2"][l], np.zeros(P - FOX_HEADS, np.float32)])[:, None],
              b_nsa=np.tile(i["b_nsa_gate_2"][l][None], (P, 1)), pos_k=pos(i["cmp_pos_k_2"][l]), pos_v=pos(i["cmp_pos_v_2"][l]),
              w2k=tile_blocks(i["cmp_w2_k_2"][l]), w2v=tile_blocks(i["cmp_w2_v_2"][l]),
              conv_w=np.concatenate([cols(i["conv_w_2"][l, tap]) for tap in range(3)], axis=1), conv_b=cols(i["conv_b_2"][l]))
    out = np.concatenate([by[name] for name in VEC2], axis=1)
    assert out.shape == (P, NVEC2)
    return out


def const2_of():
    p = np.arange(P)
    perm = np.zeros((P, P))
    for m in p:
        if m % HD < 2 * ROPE2_HALF:
            perm[m + ROPE2_HALF if m % HD < ROPE2_HALF else m - ROPE2_HALF, m] = 1
    q, k = np.arange(T)[:, None], np.arange(T)[None, :]
    back = q - k
    times = sum(((back >= 0) & (back <= w) & (back % d == 0)).astype(int) for w, d in DIL_PATTERNS)
    dil = np.where(times > 0, np.log(np.maximum(times, 1)), MASKED)
    dil = np.concatenate([dil[:P, :P], dil[P:]], axis=1)
    pick = np.zeros((P, FOX_HEADS, P))
    for h in range(FOX_HEADS):
        pick[h, h] = 1
    n = np.arange(SLOT)
    keep = np.stack([(n[None] < N_CMP) & (n[None] * CMP_STRIDE + CMP_BLOCK - 1 <= (p + P * half)[:, None]) for half in range(2)], axis=1)
    own = np.zeros((P, NSA_HEADS))
    for head in range(NSA_HEADS):
        own[SLOT * head:SLOT * head + SLOT, head] = 1
    parts = dict(perm=perm, dil=dil, pick=pick.reshape(P, -1), cmp_bias=np.where(keep, 0.0, MASKED).reshape(P, -1),
                 cmp_keep=keep.reshape(P, -1), own=own)
    return np.concatenate([parts[name].astype(np.float32) for name in CONST2], axis=1)


def kernel(**i):
    import concourse.bacc as bacc
    from concourse.bass_utils import run_bass_kernel_spmd as run

    i = {name: np.asarray(a) for name, a in i.items()}
    nc = bacc.Bacc("TRN2", target_bir_lowering=False, num_devices=1)
    arrays = {
        "x": np.ascontiguousarray(i["x"][0].T.reshape(KT, P, T).transpose(1, 0, 2)).reshape(P, -1),
        "pos1": np.ascontiguousarray(i["positions"]),
        "pos2": np.ascontiguousarray(i["positions_2"]),
        "const": const_of(i),
        "const2": const2_of(),
        "vec1": np.stack([vec1_of(i, l) for l in range(DEPTH)]),
        "vec2": np.stack([vec2_of(i, l) for l in range(DEPTH)]),
        "w1": stack_units([ffn_units(i["ffn1_w1"][l], i["ffn1_w2"][l]) + mixer1_units(i, l)
                           + ffn_units(i["ffn2_w1"][l], i["ffn2_w2"][l]) for l in range(DEPTH)]),
        "w2": stack_units([mixer2_units(i, l) + ffn_units(i["w_up_2"][l], i["w_down_2"][l]) for l in range(DEPTH)]),
    }
    io = {n: nc.dram_tensor("in_" + n, a.shape, mybir.dt.from_np(a.dtype), kind="ExternalInput").ap() for n, a in arrays.items()}
    io["out"] = nc.dram_tensor("out", (P, KT * T), F32, kind="ExternalOutput").ap()
    build(nc, io)
    r = run(nc, [{"in_" + n: a for n, a in arrays.items()}], core_ids=[0])
    got = r.results[0]["out"]
    return np.ascontiguousarray(got.reshape(P, KT, T).transpose(2, 1, 0)).reshape(1, T, D)
```
